# Optimizing a Trainium2 kernel written in Bass

```python
import jax, jax.numpy as jnp
from jax import lax
import numpy as np

D_MODEL = 1024
BATCH = 1
SEQ = 512
DEPTH = 1

CHUNK = 64
MIX_WIDTH = D_MODEL
POOL_WIDTH = MIX_WIDTH // 2
POOL_WINDOWS = (2, 4, 8, 16)
POOL_GROUPS = len(POOL_WINDOWS)
POOL_GROUP_DIM = POOL_WIDTH // POOL_GROUPS
ATTN_WIDTH = MIX_WIDTH - POOL_WIDTH
HEAD_DIM = 64
N_Q_HEADS = ATTN_WIDTH // HEAD_DIM
N_KV_HEADS = 2
GQA_GROUP = N_Q_HEADS // N_KV_HEADS
KV_WIDTH = N_KV_HEADS * HEAD_DIM
WINDOW = 128
WINDOW_CHUNKS = max(1, int(round(WINDOW / CHUNK)))
IN_WIDTH = POOL_WIDTH + ATTN_WIDTH + 2 * KV_WIDTH
PEER_HEADS = 8
PEER_NKEYS = 128
PEER_EXPERTS = PEER_NKEYS * PEER_NKEYS
PEER_TOPK = 16
PEER_QDIM = 256
PEER_HALF = PEER_QDIM // 2
PEER_TOKEN_BLOCK = 128
PLE_DIM = 256
LN_EPS = 1e-5
DEEPNORM_ALPHA = (2.0 * DEPTH) ** 0.25
DEEPNORM_BETA = (8.0 * DEPTH) ** -0.25

kernel_name = "hybrid_pool_swa_peer_deepnorm"

def _layer_norm(x, g, b):
    xf = x.astype(jnp.float32)
    mu = jnp.mean(xf, axis=-1, keepdims=True)
    var = jnp.mean(jnp.square(xf - mu), axis=-1, keepdims=True)
    y = (xf - mu) * lax.rsqrt(var + LN_EPS)
    return (y * g.astype(jnp.float32) + b.astype(jnp.float32)).astype(x.dtype)

def _alibi_slopes(n):
    return np.array([2.0 ** (-8.0 * (h + 1) / n) for h in range(n)], dtype=np.float32)

def _pool_mixer(u, w_groups, scale):
    B, S, _ = u.shape
    ug = u.reshape(B, S, POOL_GROUPS, POOL_GROUP_DIM).astype(jnp.float32)
    cs = jnp.cumsum(ug, axis=1)
    pos1 = jnp.arange(1, S + 1).astype(jnp.float32)[None, :, None]
    outs = []
    for gi, w in enumerate(POOL_WINDOWS):
        c = cs[:, :, gi]
        lag = jnp.pad(c, ((0, 0), (w, 0), (0, 0)))[:, :S]
        cnt = jnp.minimum(pos1, float(w))
        outs.append((c - lag) / cnt - ug[:, :, gi])
    d = jnp.stack(outs, axis=2).astype(u.dtype)
    y = jnp.einsum('bsgc,gcd->bsgd', d, w_groups)
    return y.reshape(B, S, POOL_WIDTH) * scale

def _window_attention(q, k, v, sinks):
    B, S, _ = q.shape
    nc = S // CHUNK
    W = WINDOW_CHUNKS
    L = W * CHUNK
    qc = q.reshape(B, nc, CHUNK, N_KV_HEADS, GQA_GROUP, HEAD_DIM)

    def band(t):
        tc = t.reshape(B, nc, CHUNK, N_KV_HEADS, HEAD_DIM)
        tp = jnp.pad(tc, ((0, 0), (W - 1, 0), (0, 0), (0, 0), (0, 0)))
        return jnp.concatenate([tp[:, j:j + nc] for j in range(W)], axis=2)

    kb, vb = band(k), band(v)
    s = jnp.einsum('bcqkgd,bcskd->bckgqs', qc, kb).astype(jnp.float32) * (HEAD_DIM ** -0.5)
    q_pos = np.arange(CHUNK)[:, None]
    k_off = np.arange(L)[None, :] - (W - 1) * CHUNK
    dist = np.abs(q_pos - k_off).astype(np.float32)
    slopes = _alibi_slopes(N_Q_HEADS).reshape(N_KV_HEADS, GQA_GROUP)
    bias = jnp.asarray(-slopes[:, :, None, None] * dist[None, None])
    valid = (np.arange(nc)[:, None] - (W - 1) + np.arange(L)[None, :] // CHUNK) >= 0
    s = s + bias[None, None]
    s = jnp.where(jnp.asarray(valid)[None, :, None, None, None, :], s, -1e30)
    sink = sinks.astype(jnp.float32).reshape(N_KV_HEADS, GQA_GROUP)[None, None, :, :, None, None]
    m = jnp.maximum(jnp.max(s, axis=-1, keepdims=True), sink)
    e = jnp.exp(s - m)
    pr = e / (jnp.sum(e, axis=-1, keepdims=True) + jnp.exp(sink - m))
    o = jnp.einsum('bckgqs,bcskd->bcqkgd', pr.astype(v.dtype), vb)
    return o.reshape(B, S, ATTN_WIDTH)

def _peer(h, wq, subkeys, u_tab, v_tab):
    B, S, D = h.shape
    T = B * S
    K = PEER_TOPK
    xt = h.reshape(T, D)
    q = (xt @ wq).reshape(T, PEER_HEADS, 2, PEER_HALF).astype(jnp.float32)
    s = jnp.einsum('thpd,hpnd->thpn', q, subkeys.astype(jnp.float32))
    sv, si = lax.top_k(s, K)
    comb = (sv[:, :, 0, :, None] + sv[:, :, 1, None, :]).reshape(T, PEER_HEADS, K * K)
    cs, ci = lax.top_k(comb, K)
    ia = jnp.take_along_axis(si[:, :, 0], ci // K, axis=-1)
    ib = jnp.take_along_axis(si[:, :, 1], ci % K, axis=-1)
    idx = ia * PEER_NKEYS + ib
    g = jax.nn.softmax(cs, axis=-1).astype(h.dtype)
    nb = T // PEER_TOKEN_BLOCK

    def block(args):
        xb, eb, gb = args
        a = jnp.einsum('td,thkd->thk', xb, u_tab[eb])
        w = gb * jax.nn.gelu(a, approximate=False)
        return jnp.einsum('thk,thkd->td', w, v_tab[eb])

    out = lax.map(block, (xt.reshape(nb, PEER_TOKEN_BLOCK, D),
                          idx.reshape(nb, PEER_TOKEN_BLOCK, PEER_HEADS, K),
                          g.reshape(nb, PEER_TOKEN_BLOCK, PEER_HEADS, K)))
    return out.reshape(B, S, D)

def setup_inputs(seed: int = 0) -> dict:
    key = jax.random.key(seed)
    ks = jax.random.split(key, 24)
    f32 = jnp.float32
    D = D_MODEL
    nrm = lambda k, shape, sc: jax.random.normal(k, shape, f32) * sc
    return {
        "x": nrm(ks[0], (BATCH, SEQ, D), 1.0),
        "p": nrm(ks[1], (DEPTH, BATCH, SEQ, PLE_DIM), 1.0),
        "ln_in_g": 1.0 + nrm(ks[2], (D,), 0.02),
        "ln_in_b": nrm(ks[3], (D,), 0.02),
        "w_in": nrm(ks[4], (DEPTH, D, IN_WIDTH), D ** -0.5),
        "pool_w": nrm(ks[5], (DEPTH, POOL_GROUPS, POOL_GROUP_DIM, POOL_GROUP_DIM), POOL_GROUP_DIM ** -0.5),
        "pool_scale": 1.0 + nrm(ks[6], (DEPTH, POOL_WIDTH), 0.02),
        "attn_sinks": nrm(ks[7], (DEPTH, N_Q_HEADS), 0.5),
        "w_o": nrm(ks[8], (DEPTH, MIX_WIDTH, D), MIX_WIDTH ** -0.5 * DEEPNORM_BETA),
        "ln1_g": 1.0 + nrm(ks[9], (DEPTH, D), 0.02),
        "ln1_b": nrm(ks[10], (DEPTH, D), 0.02),
        "peer_wq": nrm(ks[11], (DEPTH, D, PEER_HEADS * PEER_QDIM), D ** -0.5),
        "peer_subkeys": nrm(ks[12], (DEPTH, PEER_HEADS, 2, PEER_NKEYS, PEER_HALF), PEER_HALF ** -0.5),
        "peer_u": nrm(ks[13], (DEPTH, PEER_EXPERTS, D), D ** -0.5),
        "peer_v": nrm(ks[14], (DEPTH, PEER_EXPERTS, D), DEEPNORM_BETA),
        "ple_w": nrm(ks[15], (DEPTH, PLE_DIM, D), PLE_DIM ** -0.5 * DEEPNORM_BETA),
        "ple_gate_w": nrm(ks[16], (DEPTH, D, D), D ** -0.5),
        "ple_gate_b": nrm(ks[17], (DEPTH, D), 0.01),
        "ln2_g": 1.0 + nrm(ks[18], (DEPTH, D), 0.02),
        "ln2_b": nrm(ks[19], (DEPTH, D), 0.02),
    }

def reference(x, p, ln_in_g, ln_in_b, w_in, pool_w, pool_scale, attn_sinks, w_o,
              ln1_g, ln1_b, peer_wq, peer_subkeys, peer_u, peer_v,
              ple_w, ple_gate_w, ple_gate_b, ln2_g, ln2_b):
    h = _layer_norm(x, ln_in_g, ln_in_b)
    s_q = POOL_WIDTH
    s_k = s_q + ATTN_WIDTH
    s_v = s_k + KV_WIDTH
    for i in range(DEPTH):
        z = h @ w_in[i]
        y_pool = _pool_mixer(z[..., :s_q], pool_w[i], pool_scale[i])
        y_attn = _window_attention(z[..., s_q:s_k], z[..., s_k:s_v], z[..., s_v:], attn_sinks[i])
        mix = jnp.concatenate([y_pool, y_attn], axis=-1) @ w_o[i]
        h = _layer_norm(DEEPNORM_ALPHA * h + mix, ln1_g[i], ln1_b[i])
        ffn = _peer(h, peer_wq[i], peer_subkeys[i], peer_u[i], peer_v[i])
        gate = jax.nn.sigmoid(h @ ple_gate_w[i] + ple_gate_b[i])
        ple = gate * (p[i] @ ple_w[i])
        h = _layer_norm(DEEPNORM_ALPHA * h + ffn + ple, ln2_g[i], ln2_b[i])
    return h


_drawn_inputs = setup_inputs


def setup_inputs(seed=0):
    import zlib

    import numpy as np

    out = dict(_drawn_inputs(seed))
    spreads = {}
    factors = {'pool_scale': 2.742,
     'attn_sinks': 18.644,
     'ple_gate_b': 57.938,
     'ln2_g': 8.472,
     'ln2_b': 8.285}
    for name, (base, spread) in spreads.items():
        noise = np.random.default_rng([zlib.crc32(name.encode()), seed]).standard_normal(out[name].shape)
        drawn = base * np.exp(spread * noise) if base else spread * noise
        out[name] = __import__('jax').numpy.asarray(drawn.astype(out[name].dtype))
    for name, factor in factors.items():
        out[name] = (out[name] * factor).astype(out[name].dtype)
    return out
```

```python
from contextlib import ExitStack

import numpy as np

import concourse.bass as bass
from concourse import mybir

F32 = mybir.dt.float32
F16 = mybir.dt.float16
U32 = mybir.dt.uint32
ALU = mybir.AluOpType
ACT = mybir.ActivationFunctionType
AX = mybir.AxisListType

P = 128
D = 1024
T = 512
TT = T // P
KD = D // P
HALF = 512
CHUNK = 64
HD = 64
NCH = T // CHUNK
PAIRS = 4
GROUPS = 4
WINDOWS = (2, 4, 8, 16)
PAD = 16
HEADS = 8
K = 16
NKEY = 128
N_IN, N_O, N_Q, N_G, N_U, N_V = 10, 8, 16, 8, 128, 128
T_IN = 0
T_O = T_IN + N_IN
T_Q = T_O + N_O
T_G = T_Q + N_Q
T_U = T_G + N_G
T_V = T_U + N_U
T_ALL = T_V + N_V
AREA = 21500
RING = 4
SPLIT_AHEAD = 2
LOAD_AHEAD = 6
S_ACT = 16.0
S_W = 256.0
S_V = 16.0
S_G = 64.0
ALPHA = 2.0 ** 0.25
EPS = 1e-5
NEG = -1e30
LOWEST = -3.0e38

U_TOPK = 32
U_SOFTMAX = 4
U_GATES = 64
U_LAST = N_U - U_TOPK - U_SOFTMAX - U_GATES
TOK = 32
GCH = T // TOK
BATCH = 16
OT = 8
VG = 4


class Tile:

    def __init__(self, c, k=0, it=0):
        self.c, self.k, self.it = c, k, it
        self.n = c + k * it if k else c
        self.slot = c % RING
        self.round = c // RING + (k // RING) * it if k else c // RING

    def plus(self, d):
        return Tile(self.c + d, self.k, self.it)


class Tally:

    def __init__(self, eng, sem):
        self.eng, self.sem, self.count, self.turns = eng, sem, 0, 0

    def mark(self, instruction):
        instruction.then_inc(self.sem, 1)
        self.count += 1

    def settle(self):
        self.eng.wait_ge(self.sem, self.turns + self.count)

    def link(self, instruction):
        self.mark(instruction)
        self.settle()


def at_least(eng, sem, value):
    if isinstance(value, int) and value <= 0:
        return
    eng.wait_ge(sem, value)


def layer(nc, tiles, x, ple_in, ple_w, norms, gate_b, small, pool_w, subkeys, alibi, ident, iota_oh, iota_k,
          out):
    gelu_dram = nc.dram_tensor("gelu_scratch", [N_U // VG, P, VG, T], F32, kind="Internal").ap()
    gates_dram = nc.dram_tensor("gates_scratch", [GCH, P, P, TOK], F32, kind="Internal").ap()

    with ExitStack() as ctx:
        def sb(name, shape, dt=F32):
            return ctx.enter_context(nc.sbuf_tensor(name, shape, dt))

        def sem(name):
            return ctx.enter_context(nc.semaphore(name))

        bank = ctx.enter_context(nc.psum_tensor("bank", [P, 8, HALF], F32))

        raw = sb("raw", [P, RING, D])
        cut = sb("cut", [P, RING, 2, D], F16)
        hn = sb("hn", [P, TT, D])
        hT = sb("hT", [P, 2, KD, T], F16)
        norm_rows = sb("norm_rows", [P, 6, D])
        gate_b_row = sb("gate_b_row", [P, D])
        stats = sb("stats", [P, TT, 12])
        moments = sb("moments", [P, TT, 2])
        word = sb("word", [P, 1])
        variance = sb("variance", [P, TT])
        std = sb("std", [P, TT])
        rstd = sb("rstd", [P, TT])
        newton = sb("newton", [P, TT])
        small_sb = sb("small_sb", [P, 8 + GROUPS + GROUPS * PAD])
        sink = small_sb[:, 0:8]
        pool_scale = small_sb[:, 8:8 + GROUPS]
        inv_count = small_sb[:, 8 + GROUPS:].rearrange("p (g t) -> p g t", g=GROUPS)
        ident_sb = sb("ident_sb", [P, P])
        iota_oh_sb = sb("iota_oh_sb", [P, NKEY, OT], F16)
        iota_k_sb = sb("iota_k_sb", [P, K])
        area = sb("area", [P, AREA])
        taken = [0]

        def part(shape, dt=F32):
            size = int(np.prod(shape)) * (2 if dt == F16 else 4) // 4
            a = area[:, taken[0]:taken[0] + size]
            taken[0] += size
            assert taken[0] <= AREA, taken
            if dt != F32:
                a = a.bitcast(dt)
            names = "abcd"[:len(shape)]
            if len(shape) > 1:
                a = a.rearrange(f"p ({' '.join(names)}) -> p {' '.join(names)}",
                                **{c: s for c, s in zip(names, shape)})
            return a

        kT = part([CHUNK + T])
        vT = part([CHUNK + T])
        qT = part([PAIRS, T])
        pool_u = part([GROUPS, PAD + T])
        pool_a = part([PAD + T])
        pool_b = part([PAD + T])
        pool_d = part([GROUPS, T])
        pool_y = part([2, T])
        pool_w_sb = part([GROUPS, P])
        alibi_sb = part([8, P])
        v_band = part([NCH, P])
        probs = part([2, TT, P])
        probs_T = part([2, T])
        row_max = part([2, TT])
        neg_max = part([2, TT])
        row_sum = part([2, TT])
        sink_exp = part([2, TT])
        denom = part([2, TT])
        inv_den = part([2, TT])
        mixT = part([2, KD, T], F16)
        taken[0] = 0
        scores = part([2 * HEADS, T])
        queries = part([2, T])
        subkeys_sb = part([2 * HEADS, NKEY])
        side = part([2, T])
        replaced = part([TT, NKEY])
        sums = part([TT, K * K])
        sums_rep = part([TT, K * K])
        top_v = part([2, TT, K])
        top_i = part([2, TT, K], U32)
        sum_v = part([TT, K])
        sum_i = part([TT, K], U32)
        half_i = part([2, TT, K], U32)
        half_f = part([2, TT, K])
        top_f = part([2, TT, K])
        hit = part([TT * K, K])
        picked = part([3, TT, HEADS * K])
        e_sum = part([TT * HEADS])
        e_inv = part([TT * HEADS])
        rows = part([4, T], F16)
        staged = part([2, 4, BATCH], F16)
        gelu_out = sb("gelu_out", [P, VG, T])
        ple_gate = sb("ple_gate", [P, 8, HALF])
        ple_in_sb = gelu_out[:, 0:2, :]
        onehot = ple_gate[:, :, :].rearrange("p a b -> p (a b)").bitcast(F16).rearrange(
            "p (s a n t) -> p s a n t", s=4, a=BATCH // OT, t=OT)
        taken[0] = 0
        gate_chunk = part([2, P, TOK])
        onehot_hi = part([2, BATCH // OT, NKEY, OT], F16)
        onehot_lo = part([2, BATCH // OT, NKEY, OT], F16)
        taken[0] += TT * NKEY
        ple_w_sb = part([2, D])
        taken[0] = 0
        gelu_in = part([2, VG, T])
        gates_in = part([2, GCH, VG, TOK])
        weight = part([RING, T])
        weight_cut = part([RING, 2, T], F16)

        x_in, consts_in, ple_loaded, subkeys_in = sem("x_in"), sem("consts_in"), sem("ple_loaded"), sem("subkeys_in")
        tile_in = [sem(f"tile_in{s}") for s in range(RING)]
        hi_cut, lo_cut, tile_used = sem("hi_cut"), sem("lo_cut"), sem("tile_used")
        columns_out = sem("columns_out")
        stats_done, rstd_done, norm_done = sem("stats_done"), sem("rstd_done"), sem("norm_done")
        turned, turned_hi, turned_lo = sem("turned"), sem("turned_hi"), sem("turned_lo")
        pads_zero, v_turned, v_band_done = sem("pads_zero"), sem("v_turned"), sem("v_band_done")
        s_done, s_out, max_done, exp_done, probs_done = (sem(n) for n in (
            "s_done", "s_out", "max_done", "exp_done", "probs_done"))
        probs_turned, probs_T_done, pv_done, o_hi, o_lo = (sem(n) for n in (
            "probs_turned", "probs_T_done", "pv_done", "o_hi", "o_lo"))
        pool_d_done, pool_prod, pool_y_done, y_hi, y_lo = (sem(n) for n in (
            "pool_d_done", "pool_prod", "pool_y_done", "y_hi", "y_lo"))
        resid_done = sem("resid_done")
        scores_done, scores_out = sem("scores_done"), sem("scores_out")
        gate_lin, gate_sig, ple_prod, ple_out, ple_added = (sem(n) for n in (
            "gate_lin", "gate_sig", "ple_prod", "ple_out", "ple_added"))
        picks_done, gate_shift, gate_exp, gates_done = (sem(n) for n in (
            "picks_done", "gate_shift", "gate_exp", "gates_done"))
        rows_turned, rows_idx, rows_hi, rows_done = (sem(n) for n in (
            "rows_turned", "rows_idx", "rows_hi", "rows_done"))
        onehot_done, gates_prod, gates_out = sem("onehot_done"), sem("gates_prod"), sem("gates_out")
        gelu_stored = [sem(f"gelu_stored{s}") for s in range(VG)]
        gates_stored = [sem(f"gates_stored{s}") for s in range(2)]
        pair_in = [sem(f"pair_in{s}") for s in range(2)]
        weight_done, weight_hi, weight_lo = sem("weight_done"), sem("weight_hi"), sem("weight_lo")
        experts_done, final_sum, final_done, stored = (sem(n) for n in (
            "experts_done", "final_sum", "final_done", "stored"))
        dve_own = sem("dve_own")

        block = ctx.enter_context(nc.Block())

        @block.sync
        def _(sp):
            def load(t):
                at_least(sp, lo_cut, t.plus(1 - RING).n)
                src = tiles[t.n] if isinstance(t.n, int) else tiles[bass.ds(t.n, 1)].rearrange("a p n -> (a p) n")
                sp.dma_start(raw[:, t.slot, :], src).then_inc(tile_in[t.slot], 16)

            def store_gelu(group, slot, expert):
                sp.wait_ge(columns_out, N_IN + N_Q + 1 + expert)
                dst = gelu_dram[group, :, slot, :] if isinstance(group, int) else \
                    gelu_dram[bass.ds(group, 1), :, slot, :].rearrange("a p t -> (a p) t")
                sp.dma_start(dst, gelu_out[:, slot, :]).then_inc(gelu_stored[slot], 16)

            def load_pair(group, parity):
                if isinstance(group, int):
                    src = gelu_dram[group]
                else:
                    src = gelu_dram[bass.ds(group, 1)].rearrange("a p e t -> (a p) e t")
                sp.dma_start(gelu_in[:, parity], src).then_inc(pair_in[parity], 16)
                first = VG * group
                sp.dma_start(gates_in[:, parity],
                             gates_dram[:, :, bass.ds(first, VG), :].rearrange("c p e t -> p c e t")
                             ).then_inc(pair_in[parity], 16)

            for t in range(TT):
                sp.dma_start(hn[:, t, :], x[t * P:(t + 1) * P, :]).then_inc(x_in, 16)
            sp.dma_start(ident_sb[:], ident).then_inc(consts_in, 16)
            sp.dma_start(norm_rows[:], norms.partition_broadcast(P)).then_inc(consts_in, 16)
            load(Tile(0))
            load(Tile(1))
            sp.dma_start(alibi_sb, alibi).then_inc(consts_in, 16)
            sp.dma_start(small_sb[:], small).then_inc(consts_in, 16)
            sp.dma_start(pool_w_sb, pool_w).then_inc(consts_in, 16)
            sp.dma_start(iota_oh_sb[:], iota_oh).then_inc(consts_in, 16)
            sp.dma_start(iota_k_sb[:], iota_k).then_inc(consts_in, 16)
            sp.dma_start(gate_b_row[:], gate_b.partition_broadcast(P)).then_inc(consts_in, 16)
            sp.dma_start(ple_in_sb, ple_in).then_inc(ple_loaded, 16)
            for n in range(2, T_Q + RING):
                load(Tile(n))
            sp.wait_ge(resid_done, 8)
            sp.dma_start(subkeys_sb, subkeys).then_inc(subkeys_in, 16)
            sp.dma_start(ple_w_sb, ple_w).then_inc(ple_loaded, 16)
            for n in range(T_Q + RING, T_Q + LOAD_AHEAD):
                load(Tile(n))
            for n in range(T_Q, T_U):
                load(Tile(n + LOAD_AHEAD))
            with sp.Fori(0, U_TOPK // 4) as it:
                for j in range(4):
                    load(Tile(T_U + j + LOAD_AHEAD, 4, it))
                    store_gelu(it, j, 4 * it + j)
            for j in range(4):
                load(Tile(T_U + U_TOPK + j + LOAD_AHEAD))
                store_gelu(U_TOPK // 4, j, U_TOPK + j)
            e0 = U_TOPK + U_SOFTMAX
            with sp.Fori(0, U_GATES // 8) as it:
                for s in range(2):
                    for j in range(4):
                        c = e0 + 4 * s + j
                        load(Tile(T_U + c + LOAD_AHEAD, 8, it))
                        store_gelu(e0 // 4 + s + 2 * it, j, c + 8 * it)
                    sp.wait_ge(gates_out, 16 * it + 8 * s + 8)
                    sp.dma_start(gates_dram[bass.ds(2 * it + s, 1)].rearrange("a p n t -> (a p) n t"),
                                 gate_chunk[:, s]).then_inc(gates_stored[s], 16)
            e0 += U_GATES
            with sp.Fori(0, U_LAST // 4 - 1) as it:
                for j in range(4):
                    load(Tile(T_U + e0 + j + LOAD_AHEAD, 4, it))
                    store_gelu(e0 // 4 + it, j, e0 + j + 4 * it)
            for s in range(2):
                sp.wait_ge(gates_stored[s], 16 * (GCH // 2))
            for j in range(VG):
                sp.wait_ge(gelu_stored[j], 16 * 2)
            load_pair(0, 0)
            load_pair(1, 1)
            for j in range(4):
                load(Tile(T_V - 4 + j + LOAD_AHEAD))
                store_gelu(N_U // 4 - 1, j, N_U - 4 + j)
            for j in range(VG):
                sp.wait_ge(gelu_stored[j], 16 * (N_U // VG))

            def experts(pair):
                for s in range(2):
                    for j in range(VG):
                        t = Tile(T_V + 4 * s + j, 8, pair) if not isinstance(pair, int) else \
                            Tile(T_V + 8 * pair + 4 * s + j)
                        if not isinstance(pair, int) or t.n + LOAD_AHEAD < T_ALL:
                            load(t.plus(LOAD_AHEAD))
                        if j == 1 and not (isinstance(pair, int) and 2 * pair + s + 2 >= N_U // VG):
                            sp.wait_ge(weight_done, 8 * pair + 4 * (s + 1))
                            load_pair(2 * pair + s + 2, s)

            with sp.Fori(0, N_V // 8 - 1) as pair:
                experts(pair)
            experts(N_V // 8 - 1)
            for t in range(TT):
                sp.wait_ge(final_done, t + 1)
                sp.dma_start(out[t * P:(t + 1) * P, :], hn[:, t, :]).then_inc(stored, 16)
            sp.wait_ge(stored, 16 * TT)

        @block.tensor
        def _(pe):
            def turn(stage):
                for k in range(KD):
                    at_least(pe, turned_hi, KD * stage + k - 3)
                    at_least(pe, turned_lo, KD * stage + k - 3)
                    for t in range(TT):
                        last = nc.tensor.transpose(bank[:, k % 4, t * P:(t + 1) * P],
                                                   hn[:, t, k * P:(k + 1) * P], ident_sb[:])
                    last.then_inc(turned, 1)

            def columns(t, index, parity):
                pe.wait_ge(lo_cut, t.n + 1)
                at_least(pe, columns_out, index - 1)
                for k in range(KD):
                    w = [cut[:, t.slot, part_, k * P:(k + 1) * P] for part_ in range(2)]
                    dst = bank[:, 4 + parity, :]
                    nc.tensor.matmul(dst, w[0], hT[:, 0, k, :], start=(k == 0), stop=False)
                    nc.tensor.matmul(dst, w[0], hT[:, 1, k, :], start=False, stop=False)
                    last = nc.tensor.matmul(dst, w[1], hT[:, 0, k, :], start=False, stop=(k == KD - 1))
                last.then_inc(tile_used, 1)

            def tokens(t, lhs, first, last_tile, count=None):
                pe.wait_ge(lo_cut, t.n + 1)
                for tt in range(TT):
                    for step, (a, b) in enumerate(((0, 0), (0, 1), (1, 0))):
                        for h in range(2):
                            mm = nc.tensor.matmul(bank[:, 2 * tt + h, :], lhs(a)[:, tt * P:(tt + 1) * P],
                                                  cut[:, t.slot, b, h * HALF:(h + 1) * HALF],
                                                  start=(first and step == 0), stop=(last_tile and step == 2))
                    if count is not None and tt < TT - 1:
                        mm.then_inc(count, 1)
                mm.then_inc(tile_used, 1)

            def values():
                pe.wait_ge(columns_out, 2)
                for c in range(NCH):
                    last = nc.tensor.transpose(bank[:, 6 + c // 4, (c % 4) * P:(c % 4 + 1) * P],
                                               vT[:, c * CHUNK:c * CHUNK + P], ident_sb[:])
                last.then_inc(v_turned, 1)

            def attn_scores(m):
                j, kv = m // 2, m % 2
                pe.wait_ge(columns_out, 3 + j)
                at_least(pe, s_out, m - 1)
                r = slice(kv * HD, (kv + 1) * HD)
                for c in range(NCH):
                    last = nc.tensor.matmul(
                        bank[(c % 2) * CHUNK:(c % 2 + 1) * CHUNK, m % 2, (c // 2) * P:(c // 2 + 1) * P],
                        qT[r, j, c * CHUNK:(c + 1) * CHUNK], kT[r, c * CHUNK:c * CHUNK + P],
                        start=True, stop=True, skip_group_check=True)
                last.then_inc(s_done, 1)

            def turn_probs(m):
                pe.wait_ge(probs_done, m + 1)
                at_least(pe, probs_T_done, m - 1)
                for t in range(TT):
                    last = nc.tensor.transpose(bank[:, 2 + m % 2, t * P:(t + 1) * P], probs[:, m % 2, t, :],
                                               ident_sb[:])
                last.then_inc(probs_turned, 1)

            def attend(m):
                j, kv = m // 2, m % 2
                pe.wait_ge(probs_T_done, m + 1)
                pe.wait_ge(v_band_done, 2)
                at_least(pe, o_lo, j - 1)
                r = slice(kv * HD, (kv + 1) * HD)
                for c in range(NCH):
                    last = nc.tensor.matmul(bank[r, 6 + j % 2, c * CHUNK:(c + 1) * CHUNK], v_band[:, c, r],
                                            probs_T[:, m % 2, c * CHUNK:(c + 1) * CHUNK],
                                            start=True, stop=True, skip_group_check=True)
                last.then_inc(pv_done, 1)

            def pool_product(g):
                pe.wait_ge(pool_d_done, g + 1)
                at_least(pe, pool_y_done, g - 1)
                nc.tensor.matmul(bank[:, 2 + g % 2, :], pool_w_sb[:, g, :], pool_d[:, g, :],
                                 start=True, stop=True).then_inc(pool_prod, 1)

            pe.wait_ge(consts_in, 16 * 8)
            pe.wait_ge(norm_done, TT)
            turn(0)
            pe.wait_ge(turned_lo, KD)
            pe.wait_ge(pads_zero, 3)
            for n in range(3):
                columns(Tile(n), n, n % 2)
            values()
            attn_scores(0)
            columns(Tile(3), 3, 1)
            attn_scores(1)
            columns(Tile(4), 4, 0)
            turn_probs(0)
            attn_scores(2)
            columns(Tile(5), 5, 1)
            attend(0)
            turn_probs(1)
            attn_scores(3)
            columns(Tile(6), 6, 0)
            attend(1)
            turn_probs(2)
            attn_scores(4)
            columns(Tile(7), 7, 1)
            attend(2)
            turn_probs(3)
            attn_scores(5)
            columns(Tile(8), 8, 0)
            attend(3)
            turn_probs(4)
            attn_scores(6)
            columns(Tile(9), 9, 1)
            attend(4)
            turn_probs(5)
            attn_scores(7)
            attend(5)
            turn_probs(6)
            attend(6)
            turn_probs(7)
            attend(7)
            pe.wait_ge(probs_T_done, 8)
            for g in range(GROUPS):
                pool_product(g)
            pe.wait_ge(columns_out, N_IN)
            pe.wait_ge(o_lo, PAIRS)
            pe.wait_ge(pool_y_done, GROUPS)
            pe.wait_ge(s_out, 8)
            for k in range(KD):
                if k >= PAIRS:
                    pe.wait_ge(y_lo, k - PAIRS + 1)
                tokens(Tile(T_O + k), lambda a, k=k: mixT[:, a, k, :], k == 0, k == KD - 1)
            pe.wait_ge(norm_done, 2 * TT)
            turn(1)
            pe.wait_ge(turned_lo, 2 * KD)
            pe.wait_ge(subkeys_in, 16)

            def key_scores(hp, j, index):
                pe.wait_ge(columns_out, index + 1)
                at_least(pe, scores_out, hp - 1)
                for t in range(TT):
                    last = nc.tensor.matmul(bank[:, 6 + j % 2, t * P:(t + 1) * P],
                                            queries[:, j % 2, t * P:(t + 1) * P],
                                            subkeys_sb[:, hp, :] if isinstance(hp, int) else
                                            subkeys_sb[:, bass.ds(hp, 1), :].rearrange("p a n -> p (a n)"),
                                            start=True, stop=True, skip_group_check=True)
                last.then_inc(scores_done, 1)

            def retrieve(it):
                for j in range(4):
                    columns(Tile(T_Q + j, 4, it), N_IN + 4 * it + j, j % 2)
                    if j:
                        key_scores(4 * it + j - 1, j - 1, N_IN + 4 * it + j - 1)
                key_scores(4 * it + 3, 3, N_IN + 4 * it + 3)

            retrieve(0)
            with pe.Fori(1, N_Q // 4) as it:
                retrieve(it)
            pe.wait_ge(columns_out, N_IN + N_Q)
            pe.wait_ge(scores_out, N_Q)
            for k in range(KD):
                tokens(Tile(T_G + k), lambda a, k=k: hT[:, a, k, :], k == 0, k == KD - 1)
            pe.wait_ge(ple_loaded, 32)
            for b in range(8):
                pe.wait_ge(gate_lin, b + 1)
                for k in range(2):
                    mm = nc.tensor.matmul(bank[:, b, :], ple_in_sb[:, k, (b // 2) * P:(b // 2 + 1) * P],
                                          ple_w_sb[:, k, (b % 2) * HALF:(b % 2 + 1) * HALF],
                                          start=(k == 0), stop=(k == 1))
                mm.then_inc(ple_prod, 1)

            pe.wait_ge(ple_out, 8)
            u_index = N_IN + N_Q
            with pe.Fori(0, U_TOPK // 4) as it:
                for j in range(4):
                    columns(Tile(T_U + j, 4, it), u_index + 4 * it + j, j % 2)
            for j in range(4):
                columns(Tile(T_U + U_TOPK + j), u_index + U_TOPK + j, j % 2)
            pe.wait_ge(gates_done, 1)
            for w in range(3):
                for t in range(TT):
                    last = nc.tensor.transpose(bank[:, w, t * P:(t + 1) * P], picked[:, w, t, :], ident_sb[:])
                last.then_inc(rows_turned, 1)
            pe.wait_ge(rows_idx, 2)
            pe.wait_ge(rows_done, 1)

            def gate_products(q, b):
                pe.wait_ge(onehot_done, q + 1)
                for four in range(4):
                    at_least(pe, gates_out, 4 * q + four - 3)
                    for u in range(4):
                        a, t = (4 * four + u) // OT, (4 * four + u) % OT
                        dst = bank[:, four, u * P:(u + 1) * P]
                        nc.tensor.matmul(dst, onehot[:, b, a, :, t], onehot_hi[:, b, a, :, t],
                                         start=True, stop=False, skip_group_check=True)
                        mm = nc.tensor.matmul(dst, onehot[:, b, a, :, t], onehot_lo[:, b, a, :, t],
                                              start=False, stop=True, skip_group_check=True)
                    mm.then_inc(gates_prod, 1)

            def build_gates(it):
                for s in range(2):
                    for j in range(4):
                        c = U_TOPK + U_SOFTMAX + 4 * s + j
                        columns(Tile(T_U + c, 8, it), u_index + c + 8 * it, j % 2)
                        if j % 2:
                            gate_products(4 * it + 2 * s + j // 2, j // 2)

            build_gates(0)
            with pe.Fori(1, U_GATES // 8) as it:
                build_gates(it)
            e0 = U_TOPK + U_SOFTMAX + U_GATES
            with pe.Fori(0, U_LAST // 4) as it:
                for j in range(4):
                    columns(Tile(T_U + e0 + j, 4, it), u_index + e0 + j + 4 * it, j % 2)
            pe.wait_ge(columns_out, u_index + N_U)
            pe.wait_ge(gates_out, T // 4)

            def experts(pair):
                fixed = isinstance(pair, int)
                for v in range(8):
                    t = Tile(T_V + 8 * pair + v) if fixed else Tile(T_V + v, 8, pair)
                    pe.wait_ge(weight_lo, 8 * pair + v + 1)
                    end = fixed and t.n == T_ALL - 1
                    tokens(t, lambda a, v=v: weight_cut[:, v % RING, a, :], fixed and t.n == T_V, end,
                           experts_done if end else None)

            experts(0)
            with pe.Fori(1, N_V // 8 - 1) as pair:
                experts(pair)
            experts(N_V // 8 - 1)

        @block.scalar
        def _(act):
            def split_hi(t, scale=S_W):
                act.wait_ge(tile_in[t.slot], 16 * (t.round + 1))
                at_least(act, tile_used, t.n - RING + 1)
                nc.scalar.activation(cut[:, t.slot, 0, :], raw[:, t.slot, :], ACT.Copy,
                                     scale=scale).then_inc(hi_cut, 1)

            def turn_hi(stage):
                for k in range(KD):
                    act.wait_ge(turned, KD * stage + k + 1)
                    nc.scalar.activation(hT[:, 0, k, :], bank[:, k % 4, :], ACT.Copy,
                                         scale=S_ACT).then_inc(turned_hi, 1)

            def take(n, dst):
                act.wait_ge(tile_used, n + 1)
                nc.scalar.activation(dst, bank[:, 4 + n % 2, :], ACT.Copy,
                                     scale=1 / (S_W * S_ACT)).then_inc(columns_out, 1)

            def exponentials(m):
                act.wait_ge(max_done, m + 1)
                for t in range(TT):
                    nc.scalar.activation(probs[:, m % 2, t, :], probs[:, m % 2, t, :], ACT.Exp,
                                         bias=neg_max[:, m % 2, t:t + 1],
                                         accum_out=row_sum[:, m % 2, t:t + 1])
                nc.scalar.activation(sink_exp[:, m % 2, :], neg_max[:, m % 2, :], ACT.Exp,
                                     bias=sink[:, m:m + 1]).then_inc(exp_done, 1)

            def take_probs_T(m):
                act.wait_ge(probs_turned, m + 1)
                at_least(act, pv_done, m - 1)
                nc.scalar.activation(probs_T[:, m % 2, :], bank[:, 2 + m % 2, :], ACT.Copy).then_inc(probs_T_done, 1)

            def take_o(j):
                act.wait_ge(pv_done, 2 * j + 2)
                nc.scalar.activation(mixT[:, 0, j, :], bank[:, 6 + j % 2, :], ACT.Copy,
                                     scale=S_ACT).then_inc(o_hi, 1)

            def roots(stage):
                act.wait_ge(stats_done, stage + 1)
                nc.scalar.activation(std[:], variance[:], ACT.Sqrt).then_inc(rstd_done, 1)

            roots(0)
            split_hi(Tile(0))
            split_hi(Tile(1))
            turn_hi(0)
            act.wait_ge(pads_zero, 3)
            act.wait_ge(consts_in, 16 * 8)
            split_hi(Tile(2))
            take(0, kT[:, CHUNK:])
            split_hi(Tile(3))
            take(1, vT[:, CHUNK:])
            split_hi(Tile(4))
            take(2, qT[:, 0, :])
            act.wait_ge(v_turned, 1)
            for c in range(2):
                nc.scalar.activation(v_band[:, 4 * c:4 * c + 4, :],
                                     bank[:, 6 + c, :].rearrange("p (a b) -> p a b", a=4),
                                     ACT.Copy).then_inc(v_band_done, 1)
            split_hi(Tile(5))
            exponentials(0)
            take(3, qT[:, 1, :])
            split_hi(Tile(6))
            exponentials(1)
            take(4, qT[:, 2, :])
            take_probs_T(0)
            split_hi(Tile(7))
            exponentials(2)
            take(5, qT[:, 3, :])
            take_probs_T(1)
            split_hi(Tile(8))
            exponentials(3)
            take(6, pool_u[:, 0, PAD:])
            take_o(0)
            take_probs_T(2)
            split_hi(Tile(9))
            exponentials(4)
            take(7, pool_u[:, 1, PAD:])
            take_probs_T(3)
            split_hi(Tile(10))
            exponentials(5)
            take(8, pool_u[:, 2, PAD:])
            take_o(1)
            take_probs_T(4)
            split_hi(Tile(11))
            exponentials(6)
            take(9, pool_u[:, 3, PAD:])
            take_probs_T(5)
            exponentials(7)
            take_o(2)
            split_hi(Tile(12))
            take_probs_T(6)
            split_hi(Tile(13))
            take_probs_T(7)
            take_o(3)
            for g in range(GROUPS):
                act.wait_ge(pool_y_done, g + 1)
                nc.scalar.activation(mixT[:, 0, PAIRS + g, :], pool_y[:, g % 2, :], ACT.Copy,
                                     scale=S_ACT).then_inc(y_hi, 1)
            for n in range(T_O + 4, T_Q + SPLIT_AHEAD):
                split_hi(Tile(n))
            roots(1)
            turn_hi(1)

            def take_scores(hp, j):
                act.wait_ge(scores_done, hp + 1)
                dst = scores[:, hp, :] if isinstance(hp, int) else \
                    scores[:, bass.ds(hp, 1), :].rearrange("p a n -> p (a n)")
                nc.scalar.activation(dst, bank[:, 6 + j % 2, :], ACT.Copy).then_inc(scores_out, 1)

            def retrieve(it):
                for j in range(4):
                    t = Tile(T_Q + j, 4, it)
                    split_hi(t.plus(SPLIT_AHEAD))
                    act.wait_ge(tile_used, t.n + 1)
                    at_least(act, scores_done, 4 * it + j - 1)
                    nc.scalar.activation(queries[:, j % 2, :], bank[:, 4 + j % 2, :], ACT.Copy,
                                         scale=1 / (S_W * S_ACT)).then_inc(columns_out, 1)
                    if j:
                        take_scores(4 * it + j - 1, j - 1)
                take_scores(4 * it + 3, 3)

            retrieve(0)
            with act.Fori(1, N_Q // 4) as it:
                retrieve(it)
            for n in range(T_G, T_U):
                split_hi(Tile(n + SPLIT_AHEAD))
            for b in range(8):
                act.wait_ge(gate_lin, b + 1)
                nc.scalar.activation(ple_gate[:, b, :], ple_gate[:, b, :], ACT.Sigmoid).then_inc(gate_sig, 1)
            act.wait_ge(ple_out, 8)

            def gelu(t, slot, group):
                act.wait_ge(tile_used, t.n + 1)
                at_least(act, gelu_stored[slot], 16 * group)
                nc.scalar.activation(gelu_out[:, slot, :], bank[:, 4 + slot % 2, :], ACT.Gelu,
                                     scale=1 / (S_W * S_ACT)).then_inc(columns_out, 1)

            with act.Fori(0, U_TOPK // 4) as it:
                for j in range(4):
                    t = Tile(T_U + j, 4, it)
                    split_hi(t.plus(SPLIT_AHEAD))
                    gelu(t, j, it)
            for j in range(4):
                t = Tile(T_U + U_TOPK + j)
                split_hi(t.plus(SPLIT_AHEAD))
                if j == 1:
                    act.wait_ge(gate_shift, 1)
                    nc.scalar.activation(picked[:, 2], picked[:, 2], ACT.Exp).then_inc(gate_exp, 1)
                gelu(t, j, U_TOPK // 4)
            for w in range(2):
                act.wait_ge(rows_turned, w + 1)
                nc.scalar.activation(rows[:, w, :], bank[:, w, :], ACT.Copy).then_inc(rows_idx, 1)

            def take_gates(q, b, s, chunk_round):
                for four in range(4):
                    act.wait_ge(gates_prod, 4 * q + four + 1)
                    if b == 0 and four == 0:
                        at_least(act, gates_stored[s], 16 * chunk_round)
                    first = BATCH * b + 4 * four
                    nc.scalar.activation(gate_chunk[:, s, :, first:first + 4].rearrange("p n t -> p t n"),
                                         bank[:, four, :].rearrange("p (t n) -> p t n", t=4),
                                         ACT.Copy).then_inc(gates_out, 1)

            def build_gates(it):
                for s in range(2):
                    for j in range(4):
                        c = U_TOPK + U_SOFTMAX + 4 * s + j
                        t = Tile(T_U + c, 8, it)
                        split_hi(t.plus(SPLIT_AHEAD))
                        gelu(t, j, c // 4 + 2 * it)
                        if j % 2:
                            take_gates(4 * it + 2 * s + j // 2, j // 2, s, it)

            build_gates(0)
            with act.Fori(1, U_GATES // 8) as it:
                build_gates(it)
            e0 = U_TOPK + U_SOFTMAX + U_GATES
            with act.Fori(0, U_LAST // 4 - 1) as it:
                for j in range(4):
                    t = Tile(T_U + e0 + j, 4, it)
                    split_hi(t.plus(SPLIT_AHEAD))
                    gelu(t, j, e0 // 4 + it)

            def weight_high(v, slot):
                act.wait_ge(weight_done, v + 1)
                at_least(act, tile_used, T_V + v - RING + 1)
                nc.scalar.activation(weight_cut[:, slot, 0, :], weight[:, slot, :], ACT.Copy).then_inc(weight_hi, 1)

            for j in range(4):
                t = Tile(T_V - 4 + j)
                split_hi(t.plus(SPLIT_AHEAD), S_W if t.n + SPLIT_AHEAD < T_V else S_V)
                gelu(t, j, N_U // 4 - 1)
            weight_high(0, 0)
            weight_high(1, 1)

            def experts(pair):
                fixed = isinstance(pair, int)
                for v in range(8):
                    t = Tile(T_V + 8 * pair + v) if fixed else Tile(T_V + v, 8, pair)
                    if not fixed or t.n + SPLIT_AHEAD < T_ALL:
                        split_hi(t.plus(SPLIT_AHEAD), S_V)
                        weight_high(8 * pair + v + SPLIT_AHEAD, (v + SPLIT_AHEAD) % RING)

            with act.Fori(0, N_V // 8 - 1) as pair:
                experts(pair)
            experts(N_V // 8 - 1)
            roots(2)

        @block.vector
        def _(dve):
            own = Tally(dve, dve_own)

            def split_lo(t, scale=S_W):
                dve.wait_ge(hi_cut, t.n + 1)
                at_least(dve, tile_used, t.n - RING + 1)
                nc.vector.scalar_tensor_tensor(out=cut[:, t.slot, 1, :], in0=raw[:, t.slot, :], scalar=scale,
                                               in1=cut[:, t.slot, 0, :], op0=ALU.mult,
                                               op1=ALU.subtract).then_inc(lo_cut, 1)

            def turn_lo(stage):
                for k in range(KD):
                    dve.wait_ge(turned_hi, KD * stage + k + 1)
                    nc.vector.scalar_tensor_tensor(out=hT[:, 1, k, :], in0=bank[:, k % 4, :], scalar=S_ACT,
                                                   in1=hT[:, 0, k, :], op0=ALU.mult,
                                                   op1=ALU.subtract).then_inc(turned_lo, 1)

            def layer_norm(stage, t, done):
                own.link(nc.vector.tensor_scalar(hn[:, t, :], hn[:, t, :], moments[:, t, 0:1], rstd[:, t:t + 1],
                                                 ALU.subtract, ALU.mult))
                own.link(nc.vector.tensor_tensor(hn[:, t, :], hn[:, t, :], norm_rows[:, 2 * stage, :], ALU.mult))
                nc.vector.tensor_tensor(hn[:, t, :], hn[:, t, :], norm_rows[:, 2 * stage + 1, :],
                                        ALU.add).then_inc(done, 1)

            def row_stats(t):
                for h in range(2):
                    own.mark(nc.vector.bn_stats(stats[:, t, 6 * h:6 * h + 6], hn[:, t, h * HALF:(h + 1) * HALF]))

            def row_moments(stage, eps):
                own.settle()
                for t in range(TT):
                    own.mark(nc.vector.bn_aggr(moments[:, t, :], stats[:, t, :]))
                own.settle()
                nc.vector.tensor_scalar(variance[:], moments[:, :, 1], eps, None, ALU.add).then_inc(stats_done, 1)
                dve.wait_ge(rstd_done, stage + 1)
                own.link(nc.vector.reciprocal(rstd[:], std[:]))
                own.link(nc.vector.tensor_tensor(newton[:], rstd[:], rstd[:], ALU.mult))
                own.link(nc.vector.tensor_tensor(newton[:], newton[:], variance[:], ALU.mult))
                own.link(nc.vector.tensor_scalar(newton[:], newton[:], -0.5, 1.5, ALU.mult, ALU.add))
                own.link(nc.vector.tensor_tensor(rstd[:], rstd[:], newton[:], ALU.mult))

            def mask_and_max(m):
                dve.wait_ge(s_done, m + 1)
                at_least(dve, probs_turned, m - 1)
                buf = probs[:, m % 2]
                nc.vector.scalar_tensor_tensor(
                    out=buf, in0=bank[:, m % 2, :].rearrange("p (t k) -> p t k", t=TT), scalar=HD ** -0.5,
                    in1=alibi_sb[:, m:m + 1, :].to_broadcast([P, TT, P]), op0=ALU.mult,
                    op1=ALU.add).then_inc(s_out, 1)
                dve.wait_ge(s_out, m + 1)
                own.link(nc.vector.memset(buf[0:CHUNK, 0, 0:CHUNK], NEG))
                own.link(nc.vector.tensor_reduce(row_max[:, m % 2, :], buf, AX.X, ALU.max))
                nc.vector.tensor_scalar(neg_max[:, m % 2, :], row_max[:, m % 2, :], sink[:, m:m + 1], -1.0,
                                        ALU.max, ALU.mult).then_inc(max_done, 1)

            def normalise(m):
                dve.wait_ge(exp_done, m + 1)
                own.link(nc.vector.tensor_tensor(denom[:, m % 2, :], row_sum[:, m % 2, :], sink_exp[:, m % 2, :],
                                                 ALU.add))
                own.link(nc.vector.reciprocal(inv_den[:, m % 2, :], denom[:, m % 2, :]))
                nc.vector.tensor_tensor(probs[:, m % 2], probs[:, m % 2],
                                        inv_den[:, m % 2, :].unsqueeze(2).to_broadcast([P, TT, P]),
                                        ALU.mult).then_inc(probs_done, 1)

            def take_o(j):
                dve.wait_ge(o_hi, j + 1)
                nc.vector.scalar_tensor_tensor(out=mixT[:, 1, j, :], in0=bank[:, 6 + j % 2, :], scalar=S_ACT,
                                               in1=mixT[:, 0, j, :], op0=ALU.mult,
                                               op1=ALU.subtract).then_inc(o_lo, 1)

            def pool_mean(g):
                dve.wait_ge(columns_out, 7 + g)
                u = pool_u[:, g, :]
                cur, start, step, bufs = u, 0, 1, [pool_a, pool_b]
                while step < WINDOWS[g]:
                    start += step
                    nxt = bufs[0]
                    bufs.reverse()
                    own.link(nc.vector.tensor_tensor(nxt[:, start:], cur[:, start:],
                                                     cur[:, start - step:PAD + T - step], ALU.add))
                    cur, step = nxt, 2 * step
                own.link(nc.vector.scalar_tensor_tensor(out=pool_d[:, g, :], in0=cur[:, PAD:],
                                                        scalar=1.0 / WINDOWS[g], in1=u[:, PAD:], op0=ALU.mult,
                                                        op1=ALU.subtract))
                own.link(nc.vector.tensor_tensor(cur[:, PAD:2 * PAD], cur[:, PAD:2 * PAD], inv_count[:, g, :],
                                                 ALU.mult))
                nc.vector.tensor_tensor(pool_d[:, g, 0:PAD], cur[:, PAD:2 * PAD], u[:, PAD:2 * PAD],
                                        ALU.subtract).then_inc(pool_d_done, 1)
                dve.wait_ge(pool_d_done, g + 1)

            nc.vector.memset(kT[:, 0:CHUNK], 0.0).then_inc(pads_zero, 1)
            nc.vector.memset(vT[:, 0:CHUNK], 0.0).then_inc(pads_zero, 1)
            nc.vector.memset(pool_u[:, :, 0:PAD], 0.0).then_inc(pads_zero, 1)
            dve.wait_ge(pads_zero, 3)
            dve.wait_ge(x_in, 16 * TT)
            for t in range(TT):
                row_stats(t)
            row_moments(0, EPS)
            dve.wait_ge(consts_in, 16 * 8)
            for t in range(TT):
                layer_norm(0, t, norm_done)
            split_lo(Tile(0))
            split_lo(Tile(1))
            turn_lo(0)
            split_lo(Tile(2))
            split_lo(Tile(3))
            split_lo(Tile(4))
            mask_and_max(0)
            split_lo(Tile(5))
            mask_and_max(1)
            normalise(0)
            split_lo(Tile(6))
            mask_and_max(2)
            normalise(1)
            split_lo(Tile(7))
            mask_and_max(3)
            normalise(2)
            split_lo(Tile(8))
            take_o(0)
            mask_and_max(4)
            normalise(3)
            split_lo(Tile(9))
            mask_and_max(5)
            normalise(4)
            split_lo(Tile(10))
            take_o(1)
            mask_and_max(6)
            normalise(5)
            split_lo(Tile(11))
            mask_and_max(7)
            normalise(6)
            normalise(7)
            take_o(2)
            for g in range(GROUPS):
                pool_mean(g)
                if g == 0:
                    split_lo(Tile(12))
                    split_lo(Tile(13))
            take_o(3)
            for g in range(GROUPS):
                dve.wait_ge(pool_prod, g + 1)
                at_least(dve, y_lo, g - 1)
                nc.vector.tensor_scalar(pool_y[:, g % 2, :], bank[:, 2 + g % 2, :], pool_scale[:, g:g + 1], None,
                                        ALU.mult).then_inc(pool_y_done, 1)
                dve.wait_ge(y_hi, g + 1)
                nc.vector.scalar_tensor_tensor(out=mixT[:, 1, PAIRS + g, :], in0=pool_y[:, g % 2, :],
                                               scalar=S_ACT, in1=mixT[:, 0, PAIRS + g, :], op0=ALU.mult,
                                               op1=ALU.subtract).then_inc(y_lo, 1)
            for n in range(T_O + 4, T_Q + SPLIT_AHEAD):
                split_lo(Tile(n))
            dve.wait_ge(tile_used, T_Q)
            for b in range(8):
                nc.vector.scalar_tensor_tensor(
                    out=hn[:, b // 2, (b % 2) * HALF:(b % 2 + 1) * HALF], in0=bank[:, b, :],
                    scalar=1 / (S_W * S_ACT * ALPHA), in1=hn[:, b // 2, (b % 2) * HALF:(b % 2 + 1) * HALF],
                    op0=ALU.mult, op1=ALU.add).then_inc(resid_done, 1)
            dve.wait_ge(resid_done, 8)
            for t in range(TT):
                row_stats(t)
            row_moments(1, EPS / ALPHA ** 2)
            for t in range(TT):
                layer_norm(1, t, norm_done)
            turn_lo(1)
            for n in range(T_Q + SPLIT_AHEAD, T_U + SPLIT_AHEAD):
                split_lo(Tile(n))
            dve.wait_ge(tile_used, T_U)
            for b in range(8):
                nc.vector.scalar_tensor_tensor(out=ple_gate[:, b, :], in0=bank[:, b, :],
                                               scalar=1 / (S_W * S_ACT),
                                               in1=gate_b_row[:, (b % 2) * HALF:(b % 2 + 1) * HALF],
                                               op0=ALU.mult, op1=ALU.add).then_inc(gate_lin, 1)
            for b in range(8):
                dve.wait_ge(ple_prod, b + 1)
                dve.wait_ge(gate_sig, b + 1)
                nc.vector.scalar_tensor_tensor(out=ple_gate[:, b, :], in0=bank[:, b, :], scalar=1 / ALPHA,
                                               in1=ple_gate[:, b, :], op0=ALU.mult,
                                               op1=ALU.mult).then_inc(ple_out, 1)
            dve.wait_ge(ple_out, 8)
            for b in range(8):
                rows_b = hn[:, b // 2, (b % 2) * HALF:(b % 2 + 1) * HALF]
                nc.vector.tensor_tensor(rows_b, rows_b, ple_gate[:, b, :], ALU.add).then_inc(ple_added, 1)
            dve.wait_ge(ple_added, 8)
            dve.wait_ge(scores_out, N_Q)

            def top16(values, index, source, spare):
                def settle():
                    own.settle()
                    own.mark(nc.vector.memset(word[:], 0.0))

                settle()
                for t in range(TT):
                    own.mark(nc.vector.max(values[:, t, 0:8], source[:, t, :]))
                settle()
                for t in range(TT):
                    own.mark(nc.vector.max_index(index[:, t, 0:8], values[:, t, 0:8], source[:, t, :]))
                for t in range(TT):
                    own.mark(nc.vector.match_replace(spare[:, t, :], values[:, t, 0:8], source[:, t, :], LOWEST))
                settle()
                for t in range(TT):
                    own.mark(nc.vector.max(values[:, t, 8:16], spare[:, t, :]))
                settle()
                for t in range(TT):
                    own.mark(nc.vector.max_index(index[:, t, 8:16], values[:, t, 8:16], spare[:, t, :]))

            def add_sides():
                own.settle()
                own.mark(nc.vector.tensor_tensor(
                    sums.rearrange("p t (a b) -> p t a b", a=K),
                    top_v[:, 0].unsqueeze(3).to_broadcast([P, TT, K, K]),
                    top_v[:, 1].unsqueeze(2).to_broadcast([P, TT, K, K]), ALU.add))
                own.mark(nc.vector.tensor_copy(top_f, top_i))
                own.settle()

            def pick(head):
                own.settle()
                own.mark(nc.vector.tensor_single_scalar(half_i[:, 0], sum_i, 4, ALU.logical_shift_right))
                own.mark(nc.vector.tensor_single_scalar(half_i[:, 1], sum_i, K - 1, ALU.bitwise_and))
                own.settle()
                own.link(nc.vector.tensor_copy(half_f, half_i))
                for p in range(2):
                    hit3 = hit.rearrange("p (t k) m -> p t k m", t=TT)
                    own.link(nc.vector.tensor_tensor(
                        hit, iota_k_sb[:].unsqueeze(1).to_broadcast([P, TT * K, K]),
                        half_f[:, p].rearrange("p t k -> p (t k)").unsqueeze(2).to_broadcast([P, TT * K, K]),
                        ALU.is_equal))
                    own.link(nc.vector.tensor_tensor(
                        hit3, hit3, top_f[:, p].unsqueeze(2).to_broadcast([P, TT, K, K]), ALU.mult))
                    own.link(nc.vector.tensor_reduce(
                        picked[:, p, :, bass.ds(K * head, K)], hit3, AX.X, ALU.add))
                own.mark(nc.vector.tensor_copy(picked[:, 2, :, bass.ds(K * head, K)], sum_v))
                own.settle()

            per, before = 85, own.count
            with dve.Fori(0, U_TOPK // 4) as head:
                own.turns = per * head
                start = own.count
                t = Tile(T_U, 4, head)
                split_lo(t.plus(SPLIT_AHEAD))
                own.link(nc.vector.tensor_copy(side, scores[:, bass.ds(2 * head, 2), :]))
                for p in range(2):
                    if p:
                        split_lo(t.plus(SPLIT_AHEAD + 1))
                    top16(top_v[:, p], top_i[:, p], side[:, p].rearrange("p (t n) -> p t n", t=TT), replaced)
                    own.settle()
                add_sides()
                split_lo(t.plus(SPLIT_AHEAD + 2))
                top16(sum_v, sum_i, sums, sums_rep)
                split_lo(t.plus(SPLIT_AHEAD + 3))
                pick(head)
                assert own.count - start == per, own.count - start
            own.turns, own.count = 0, before + per * (U_TOPK // 4)
            t = Tile(T_U + U_TOPK)
            split_lo(t.plus(SPLIT_AHEAD))
            e_view = picked[:, 2].rearrange("p t (h k) -> p (t h) k", k=K)
            own.link(nc.vector.tensor_copy(e_sum, e_view[:, :, 0]))
            nc.vector.tensor_tensor(e_view, e_view, e_sum.unsqueeze(2).to_broadcast([P, TT * HEADS, K]),
                                    ALU.subtract).then_inc(gate_shift, 1)
            split_lo(t.plus(SPLIT_AHEAD + 1))
            split_lo(t.plus(SPLIT_AHEAD + 2))
            dve.wait_ge(gate_exp, 1)
            own.link(nc.vector.tensor_reduce(e_sum, e_view, AX.X, ALU.add))
            own.link(nc.vector.reciprocal(e_inv, e_sum))
            nc.vector.tensor_tensor(e_view, e_view, e_inv.unsqueeze(2).to_broadcast([P, TT * HEADS, K]),
                                    ALU.mult).then_inc(gates_done, 1)
            split_lo(t.plus(SPLIT_AHEAD + 3))
            dve.wait_ge(rows_turned, 3)
            nc.vector.tensor_scalar(rows[:, 2, :], bank[:, 2, :], S_G, None, ALU.mult).then_inc(rows_hi, 1)
            dve.wait_ge(rows_hi, 1)
            nc.vector.scalar_tensor_tensor(out=rows[:, 3, :], in0=bank[:, 2, :], scalar=S_G, in1=rows[:, 2, :],
                                           op0=ALU.mult, op1=ALU.subtract).then_inc(rows_done, 1)
            dve.wait_ge(rows_done, 1)
            dve.wait_ge(rows_idx, 2)

            def onehots(q, b, first):
                shape = [P, BATCH // OT, NKEY, OT]
                if not first:
                    dve.wait_ge(gates_prod, 4 * q - 4)
                own.link(nc.vector.tensor_copy(staged[:, b], rows[:, :, bass.ds(BATCH * q, BATCH)]))
                cols = [staged[:, b, w, :].rearrange("p (a t) -> p a t", t=OT).unsqueeze(2).to_broadcast(shape)
                        for w in range(4)]
                keys = iota_oh_sb[:].unsqueeze(1).to_broadcast(shape)
                own.mark(nc.vector.tensor_tensor(onehot[:, b], keys, cols[0], ALU.is_equal))
                own.mark(nc.vector.tensor_tensor(onehot[:, 2], keys, cols[1], ALU.is_equal))
                own.settle()
                own.mark(nc.vector.tensor_tensor(onehot_hi[:, b], onehot[:, 2], cols[2], ALU.mult))
                nc.vector.tensor_tensor(onehot_lo[:, b], onehot[:, 2], cols[3], ALU.mult).then_inc(onehot_done, 1)

            def build_gates(it, first):
                for s in range(2):
                    for j in range(4):
                        c = U_TOPK + U_SOFTMAX + 4 * s + j
                        split_lo(Tile(T_U + c + SPLIT_AHEAD, 8, it))
                        if j % 2 == 0:
                            q = 4 * it + 2 * s + j // 2
                            if not (first and s == 0 and j == 0):
                                dve.wait_ge(onehot_done, q)
                            onehots(q, j // 2, first and s == 0)

            build_gates(0, True)
            per, before = 16, own.count
            with dve.Fori(1, U_GATES // 8) as it:
                own.turns = per * (it - 1)
                start = own.count
                build_gates(it, False)
                assert own.count - start == per, own.count - start
            own.turns, own.count = 0, before + per * (U_GATES // 8 - 1)
            e0 = U_TOPK + U_SOFTMAX + U_GATES
            with dve.Fori(0, U_LAST // 4 - 1) as it:
                for j in range(4):
                    split_lo(Tile(T_U + e0 + j + SPLIT_AHEAD, 4, it))

            def make_weight(v, slot, parity, rounds):
                dve.wait_ge(pair_in[parity], 32 * (rounds + 1))
                at_least(dve, weight_lo, v - RING + 1)
                nc.vector.tensor_tensor(
                    weight[:, slot, :].rearrange("p (c t) -> p c t", t=TOK),
                    gelu_in[:, parity, slot, :].rearrange("p (c t) -> p c t", t=TOK),
                    gates_in[:, parity, :, slot, :], ALU.mult).then_inc(weight_done, 1)

            def weight_low(v, slot):
                dve.wait_ge(weight_hi, v + 1)
                nc.vector.tensor_tensor(weight_cut[:, slot, 1, :], weight[:, slot, :], weight_cut[:, slot, 0, :],
                                        ALU.subtract).then_inc(weight_lo, 1)

            for j in range(4):
                m = T_V - 4 + j + SPLIT_AHEAD
                split_lo(Tile(m), S_W if m < T_V else S_V)
            for v in range(SPLIT_AHEAD + 1):
                make_weight(v, v, 0, 0)
            for v in range(SPLIT_AHEAD):
                weight_low(v, v)

            def experts(pair):
                fixed = isinstance(pair, int)
                for v in range(8):
                    t = Tile(T_V + 8 * pair + v) if fixed else Tile(T_V + v, 8, pair)
                    if not fixed or t.n + SPLIT_AHEAD + 1 < T_ALL:
                        w = v + SPLIT_AHEAD + 1
                        make_weight(8 * pair + w, w % RING, (w // 4) % 2, pair + w // 8)
                    if not fixed or t.n + SPLIT_AHEAD < T_ALL:
                        weight_low(8 * pair + v + SPLIT_AHEAD, (v + SPLIT_AHEAD) % RING)
                        split_lo(t.plus(SPLIT_AHEAD), S_V)

            with dve.Fori(0, N_V // 8 - 1) as pair:
                experts(pair)
            experts(N_V // 8 - 1)
            for t in range(TT):
                if t < TT - 1:
                    dve.wait_ge(experts_done, t + 1)
                else:
                    dve.wait_ge(tile_used, T_ALL)
                for h in range(2):
                    rows_b = hn[:, t, h * HALF:(h + 1) * HALF]
                    nc.vector.scalar_tensor_tensor(out=rows_b, in0=bank[:, 2 * t + h, :],
                                                   scalar=1 / (S_G * S_V * ALPHA), in1=rows_b, op0=ALU.mult,
                                                   op1=ALU.add).then_inc(final_sum, 1)
                dve.wait_ge(final_sum, 2 * t + 2)
                row_stats(t)
            row_moments(2, EPS / ALPHA ** 2)
            for t in range(TT):
                layer_norm(2, t, final_done)


def _tables():
    q, k = np.arange(CHUNK)[:, None], np.arange(P)[None, :] - CHUNK
    dist = np.abs(q - k).astype(np.float32)
    heads = [m // 2 + 4 * (m % 2) for m in range(8)]
    slopes = np.array([2.0 ** (-(h + 1)) for h in heads], np.float32)
    alibi = np.tile(-slopes[None, :, None] * dist[:, None, :], (2, 1, 1)).astype(np.float32)
    counts = np.stack([1.0 / np.minimum(np.arange(1, PAD + 1), w) for w in WINDOWS]).astype(np.float32)
    counts = np.broadcast_to(counts.reshape(1, -1), (P, GROUPS * PAD))
    onehot = np.broadcast_to(np.arange(NKEY, dtype=np.float16)[None, :, None], (P, NKEY, OT))
    keys = np.broadcast_to(np.arange(K, dtype=np.float32)[None, :], (P, K))
    return alibi, counts, np.eye(P, dtype=np.float32), onehot, keys


def kernel(x, p, ln_in_g, ln_in_b, w_in, pool_w, pool_scale, attn_sinks, w_o, ln1_g, ln1_b, peer_wq,
           peer_subkeys, peer_u, peer_v, ple_w, ple_gate_w, ple_gate_b, ln2_g, ln2_b):
    import concourse.bacc as bacc
    from concourse.bass_utils import run_bass_kernel_spmd

    alibi, counts, ident, onehot, keys = _tables()
    a = np.asarray
    c = lambda v: np.ascontiguousarray(v, dtype=np.float32)
    w_in, w_o = a(w_in)[0], a(w_o)[0]
    pool_n = GROUPS * P
    pair_cols = [np.r_[j * HD:(j + 1) * HD, (j + 4) * HD:(j + 5) * HD] for j in range(PAIRS)]
    cols = [np.arange(2 * pool_n, 2 * pool_n + 2 * P)] + [pool_n + pc for pc in pair_cols] + [np.arange(pool_n)]
    w_in = w_in[:, np.concatenate(cols)]
    rows = [pool_n + pc for pc in pair_cols] + [np.arange(pool_n)]
    w_o = w_o[np.concatenate(rows)]
    by_columns = lambda w, n: w.reshape(KD, P, n, P).transpose(2, 1, 0, 3).reshape(n, P, D)
    by_rows = lambda w: w.reshape(KD, P, D)
    u = a(peer_u)[0].reshape(P, N_U, KD, P).transpose(1, 3, 2, 0).reshape(N_U, P, D)
    v = a(peer_v)[0].reshape(P, N_V, D).transpose(1, 0, 2)
    tiles = np.concatenate([by_columns(w_in, N_IN), by_rows(w_o), by_columns(a(peer_wq)[0], N_Q),
                            by_rows(a(ple_gate_w)[0]), u, v])
    order = [m // 2 + 4 * (m % 2) for m in range(8)]
    small = np.concatenate([
        np.broadcast_to(a(attn_sinks)[0][order][None, :], (P, 8)),
        a(pool_scale)[0].reshape(GROUPS, P).T, counts], axis=1)
    arrays = {
        "tiles": c(tiles),
        "x": c(a(x).reshape(T, D)),
        "ple_in": c(a(p).reshape(T, 2, P).transpose(2, 1, 0)),
        "ple_w": c(a(ple_w)[0].reshape(2, P, D).transpose(1, 0, 2)),
        "norms": c(np.stack([a(ln_in_g), a(ln_in_b), a(ln1_g)[0], a(ln1_b)[0], a(ln2_g)[0], a(ln2_b)[0]])),
        "gate_b": c(a(ple_gate_b)[0]),
        "small": c(small),
        "pool_w": c(a(pool_w)[0].transpose(1, 0, 2)),
        "subkeys": c(a(peer_subkeys)[0].reshape(2 * HEADS, NKEY, P).transpose(2, 0, 1)),
        "alibi": c(alibi),
        "ident": c(ident),
        "iota_oh": np.ascontiguousarray(onehot),
        "iota_k": c(keys),
    }
    nc = bacc.Bacc("TRN2", target_bir_lowering=False, num_devices=1)
    args = [nc.dram_tensor(f"{n}_dram", v_.shape, mybir.dt.from_np(v_.dtype), kind="ExternalInput").ap()
            for n, v_ in arrays.items()]
    out = nc.dram_tensor("out_dram", [T, D], F32, kind="ExternalOutput").ap()
    layer(nc, *args, out)
    r = run_bass_kernel_spmd(nc, [{f"{n}_dram": v_ for n, v_ in arrays.items()}], core_ids=[0])
    return r.results[0]["out_dram"].reshape(1, T, D)
```

```python
from contextlib import ExitStack

import numpy as np

import concourse.bass as bass
from concourse import mybir

F32 = mybir.dt.float32
F16 = mybir.dt.float16
U32 = mybir.dt.uint32
ALU = mybir.AluOpType
ACT = mybir.ActivationFunctionType
AX = mybir.AxisListType

P = 128
D = 1024
T = 512
TT = T // P
ND = TT - 1
TD = ND * P
KD = D // P
HALF = 512
CHUNK = 64
HD = 64
NCH = T // CHUNK
PAIRS = 4
GROUPS = 4
WINDOWS = (2, 4, 8, 16)
PAD = 16
HEADS = 8
K = 16
NKEY = 128
N_IN, N_O, N_Q, N_G, N_U, N_V = 10, 8, 16, 8, 128, 128
COLUMNS = ("k", "v", "q0", "q1", "u0", "q2", "u1", "q3", "u2", "u3")
IN_SBUF = {name: i + 1 for i, name in enumerate(COLUMNS)}
T_IN = 0
T_O = T_IN + N_IN
T_Q = T_O + N_O
T_G = T_Q + N_Q
T_U = T_G + N_G
T_V = T_U + N_U
T_ALL = T_V + N_V
AREA = 21500
RING = 4
SPLIT_AHEAD = 2
LOAD_AHEAD = 6
S_ACT = 16.0
S_W = 256.0
S_V = 16.0
S_G = 64.0
ALPHA = 2.0 ** 0.25
EPS = 1e-5
NEG = -1e30
LOWEST = -3.0e38

Q_HEADS = N_Q // 4 - 1
G_HEADS = 2
U_HEADS = HEADS - Q_HEADS - G_HEADS
U_TOPK = 8 * U_HEADS
U_SOFTMAX = 8
U_GATES = TD // 8
U_LAST = N_U - U_TOPK - U_SOFTMAX - U_GATES
U_TAIL = 8
TOK = 32
GCH = TD // TOK
HK = HEADS * K
ROW_RING = 4
DOTS_GATES = U_GATES
assert DOTS_GATES + 2 * (U_LAST - U_TAIL) == HK and U_LAST % 8 == 0 and N_V == HK
BATCH = 16
OT = 8
VG = 4


FINAL_ORDER = (ND, *range(ND))


class Tile:

    def __init__(self, c, k=0, it=0):
        self.c, self.k, self.it = c, k, it
        self.n = c + k * it if k else c
        self.slot = c % RING
        self.round = c // RING + (k // RING) * it if k else c // RING

    def plus(self, d):
        return Tile(self.c + d, self.k, self.it)


class Tally:

    def __init__(self, eng, sem):
        self.eng, self.sem, self.count, self.turns = eng, sem, 0, 0

    def mark(self, instruction):
        instruction.then_inc(self.sem, 1)
        self.count += 1

    def settle(self):
        self.eng.wait_ge(self.sem, self.turns + self.count)

    def link(self, instruction):
        self.mark(instruction)
        self.settle()


def at_least(eng, sem, value):
    if isinstance(value, int) and value <= 0:
        return
    eng.wait_ge(sem, value)


def layer(nc, tiles, u_rows, x, ple_in, ple_w, norms, gate_b, small, pool_w, subkeys, alibi, ident, iota_oh, iota_k,
          out):
    gelu_dram = nc.dram_tensor("gelu_scratch", [N_U // VG, P, VG, TD], F32, kind="Internal").ap()
    gates_dram = nc.dram_tensor("gates_scratch", [GCH, P, P, TOK], F32, kind="Internal").ap()

    with ExitStack() as ctx:
        def sb(name, shape, dt=F32):
            return ctx.enter_context(nc.sbuf_tensor(name, shape, dt))

        def sem(name):
            return ctx.enter_context(nc.semaphore(name))

        bank = ctx.enter_context(nc.psum_tensor("bank", [P, 8, HALF], F32))

        raw = sb("raw", [P, RING, D])
        cut = sb("cut", [P, RING, 2, D], F16)
        hn = sb("hn", [P, TT, D])
        hT = sb("hT", [P, 2, KD, T], F16)
        norm_rows = sb("norm_rows", [P, 2, D])
        gate_b_row = sb("gate_b_row", [P, D])
        stats = sb("stats", [P, TT, 12])
        moments = sb("moments", [P, TT, 2])
        word = sb("word", [P, 1])
        variance = sb("variance", [P, TT])
        std = sb("std", [P, TT])
        rstd = sb("rstd", [P, TT])
        newton = sb("newton", [P, TT])
        pool_scale_s = sb("pool_scale_s", [P, GROUPS])
        small_sb = sb("small_sb", [P, 8 + GROUPS + GROUPS * PAD])
        sink = small_sb[:, 0:8]
        pool_scale = small_sb[:, 8:8 + GROUPS]
        inv_count = small_sb[:, 8 + GROUPS:].rearrange("p (g t) -> p g t", g=GROUPS)
        ident_sb = sb("ident_sb", [P, P])
        iota_oh_sb = sb("iota_oh_sb", [P, NKEY, OT], F16)
        iota_k_sb = sb("iota_k_sb", [P, K])
        area = sb("area", [P, AREA])
        taken = [0]

        def part(shape, dt=F32):
            size = int(np.prod(shape)) * (2 if dt == F16 else 4) // 4
            a = area[:, taken[0]:taken[0] + size]
            taken[0] += size
            assert taken[0] <= AREA, taken
            if dt != F32:
                a = a.bitcast(dt)
            names = "abcd"[:len(shape)]
            if len(shape) > 1:
                a = a.rearrange(f"p ({' '.join(names)}) -> p {' '.join(names)}",
                                **{c: s for c, s in zip(names, shape)})
            return a

        kT = part([CHUNK + T])
        vT = part([CHUNK + T])
        qT = part([PAIRS, T])
        pool_u = part([GROUPS, PAD + T])
        pool_a = part([PAD + T])
        pool_b = part([PAD + T])
        pool_d = part([GROUPS, T])
        pool_w_sb = part([GROUPS, P])
        alibi_sb = part([8, P])
        v_band = part([NCH, P])
        probs = part([2, TT, P])
        probs_T = part([2, T])
        row_max = part([2, TT])
        neg_max = part([2, TT])
        row_sum = part([2, TT])
        sink_exp = part([2, TT])
        denom = part([2, TT])
        inv_den = part([2, TT])
        mixT = part([2, KD, T], F16)
        taken[0] = 0
        scores = part([2 * HEADS, T])
        queries = part([2, T])
        subkeys_sb = part([2 * HEADS, NKEY])
        side = part([2, T])
        replaced = part([TT, NKEY])
        sums = part([TT, K * K])
        sums_rep = part([TT, K * K])
        top_v = part([2, TT, K])
        top_i = part([2, TT, K], U32)
        sum_v = part([TT, K])
        sum_i = part([TT, K], U32)
        half_i = part([2, TT, K], U32)
        half_f = part([2, TT, K])
        top_f = part([2, TT, K])
        hit = part([TT * K, K])
        picked = part([3, TT, HEADS * K])
        e_sum = part([TT * HEADS])
        e_inv = part([TT * HEADS])
        rows = part([4, TD], F16)
        staged = part([2, 4, BATCH], F16)
        gelu_out = sb("gelu_out", [P, VG, TD])
        ple_gate = sb("ple_gate", [P, 8, HALF])
        ple_in_sb = gelu_out[:, :, :].rearrange("p s t -> p (s t)")[:, 0:2 * T].rearrange("p (k t) -> p k t", k=2)
        ple_w_sb = ple_gate[:, 0:4, :].rearrange("p (k a) n -> p k (a n)", k=2)
        ple_sb = sb("ple_sb", [P, 8, HALF])
        onehot = ple_gate[:, :, :].rearrange("p a b -> p (a b)").bitcast(F16).rearrange(
            "p (s a n t) -> p s a n t", s=4, a=BATCH // OT, t=OT)
        sparse_sum = ple_gate[:, 2 * ND:, :].rearrange("p a n -> p (a n)")
        expert_rows = ple_sb[:, :, :].rearrange("p (s a) n -> p s (a n)", s=ROW_RING)
        pool_word = sb("pool_word", [P, 1])
        expert_f = sb("expert_f", [P, 2, HK])
        expert_id = sb("expert_id", [P, 2, HK], U32)
        ids_now = sb("ids_now", [P, 2, 8], U32)
        dots_now = sb("dots_now", [P, 16])
        dots = sb("dots", [P, HK])
        sparse_w = sb("sparse_w", [P, HK])
        sparse_w_now = sb("sparse_w_now", [P, 8])
        taken[0] = 0
        gate_chunk = part([2, P, TOK])
        onehot_hi = part([2, BATCH // OT, NKEY, OT], F16)
        onehot_lo = part([2, BATCH // OT, NKEY, OT], F16)
        taken[0] = 0
        gelu_in = part([2, VG, TD])
        gates_in = part([2, GCH, VG, TOK])
        weight = part([RING, TD])
        weight_cut = part([RING, 2, TD], F16)

        consts_in, ple_loaded, subkeys_in, norms_in = (sem(n) for n in (
            "consts_in", "ple_loaded", "subkeys_in", "norms_in"))
        x_in = [sem(f"x_in{t}") for t in range(TT)]
        tile_in = [sem(f"tile_in{s}") for s in range(RING)]
        hi_cut, lo_cut, tile_used = sem("hi_cut"), sem("lo_cut"), sem("tile_used")
        columns_out = sem("columns_out")
        stats_done, rstd_done, norm_done = sem("stats_done"), sem("rstd_done"), sem("norm_done")
        turned, turned_hi, turned_lo = sem("turned"), sem("turned_hi"), sem("turned_lo")
        pads_zero, v_turned, v_band_done = sem("pads_zero"), sem("v_turned"), sem("v_band_done")
        s_done, s_out, max_done, exp_done, probs_done = (sem(n) for n in (
            "s_done", "s_out", "max_done", "exp_done", "probs_done"))
        probs_turned, probs_T_done, pv_done, o_hi, o_lo = (sem(n) for n in (
            "probs_turned", "probs_T_done", "pv_done", "o_hi", "o_lo"))
        pool_d_done, pool_prod, pool_own, scale_done, y_hi, y_lo = (sem(n) for n in (
            "pool_d_done", "pool_prod", "pool_own", "scale_done", "y_hi", "y_lo"))
        mix_done, resid_done = sem("mix_done"), sem("resid_done")
        scores_done, scores_out = sem("scores_done"), sem("scores_out")
        ple_prod, ple_out, gate_prod, gate_lin, gate_biased, gate_sig, gated, ple_added = (sem(n) for n in (
            "ple_prod", "ple_out", "gate_prod", "gate_lin", "gate_biased", "gate_sig", "gated", "ple_added"))
        rows_in = [sem(f"rows_in{s}") for s in range(ROW_RING)]
        ids_done, rows_used, dots_done, dots_gelu = (sem(n) for n in (
            "ids_done", "rows_used", "dots_done", "dots_gelu"))
        picks_done, gate_shift, gate_exp, gates_done = (sem(n) for n in (
            "picks_done", "gate_shift", "gate_exp", "gates_done"))
        rows_turned, rows_idx, rows_hi, rows_done = (sem(n) for n in (
            "rows_turned", "rows_idx", "rows_hi", "rows_done"))
        onehot_done, gates_prod, gates_out = sem("onehot_done"), sem("gates_prod"), sem("gates_out")
        gelu_stored = [sem(f"gelu_stored{s}") for s in range(VG)]
        gates_stored = [sem(f"gates_stored{s}") for s in range(2)]
        pair_in = [sem(f"pair_in{s}") for s in range(2)]
        weight_done, weight_hi, weight_lo = sem("weight_done"), sem("weight_hi"), sem("weight_lo")
        experts_done, final_sum, final_done, stored = (sem(n) for n in (
            "experts_done", "final_sum", "final_done", "stored"))
        dve_own = sem("dve_own")

        block = ctx.enter_context(nc.Block())

        @block.sync
        def _(sp):
            def load(t):
                at_least(sp, lo_cut, t.plus(1 - RING).n)
                src = tiles[t.n] if isinstance(t.n, int) else tiles[bass.ds(t.n, 1)].rearrange("a p n -> (a p) n")
                sp.dma_start(raw[:, t.slot, :], src).then_inc(tile_in[t.slot], 16)

            def store_gelu(group, slot, expert):
                sp.wait_ge(columns_out, N_IN + N_Q + 1 + expert)
                dst = gelu_dram[group, :, slot, :] if isinstance(group, int) else \
                    gelu_dram[bass.ds(group, 1), :, slot, :].rearrange("a p t -> (a p) t")
                sp.dma_start(dst, gelu_out[:, slot, :]).then_inc(gelu_stored[slot], 16)

            def load_pair(group, parity):
                if isinstance(group, int):
                    src = gelu_dram[group]
                else:
                    src = gelu_dram[bass.ds(group, 1)].rearrange("a p e t -> (a p) e t")
                sp.dma_start(gelu_in[:, parity], src).then_inc(pair_in[parity], 16)
                first = VG * group
                sp.dma_start(gates_in[:, parity],
                             gates_dram[:, :, bass.ds(first, VG), :].rearrange("c p e t -> p c e t")
                             ).then_inc(pair_in[parity], 16)

            def load_norms(stage):
                at_least(sp, norm_done, TT * stage)
                sp.dma_start(norm_rows[:], norms[stage].partition_broadcast(P)).then_inc(norms_in, 16)

            for t in range(TT):
                sp.dma_start(hn[:, t, :], x[t * P:(t + 1) * P, :]).then_inc(x_in[t], 16)
            sp.dma_start(ple_in_sb, ple_in).then_inc(ple_loaded, 16)
            sp.dma_start(ple_w_sb, ple_w).then_inc(ple_loaded, 16)
            load_norms(0)
            sp.dma_start(ident_sb[:], ident).then_inc(consts_in, 16)
            load(Tile(0))
            load(Tile(1))
            sp.dma_start(alibi_sb, alibi).then_inc(consts_in, 16)
            sp.dma_start(small_sb[:], small).then_inc(consts_in, 16)
            sp.dma_start(pool_w_sb, pool_w).then_inc(consts_in, 16)
            load(Tile(2))
            load(Tile(3))
            sp.dma_start(iota_oh_sb[:], iota_oh).then_inc(consts_in, 16)
            sp.dma_start(iota_k_sb[:], iota_k).then_inc(consts_in, 16)
            sp.dma_start(gate_b_row[:], gate_b.partition_broadcast(P)).then_inc(consts_in, 16)
            load_norms(1)
            for n in range(4, T_Q + RING):
                load(Tile(n))
            sp.wait_ge(resid_done, 8)
            sp.dma_start(subkeys_sb, subkeys).then_inc(subkeys_in, 16)
            for n in range(T_Q + RING, T_Q + LOAD_AHEAD):
                load(Tile(n))
            load_norms(2)
            for n in range(T_Q, T_U):
                load(Tile(n + LOAD_AHEAD))
            with sp.Fori(0, U_TOPK // 4) as it:
                for j in range(4):
                    load(Tile(T_U + j + LOAD_AHEAD, 4, it))
                    store_gelu(it, j, 4 * it + j)
            for c in range(U_TOPK, U_TOPK + U_SOFTMAX):
                load(Tile(T_U + c + LOAD_AHEAD))
                store_gelu(c // 4, c % 4, c)
            e0 = U_TOPK + U_SOFTMAX
            with sp.Fori(0, U_GATES // 8) as it:
                for s in range(2):
                    for j in range(4):
                        c = e0 + 4 * s + j
                        load(Tile(T_U + c + LOAD_AHEAD, 8, it))
                        store_gelu(e0 // 4 + s + 2 * it, j, c + 8 * it)
                    sp.wait_ge(gates_out, 16 * it + 8 * s + 8)
                    sp.dma_start(gates_dram[bass.ds(2 * it + s, 1)].rearrange("a p n t -> (a p) n t"),
                                 gate_chunk[:, s]).then_inc(gates_stored[s], 16)
            e0 += U_GATES
            with sp.Fori(0, U_LAST // 4 - 1) as it:
                for j in range(4):
                    load(Tile(T_U + e0 + j + LOAD_AHEAD, 4, it))
                    store_gelu(e0 // 4 + it, j, e0 + j + 4 * it)
            for s in range(2):
                sp.wait_ge(gates_stored[s], 16 * (GCH // 2))
            for j in range(VG):
                sp.wait_ge(gelu_stored[j], 16 * 2)
            load_pair(0, 0)
            load_pair(1, 1)
            for j in range(4):
                load(Tile(T_V - 4 + j + LOAD_AHEAD))
                store_gelu(N_U // 4 - 1, j, N_U - 4 + j)
            for j in range(VG):
                sp.wait_ge(gelu_stored[j], 16 * (N_U // VG))

            def experts(pair):
                for s in range(2):
                    for j in range(VG):
                        t = Tile(T_V + 4 * s + j, 8, pair) if not isinstance(pair, int) else \
                            Tile(T_V + 8 * pair + 4 * s + j)
                        if not isinstance(pair, int) or t.n + LOAD_AHEAD < T_ALL:
                            load(t.plus(LOAD_AHEAD))
                        if j == 1 and not (isinstance(pair, int) and 2 * pair + s + 2 >= N_U // VG):
                            sp.wait_ge(weight_done, 8 * pair + 4 * (s + 1))
                            load_pair(2 * pair + s + 2, s)

            with sp.Fori(0, N_V // 8 - 1) as pair:
                experts(pair)
            experts(N_V // 8 - 1)
            for i, t in enumerate(FINAL_ORDER):
                sp.wait_ge(final_done, i + 1)
                sp.dma_start(out[t * P:(t + 1) * P, :], hn[:, t, :]).then_inc(stored, 16)
            sp.wait_ge(stored, 16 * TT)

        @block.gpsimd
        def _(pool):
            own = Tally(pool, pool_own)
            pool.wait_ge(pads_zero, 3)
            pool.wait_ge(consts_in, 16 * 7)
            for g in range(GROUPS):
                pool.wait_ge(columns_out, IN_SBUF[f"u{g}"])
                u = pool_u[:, g, :]
                cur, start, step, bufs = u, 0, 1, [pool_a, pool_b]
                while step < WINDOWS[g]:
                    start += step
                    nxt = bufs[0]
                    bufs.reverse()
                    own.link(nc.gpsimd.tensor_tensor(nxt[:, start:], cur[:, start:],
                                                     cur[:, start - step:PAD + T - step], ALU.add))
                    cur, step = nxt, 2 * step
                own.mark(nc.gpsimd.tensor_tensor(pool_d[:, g, 0:PAD], cur[:, PAD:2 * PAD], inv_count[:, g, :],
                                                 ALU.mult))
                own.mark(nc.gpsimd.tensor_scalar(pool_d[:, g, PAD:], cur[:, 2 * PAD:], 1.0 / WINDOWS[g], None,
                                                 ALU.mult))
                own.settle()
                nc.gpsimd.tensor_tensor(pool_d[:, g, :], pool_d[:, g, :], u[:, PAD:],
                                        ALU.subtract).then_inc(pool_d_done, 1)

            pool.wait_ge(ids_done, 1)
            pool.wait_ge(ple_added, ND)
            pool.wait_ge(gated, TT)
            v_rows = tiles.rearrange("n p d -> (n p) d")

            def gather(kind, it):
                def carry():
                    own.settle()
                    own.mark(nc.gpsimd.tensor_tensor(pool_word[:], pool_word[:], pool_word[:], ALU.add))

                for s in range(2):
                    carry()
                    own.mark(nc.gpsimd.tensor_copy(ids_now[:, s, :],
                                                   expert_id[:, kind, bass.ds(16 * it + 8 * s, 8)]))
                    for j in range(8):
                        if kind == 1 or not isinstance(it, int) or 8 * s + j >= ROW_RING:
                            pool.wait_ge(rows_used, HK * kind + 16 * it + 8 * s + j - ROW_RING + 1)
                        carry()
                        nc.gpsimd.indirect_dma_start(
                            expert_rows[:, j % ROW_RING, :], None, v_rows if kind else u_rows,
                            bass.IndirectOffsetOnAxis(ap=ids_now[:, s, j:j + 1], axis=0)
                        ).then_inc(rows_in[j % ROW_RING], 16)

            GATHER_OWN = 20
            own.link(nc.gpsimd.memset(pool_word[:], 0.0))
            gather(0, 0)
            before = own.count
            with pool.Fori(1, HK // 16) as it:
                own.turns, own.count = GATHER_OWN * (it - 1), before
                gather(0, it)
            before += GATHER_OWN * (HK // 16 - 1)
            with pool.Fori(0, HK // 16) as it:
                own.turns, own.count = GATHER_OWN * it, before
                gather(1, it)
                assert own.count - before == GATHER_OWN

        @block.tensor
        def _(pe):
            def turn(stage):
                for i in range(2 * TT):
                    t, kh = i // 2, i % 2
                    pe.wait_ge(norm_done, TT * stage + t + 1)
                    at_least(pe, turned_hi, KD * stage + i - 3)
                    at_least(pe, turned_lo, KD * stage + i - 3)
                    for k in range(4):
                        last = nc.tensor.transpose(bank[:, i % 4, k * P:(k + 1) * P],
                                                   hn[:, t, (4 * kh + k) * P:(4 * kh + k + 1) * P], ident_sb[:])
                    last.then_inc(turned, 1)

            def columns(t, index, parity, width=T):
                pe.wait_ge(lo_cut, t.n + 1)
                at_least(pe, columns_out, index - 1)
                for k in range(KD):
                    w = [cut[:, t.slot, part_, k * P:(k + 1) * P] for part_ in range(2)]
                    dst = bank[:, 4 + parity, 0:width]
                    nc.tensor.matmul(dst, w[0], hT[:, 0, k, 0:width], start=(k == 0), stop=False)
                    nc.tensor.matmul(dst, w[0], hT[:, 1, k, 0:width], start=False, stop=False)
                    last = nc.tensor.matmul(dst, w[1], hT[:, 0, k, 0:width], start=False, stop=(k == KD - 1))
                last.then_inc(tile_used, 1)

            def tokens(t, lhs, first, last_tile, count=None, token_tiles=TT):
                pe.wait_ge(lo_cut, t.n + 1)
                for tt in range(token_tiles):
                    for step, (a, b) in enumerate(((0, 0), (0, 1), (1, 0))):
                        for h in range(2):
                            mm = nc.tensor.matmul(bank[:, 2 * tt + h, :], lhs(a)[:, tt * P:(tt + 1) * P],
                                                  cut[:, t.slot, b, h * HALF:(h + 1) * HALF],
                                                  start=(first and step == 0), stop=(last_tile and step == 2))
                    if count is not None and tt < token_tiles - 1:
                        mm.then_inc(count, 1)
                mm.then_inc(tile_used, 1)

            def values():
                pe.wait_ge(columns_out, 2)
                for c in range(NCH):
                    last = nc.tensor.transpose(bank[:, 6 + c // 4, (c % 4) * P:(c % 4 + 1) * P],
                                               vT[:, c * CHUNK:c * CHUNK + P], ident_sb[:])
                last.then_inc(v_turned, 1)

            def attn_scores(m):
                j, kv = m // 2, m % 2
                pe.wait_ge(columns_out, IN_SBUF[f"q{j}"])
                at_least(pe, s_out, m - 1)
                r = slice(kv * HD, (kv + 1) * HD)
                for c in range(NCH):
                    last = nc.tensor.matmul(
                        bank[(c % 2) * CHUNK:(c % 2 + 1) * CHUNK, m % 2, (c // 2) * P:(c // 2 + 1) * P],
                        qT[r, j, c * CHUNK:(c + 1) * CHUNK], kT[r, c * CHUNK:c * CHUNK + P],
                        start=True, stop=True, skip_group_check=True)
                last.then_inc(s_done, 1)

            def turn_probs(m, pooled=0):
                pe.wait_ge(probs_done, m + 1)
                at_least(pe, probs_T_done, m - 1)
                at_least(pe, y_lo, pooled)
                for t in range(TT):
                    last = nc.tensor.transpose(bank[:, 2 + m % 2, t * P:(t + 1) * P], probs[:, m % 2, t, :],
                                               ident_sb[:])
                last.then_inc(probs_turned, 1)

            def attend(m):
                j, kv = m // 2, m % 2
                pe.wait_ge(probs_T_done, m + 1)
                pe.wait_ge(v_band_done, 2)
                at_least(pe, o_lo, j - 1)
                r = slice(kv * HD, (kv + 1) * HD)
                for c in range(NCH):
                    last = nc.tensor.matmul(bank[r, 6 + j % 2, c * CHUNK:(c + 1) * CHUNK], v_band[:, c, r],
                                            probs_T[:, m % 2, c * CHUNK:(c + 1) * CHUNK],
                                            start=True, stop=True, skip_group_check=True)
                last.then_inc(pv_done, 1)

            def pool_product(g, turned_m):
                pe.wait_ge(pool_d_done, g + 1)
                pe.wait_ge(probs_T_done, turned_m)
                at_least(pe, y_lo, g - 1)
                nc.tensor.matmul(bank[:, 2 + g % 2, :], pool_w_sb[:, g, :], pool_d[:, g, :],
                                 start=True, stop=True).then_inc(pool_prod, 1)

            pe.wait_ge(ple_loaded, 32)
            for b in range(8):
                for k in range(2):
                    mm = nc.tensor.matmul(bank[:, b, :], ple_in_sb[:, k, (b // 2) * P:(b // 2 + 1) * P],
                                          ple_w_sb[:, k, (b % 2) * HALF:(b % 2 + 1) * HALF],
                                          start=(k == 0), stop=(k == 1))
                mm.then_inc(ple_prod, 1)
            pe.wait_ge(consts_in, 16 * 7)
            pe.wait_ge(ple_out, 8)
            turn(0)
            pe.wait_ge(turned_lo, KD)
            pe.wait_ge(pads_zero, 3)
            for n in range(3):
                columns(Tile(n), n, n % 2)
            values()
            attn_scores(0)
            columns(Tile(3), 3, 1)
            attn_scores(1)
            columns(Tile(4), 4, 0)
            turn_probs(0)
            attn_scores(2)
            columns(Tile(5), 5, 1)
            attend(0)
            turn_probs(1)
            attn_scores(3)
            columns(Tile(6), 6, 0)
            attend(1)
            turn_probs(2)
            attn_scores(4)
            columns(Tile(7), 7, 1)
            attend(2)
            pool_product(0, 3)
            turn_probs(3)
            attn_scores(5)
            columns(Tile(8), 8, 0)
            attend(3)
            turn_probs(4, 1)
            attn_scores(6)
            columns(Tile(9), 9, 1)
            attend(4)
            pool_product(1, 5)
            turn_probs(5, 2)
            attn_scores(7)
            attend(5)
            pool_product(2, 6)
            turn_probs(6, 3)
            attend(6)
            turn_probs(7)
            attend(7)
            pool_product(3, 8)
            pe.wait_ge(columns_out, N_IN)
            pe.wait_ge(o_lo, PAIRS)
            pe.wait_ge(y_lo, GROUPS)
            pe.wait_ge(s_out, 8)
            for k in range(KD):
                tokens(Tile(T_O + k), lambda a, k=k: mixT[:, a, k, :], k == 0, k == KD - 1,
                       mix_done if k == KD - 1 else None)
            pe.wait_ge(resid_done, 8)
            turn(1)
            pe.wait_ge(turned_lo, 2 * KD)
            pe.wait_ge(subkeys_in, 16)

            def key_scores(hp, j, index):
                pe.wait_ge(columns_out, index + 1)
                at_least(pe, scores_out, hp - 1)
                for t in range(TT):
                    last = nc.tensor.matmul(bank[:, 6 + j % 2, t * P:(t + 1) * P],
                                            queries[:, j % 2, t * P:(t + 1) * P],
                                            subkeys_sb[:, hp, :] if isinstance(hp, int) else
                                            subkeys_sb[:, bass.ds(hp, 1), :].rearrange("p a n -> p (a n)"),
                                            start=True, stop=True, skip_group_check=True)
                last.then_inc(scores_done, 1)

            def retrieve(it):
                for j in range(4):
                    columns(Tile(T_Q + j, 4, it), N_IN + 4 * it + j, j % 2)
                    if j:
                        key_scores(4 * it + j - 1, j - 1, N_IN + 4 * it + j - 1)
                key_scores(4 * it + 3, 3, N_IN + 4 * it + 3)

            retrieve(0)
            with pe.Fori(1, N_Q // 4) as it:
                retrieve(it)
            pe.wait_ge(columns_out, N_IN + N_Q)
            pe.wait_ge(scores_out, N_Q)
            for k in range(KD):
                tokens(Tile(T_G + k), lambda a, k=k: hT[:, a, k, :], k == 0, k == KD - 1,
                       gate_prod if k == KD - 1 else None)
            pe.wait_ge(gate_lin, 8)
            u_index = N_IN + N_Q
            with pe.Fori(0, U_TOPK // 4) as it:
                for j in range(4):
                    columns(Tile(T_U + j, 4, it), u_index + 4 * it + j, j % 2, TD)
            for j in range(U_SOFTMAX):
                if j == U_SOFTMAX - 2:
                    pe.wait_ge(gates_done, 1)
                    for w in range(3):
                        for t in range(ND):
                            last = nc.tensor.transpose(bank[:, w, t * P:(t + 1) * P], picked[:, w, t, :],
                                                       ident_sb[:])
                        last.then_inc(rows_turned, 1)
                columns(Tile(T_U + U_TOPK + j), u_index + U_TOPK + j, j % 2, TD)
            pe.wait_ge(rows_idx, 2)
            pe.wait_ge(rows_done, 1)

            def gate_products(q, b):
                pe.wait_ge(onehot_done, q + 1)
                for four in range(4):
                    at_least(pe, gates_out, 4 * q + four - 3)
                    for u in range(4):
                        a, t = (4 * four + u) // OT, (4 * four + u) % OT
                        dst = bank[:, four, u * P:(u + 1) * P]
                        nc.tensor.matmul(dst, onehot[:, b, a, :, t], onehot_hi[:, b, a, :, t],
                                         start=True, stop=False, skip_group_check=True)
                        mm = nc.tensor.matmul(dst, onehot[:, b, a, :, t], onehot_lo[:, b, a, :, t],
                                              start=False, stop=True, skip_group_check=True)
                    mm.then_inc(gates_prod, 1)

            def build_gates(it):
                for s in range(2):
                    for j in range(4):
                        c = U_TOPK + U_SOFTMAX + 4 * s + j
                        columns(Tile(T_U + c, 8, it), u_index + c + 8 * it, j % 2, TD)
                        if j % 2:
                            gate_products(4 * it + 2 * s + j // 2, j // 2)

            build_gates(0)
            with pe.Fori(1, U_GATES // 8) as it:
                build_gates(it)
            e0 = U_TOPK + U_SOFTMAX + U_GATES
            with pe.Fori(0, U_LAST // 4) as it:
                for j in range(4):
                    columns(Tile(T_U + e0 + j, 4, it), u_index + e0 + j + 4 * it, j % 2, TD)
            pe.wait_ge(columns_out, u_index + N_U)
            pe.wait_ge(gates_out, TD // 4)

            def experts(pair):
                fixed = isinstance(pair, int)
                for v in range(8):
                    t = Tile(T_V + 8 * pair + v) if fixed else Tile(T_V + v, 8, pair)
                    pe.wait_ge(weight_lo, 8 * pair + v + 1)
                    end = fixed and t.n == T_ALL - 1
                    tokens(t, lambda a, v=v: weight_cut[:, v % RING, a, :], fixed and t.n == T_V, end,
                           experts_done if end else None, ND)

            experts(0)
            with pe.Fori(1, N_V // 8 - 1) as pair:
                experts(pair)
            experts(N_V // 8 - 1)

        @block.scalar
        def _(act):
            def split_hi(t, scale=S_W):
                act.wait_ge(tile_in[t.slot], 16 * (t.round + 1))
                at_least(act, tile_used, t.n - RING + 1)
                nc.scalar.activation(cut[:, t.slot, 0, :], raw[:, t.slot, :], ACT.Copy,
                                     scale=scale).then_inc(hi_cut, 1)

            def turn_hi(stage):
                for i in range(2 * TT):
                    t, kh = i // 2, i % 2
                    act.wait_ge(turned, KD * stage + i + 1)
                    nc.scalar.activation(hT[:, 0, 4 * kh:4 * kh + 4, t * P:(t + 1) * P],
                                         bank[:, i % 4, :].rearrange("p (k t) -> p k t", k=4), ACT.Copy,
                                         scale=S_ACT).then_inc(turned_hi, 1)

            def take(n, dst):
                act.wait_ge(tile_used, n + 1)
                nc.scalar.activation(dst, bank[:, 4 + n % 2, :], ACT.Copy,
                                     scale=1 / (S_W * S_ACT)).then_inc(columns_out, 1)

            def exponentials(m):
                act.wait_ge(max_done, m + 1)
                for t in range(TT):
                    nc.scalar.activation(probs[:, m % 2, t, :], probs[:, m % 2, t, :], ACT.Exp,
                                         bias=neg_max[:, m % 2, t:t + 1],
                                         accum_out=row_sum[:, m % 2, t:t + 1])
                nc.scalar.activation(sink_exp[:, m % 2, :], neg_max[:, m % 2, :], ACT.Exp,
                                     bias=sink[:, m:m + 1]).then_inc(exp_done, 1)

            def take_probs_T(m):
                act.wait_ge(probs_turned, m + 1)
                at_least(act, pv_done, m - 1)
                nc.scalar.activation(probs_T[:, m % 2, :], bank[:, 2 + m % 2, :], ACT.Copy).then_inc(probs_T_done, 1)

            def take_o(j):
                act.wait_ge(pv_done, 2 * j + 2)
                nc.scalar.activation(mixT[:, 0, j, :], bank[:, 6 + j % 2, :], ACT.Copy,
                                     scale=S_ACT).then_inc(o_hi, 1)

            def roots(stage):
                act.wait_ge(stats_done, stage + 1)
                nc.scalar.activation(std[:], variance[:], ACT.Sqrt).then_inc(rstd_done, 1)

            def take_y(g):
                act.wait_ge(pool_prod, g + 1)
                act.wait_ge(scale_done, 1)
                nc.scalar.activation(mixT[:, 0, PAIRS + g, :], bank[:, 2 + g % 2, :], ACT.Copy,
                                     scale=pool_scale_s[:, g:g + 1]).then_inc(y_hi, 1)

            roots(0)
            for b in range(8):
                act.wait_ge(ple_prod, b + 1)
                nc.scalar.activation(ple_sb[:, b, :], bank[:, b, :], ACT.Copy).then_inc(ple_out, 1)
            split_hi(Tile(0))
            split_hi(Tile(1))
            turn_hi(0)
            act.wait_ge(pads_zero, 3)
            act.wait_ge(consts_in, 16 * 7)
            split_hi(Tile(2))
            take(0, kT[:, CHUNK:])
            split_hi(Tile(3))
            take(1, vT[:, CHUNK:])
            split_hi(Tile(4))
            take(2, qT[:, 0, :])
            act.wait_ge(v_turned, 1)
            for c in range(2):
                nc.scalar.activation(v_band[:, 4 * c:4 * c + 4, :],
                                     bank[:, 6 + c, :].rearrange("p (a b) -> p a b", a=4),
                                     ACT.Copy).then_inc(v_band_done, 1)
            split_hi(Tile(5))
            exponentials(0)
            take(3, qT[:, 1, :])
            split_hi(Tile(6))
            exponentials(1)
            take(4, pool_u[:, 0, PAD:])
            take_probs_T(0)
            split_hi(Tile(7))
            exponentials(2)
            take(5, qT[:, 2, :])
            take_probs_T(1)
            split_hi(Tile(8))
            exponentials(3)
            take(6, pool_u[:, 1, PAD:])
            take_probs_T(2)
            take_o(0)
            split_hi(Tile(9))
            exponentials(4)
            take(7, qT[:, 3, :])
            take_y(0)
            take_probs_T(3)
            split_hi(Tile(10))
            exponentials(5)
            take(8, pool_u[:, 2, PAD:])
            take_probs_T(4)
            take_o(1)
            split_hi(Tile(11))
            exponentials(6)
            take(9, pool_u[:, 3, PAD:])
            take_y(1)
            take_probs_T(5)
            exponentials(7)
            split_hi(Tile(12))
            take_y(2)
            take_probs_T(6)
            take_o(2)
            split_hi(Tile(13))
            take_probs_T(7)
            take_o(3)
            take_y(3)
            for n in range(T_O + 4, T_Q + SPLIT_AHEAD):
                split_hi(Tile(n))
            roots(1)
            turn_hi(1)

            def take_scores(hp, j):
                act.wait_ge(scores_done, hp + 1)
                dst = scores[:, hp, :] if isinstance(hp, int) else \
                    scores[:, bass.ds(hp, 1), :].rearrange("p a n -> p (a n)")
                nc.scalar.activation(dst, bank[:, 6 + j % 2, :], ACT.Copy).then_inc(scores_out, 1)

            def retrieve(it):
                for j in range(4):
                    t = Tile(T_Q + j, 4, it)
                    split_hi(t.plus(SPLIT_AHEAD))
                    act.wait_ge(tile_used, t.n + 1)
                    at_least(act, scores_done, 4 * it + j - 1)
                    nc.scalar.activation(queries[:, j % 2, :], bank[:, 4 + j % 2, :], ACT.Copy,
                                         scale=1 / (S_W * S_ACT)).then_inc(columns_out, 1)
                    if j:
                        take_scores(4 * it + j - 1, j - 1)
                take_scores(4 * it + 3, 3)

            retrieve(0)
            with act.Fori(1, N_Q // 4) as it:
                retrieve(it)
            for n in range(T_G, T_U):
                split_hi(Tile(n + SPLIT_AHEAD))
            for b in range(8):
                if b < 6:
                    act.wait_ge(gate_prod, b // 2 + 1)
                else:
                    act.wait_ge(tile_used, T_U)
                nc.scalar.activation(ple_gate[:, b, :], bank[:, b, :], ACT.Copy,
                                     scale=1 / (S_W * S_ACT)).then_inc(gate_lin, 1)

            def gelu(t, slot, group):
                act.wait_ge(tile_used, t.n + 1)
                at_least(act, gelu_stored[slot], 16 * group)
                nc.scalar.activation(gelu_out[:, slot, :], bank[:, 4 + slot % 2, 0:TD], ACT.Gelu,
                                     scale=1 / (S_W * S_ACT)).then_inc(columns_out, 1)

            for j in range(4):
                split_hi(Tile(T_U + j + SPLIT_AHEAD))
                gelu(Tile(T_U + j), j, 0)
            with act.Fori(1, U_TOPK // 4) as it:
                for j in range(4):
                    t = Tile(T_U + j, 4, it)
                    split_hi(t.plus(SPLIT_AHEAD))
                    gelu(t, j, it)
            for j in range(U_SOFTMAX):
                t = Tile(T_U + U_TOPK + j)
                split_hi(t.plus(SPLIT_AHEAD))
                if j == 0:
                    act.wait_ge(gate_shift, 1)
                    nc.scalar.activation(picked[:, 2], picked[:, 2], ACT.Exp).then_inc(gate_exp, 1)
                if j in (1, 2):
                    for tt in (2 * j - 2, 2 * j - 1):
                        act.wait_ge(gate_biased, tt + 1)
                        nc.scalar.activation(ple_gate[:, 2 * tt:2 * tt + 2, :], ple_gate[:, 2 * tt:2 * tt + 2, :],
                                             ACT.Sigmoid).then_inc(gate_sig, 1)
                gelu(t, j % 4, (U_TOPK + j) // 4)
                if j == U_SOFTMAX - 3:
                    for w in range(2):
                        act.wait_ge(rows_turned, w + 1)
                        nc.scalar.activation(rows[:, w, :], bank[:, w, 0:TD], ACT.Copy).then_inc(rows_idx, 1)

            def take_gates(q, b, s, chunk_round):
                for four in range(4):
                    act.wait_ge(gates_prod, 4 * q + four + 1)
                    if b == 0 and four == 0:
                        at_least(act, gates_stored[s], 16 * chunk_round)
                    first = BATCH * b + 4 * four
                    nc.scalar.activation(gate_chunk[:, s, :, first:first + 4].rearrange("p n t -> p t n"),
                                         bank[:, four, :].rearrange("p (t n) -> p t n", t=4),
                                         ACT.Copy).then_inc(gates_out, 1)

            def build_gates(it):
                for s in range(2):
                    for j in range(4):
                        c = U_TOPK + U_SOFTMAX + 4 * s + j
                        t = Tile(T_U + c, 8, it)
                        split_hi(t.plus(SPLIT_AHEAD))
                        gelu(t, j, c // 4 + 2 * it)
                        if j % 2:
                            take_gates(4 * it + 2 * s + j // 2, j // 2, s, it)

            build_gates(0)
            with act.Fori(1, U_GATES // 8) as it:
                build_gates(it)
            e0 = U_TOPK + U_SOFTMAX + U_GATES
            with act.Fori(0, U_LAST // 4 - 1) as it:
                for j in range(4):
                    t = Tile(T_U + e0 + j, 4, it)
                    split_hi(t.plus(SPLIT_AHEAD))
                    gelu(t, j, e0 // 4 + it)

            def weight_high(v, slot):
                act.wait_ge(weight_done, v + 1)
                at_least(act, tile_used, T_V + v - RING + 1)
                nc.scalar.activation(weight_cut[:, slot, 0, :], weight[:, slot, :], ACT.Copy).then_inc(weight_hi, 1)

            for j in range(4):
                t = Tile(T_V - 4 + j)
                split_hi(t.plus(SPLIT_AHEAD), S_W if t.n + SPLIT_AHEAD < T_V else S_V)
                gelu(t, j, N_U // 4 - 1)
                if j == 0:
                    act.wait_ge(dots_done, 1)
                    nc.scalar.activation(dots[:], dots[:], ACT.Gelu).then_inc(dots_gelu, 1)
            weight_high(0, 0)
            weight_high(1, 1)

            def experts(pair):
                fixed = isinstance(pair, int)
                for v in range(8):
                    t = Tile(T_V + 8 * pair + v) if fixed else Tile(T_V + v, 8, pair)
                    if not fixed or t.n + SPLIT_AHEAD < T_ALL:
                        split_hi(t.plus(SPLIT_AHEAD), S_V)
                        weight_high(8 * pair + v + SPLIT_AHEAD, (v + SPLIT_AHEAD) % RING)

            with act.Fori(0, N_V // 8 - 1) as pair:
                experts(pair)
            experts(N_V // 8 - 1)
            roots(2)

        @block.vector
        def _(dve):
            own = Tally(dve, dve_own)

            def split_lo(t, scale=S_W):
                dve.wait_ge(hi_cut, t.n + 1)
                at_least(dve, tile_used, t.n - RING + 1)
                nc.vector.scalar_tensor_tensor(out=cut[:, t.slot, 1, :], in0=raw[:, t.slot, :], scalar=scale,
                                               in1=cut[:, t.slot, 0, :], op0=ALU.mult,
                                               op1=ALU.subtract).then_inc(lo_cut, 1)

            def turn_lo(stage):
                for i in range(2 * TT):
                    t, kh = i // 2, i % 2
                    dve.wait_ge(turned_hi, KD * stage + i + 1)
                    nc.vector.scalar_tensor_tensor(
                        out=hT[:, 1, 4 * kh:4 * kh + 4, t * P:(t + 1) * P],
                        in0=bank[:, i % 4, :].rearrange("p (k t) -> p k t", k=4), scalar=S_ACT,
                        in1=hT[:, 0, 4 * kh:4 * kh + 4, t * P:(t + 1) * P], op0=ALU.mult,
                        op1=ALU.subtract).then_inc(turned_lo, 1)

            def layer_norm(stage, t, done):
                own.link(nc.vector.tensor_scalar(hn[:, t, :], hn[:, t, :], moments[:, t, 0:1], rstd[:, t:t + 1],
                                                 ALU.subtract, ALU.mult))
                own.link(nc.vector.tensor_tensor(hn[:, t, :], hn[:, t, :], norm_rows[:, 0, :], ALU.mult))
                nc.vector.tensor_tensor(hn[:, t, :], hn[:, t, :], norm_rows[:, 1, :],
                                        ALU.add).then_inc(done, 1)

            def row_stats(t):
                for h in range(2):
                    own.mark(nc.vector.bn_stats(stats[:, t, 6 * h:6 * h + 6], hn[:, t, h * HALF:(h + 1) * HALF]))

            def row_moments(stage, eps):
                own.settle()
                for t in range(TT):
                    own.mark(nc.vector.bn_aggr(moments[:, t, :], stats[:, t, :]))
                own.settle()
                nc.vector.tensor_scalar(variance[:], moments[:, :, 1], eps, None, ALU.add).then_inc(stats_done, 1)
                dve.wait_ge(rstd_done, stage + 1)
                own.link(nc.vector.reciprocal(rstd[:], std[:]))
                own.link(nc.vector.tensor_tensor(newton[:], rstd[:], rstd[:], ALU.mult))
                own.link(nc.vector.tensor_tensor(newton[:], newton[:], variance[:], ALU.mult))
                own.link(nc.vector.tensor_scalar(newton[:], newton[:], -0.5, 1.5, ALU.mult, ALU.add))
                own.link(nc.vector.tensor_tensor(rstd[:], rstd[:], newton[:], ALU.mult))

            def mask_and_max(m):
                dve.wait_ge(s_done, m + 1)
                at_least(dve, probs_turned, m - 1)
                buf = probs[:, m % 2]
                nc.vector.scalar_tensor_tensor(
                    out=buf, in0=bank[:, m % 2, :].rearrange("p (t k) -> p t k", t=TT), scalar=HD ** -0.5,
                    in1=alibi_sb[:, m:m + 1, :].to_broadcast([P, TT, P]), op0=ALU.mult,
                    op1=ALU.add).then_inc(s_out, 1)
                dve.wait_ge(s_out, m + 1)
                own.link(nc.vector.memset(buf[0:CHUNK, 0, 0:CHUNK], NEG))
                own.link(nc.vector.tensor_reduce(row_max[:, m % 2, :], buf, AX.X, ALU.max))
                nc.vector.tensor_scalar(neg_max[:, m % 2, :], row_max[:, m % 2, :], sink[:, m:m + 1], -1.0,
                                        ALU.max, ALU.mult).then_inc(max_done, 1)

            def normalise(m):
                dve.wait_ge(exp_done, m + 1)
                own.link(nc.vector.tensor_tensor(denom[:, m % 2, :], row_sum[:, m % 2, :], sink_exp[:, m % 2, :],
                                                 ALU.add))
                own.link(nc.vector.reciprocal(inv_den[:, m % 2, :], denom[:, m % 2, :]))
                nc.vector.tensor_tensor(probs[:, m % 2], probs[:, m % 2],
                                        inv_den[:, m % 2, :].unsqueeze(2).to_broadcast([P, TT, P]),
                                        ALU.mult).then_inc(probs_done, 1)

            def take_o(j):
                dve.wait_ge(o_hi, j + 1)
                nc.vector.scalar_tensor_tensor(out=mixT[:, 1, j, :], in0=bank[:, 6 + j % 2, :], scalar=S_ACT,
                                               in1=mixT[:, 0, j, :], op0=ALU.mult,
                                               op1=ALU.subtract).then_inc(o_lo, 1)

            def take_y(g):
                dve.wait_ge(y_hi, g + 1)
                nc.vector.scalar_tensor_tensor(out=mixT[:, 1, PAIRS + g, :], in0=bank[:, 2 + g % 2, :],
                                               scalar=pool_scale_s[:, g:g + 1], in1=mixT[:, 0, PAIRS + g, :],
                                               op0=ALU.mult, op1=ALU.subtract).then_inc(y_lo, 1)

            nc.vector.memset(kT[:, 0:CHUNK], 0.0).then_inc(pads_zero, 1)
            nc.vector.memset(vT[:, 0:CHUNK], 0.0).then_inc(pads_zero, 1)
            nc.vector.memset(pool_u[:, :, 0:PAD], 0.0).then_inc(pads_zero, 1)
            dve.wait_ge(pads_zero, 3)
            for t in range(TT):
                dve.wait_ge(x_in[t], 16)
                row_stats(t)
            row_moments(0, EPS)
            dve.wait_ge(norms_in, 16)
            for t in range(TT):
                layer_norm(0, t, norm_done)
            dve.wait_ge(consts_in, 16 * 7)
            nc.vector.tensor_scalar(pool_scale_s[:], pool_scale, S_ACT, None, ALU.mult).then_inc(scale_done, 1)
            dve.wait_ge(scale_done, 1)
            split_lo(Tile(0))
            split_lo(Tile(1))
            turn_lo(0)
            split_lo(Tile(2))
            split_lo(Tile(3))
            split_lo(Tile(4))
            mask_and_max(0)
            split_lo(Tile(5))
            mask_and_max(1)
            normalise(0)
            split_lo(Tile(6))
            mask_and_max(2)
            normalise(1)
            split_lo(Tile(7))
            mask_and_max(3)
            normalise(2)
            split_lo(Tile(8))
            mask_and_max(4)
            normalise(3)
            take_o(0)
            split_lo(Tile(9))
            take_y(0)
            mask_and_max(5)
            normalise(4)
            split_lo(Tile(10))
            mask_and_max(6)
            normalise(5)
            take_o(1)
            split_lo(Tile(11))
            take_y(1)
            mask_and_max(7)
            normalise(6)
            split_lo(Tile(12))
            take_y(2)
            normalise(7)
            take_o(2)
            split_lo(Tile(13))
            take_o(3)
            take_y(3)
            for n in range(T_O + 4, T_Q + SPLIT_AHEAD):
                split_lo(Tile(n))
            for t in range(TT):
                if t < TT - 1:
                    dve.wait_ge(mix_done, t + 1)
                else:
                    dve.wait_ge(tile_used, T_Q)
                for h in range(2):
                    rows_b = hn[:, t, h * HALF:(h + 1) * HALF]
                    nc.vector.scalar_tensor_tensor(out=rows_b, in0=bank[:, 2 * t + h, :],
                                                   scalar=1 / (S_W * S_ACT * ALPHA), in1=rows_b, op0=ALU.mult,
                                                   op1=ALU.add).then_inc(resid_done, 1)
                dve.wait_ge(resid_done, 2 * t + 2)
                row_stats(t)
            row_moments(1, EPS / ALPHA ** 2)
            dve.wait_ge(norms_in, 32)
            for t in range(TT):
                layer_norm(1, t, norm_done)
            turn_lo(1)
            def top16(values, index, source, spare):
                def settle():
                    own.settle()
                    own.mark(nc.vector.memset(word[:], 0.0))

                settle()
                for t in range(TT):
                    own.mark(nc.vector.max(values[:, t, 0:8], source[:, t, :]))
                settle()
                for t in range(TT):
                    own.mark(nc.vector.max_index(index[:, t, 0:8], values[:, t, 0:8], source[:, t, :]))
                for t in range(TT):
                    own.mark(nc.vector.match_replace(spare[:, t, :], values[:, t, 0:8], source[:, t, :], LOWEST))
                settle()
                for t in range(TT):
                    own.mark(nc.vector.max(values[:, t, 8:16], spare[:, t, :]))
                settle()
                for t in range(TT):
                    own.mark(nc.vector.max_index(index[:, t, 8:16], values[:, t, 8:16], spare[:, t, :]))

            def add_sides():
                own.settle()
                own.mark(nc.vector.tensor_tensor(
                    sums.rearrange("p t (a b) -> p t a b", a=K),
                    top_v[:, 0].unsqueeze(3).to_broadcast([P, TT, K, K]),
                    top_v[:, 1].unsqueeze(2).to_broadcast([P, TT, K, K]), ALU.add))
                own.mark(nc.vector.tensor_copy(top_f, top_i))
                own.settle()

            def pick(head):
                own.settle()
                own.mark(nc.vector.tensor_single_scalar(half_i[:, 0], sum_i, 4, ALU.logical_shift_right))
                own.mark(nc.vector.tensor_single_scalar(half_i[:, 1], sum_i, K - 1, ALU.bitwise_and))
                own.settle()
                own.link(nc.vector.tensor_copy(half_f, half_i))
                for p in range(2):
                    hit3 = hit.rearrange("p (t k) m -> p t k m", t=TT)
                    own.link(nc.vector.tensor_tensor(
                        hit, iota_k_sb[:].unsqueeze(1).to_broadcast([P, TT * K, K]),
                        half_f[:, p].rearrange("p t k -> p (t k)").unsqueeze(2).to_broadcast([P, TT * K, K]),
                        ALU.is_equal))
                    own.link(nc.vector.tensor_tensor(
                        hit3, hit3, top_f[:, p].unsqueeze(2).to_broadcast([P, TT, K, K]), ALU.mult))
                    own.link(nc.vector.tensor_reduce(
                        picked[:, p, :, bass.ds(K * head, K)], hit3, AX.X, ALU.add))
                own.mark(nc.vector.tensor_copy(picked[:, 2, :, bass.ds(K * head, K)], sum_v))
                own.settle()

            def top_k(head, tile, every=1):
                start = own.count

                def split(j):
                    for d in range(every * j, every * j + every):
                        split_lo(tile.plus(SPLIT_AHEAD + d))

                split(0)
                own.link(nc.vector.tensor_copy(side, scores[:, bass.ds(2 * head, 2), :]))
                for p in range(2):
                    if p:
                        split(1)
                    top16(top_v[:, p], top_i[:, p], side[:, p].rearrange("p (t n) -> p t n", t=TT), replaced)
                    own.settle()
                add_sides()
                split(2)
                top16(sum_v, sum_i, sums, sums_rep)
                split(3)
                pick(head)
                assert own.count - start == STEPS, own.count - start

            STEPS, GATES_OWN, LAST_OWN = 85, 25, 17
            for j in range(4):
                split_lo(Tile(T_Q + j + SPLIT_AHEAD))
            before = own.count
            with dve.Fori(1, N_Q // 4) as it:
                own.turns = STEPS * (it - 1)
                own.count = before
                dve.wait_ge(scores_out, 2 * it)
                top_k(it - 1, Tile(T_Q, 4, it))
            own.turns, own.count = 0, before + STEPS * Q_HEADS
            for g in range(G_HEADS):
                dve.wait_ge(scores_out, 2 * (Q_HEADS + g) + 2)
                top_k(Q_HEADS + g, Tile(T_G + 4 * g))
            before = own.count
            with dve.Fori(0, U_HEADS) as it:
                own.turns = STEPS * it
                own.count = before
                top_k(it + Q_HEADS + G_HEADS, Tile(T_U, 8, it), 2)
            own.turns, own.count = 0, before + STEPS * U_HEADS
            t = Tile(T_U + U_TOPK)
            split_lo(t.plus(SPLIT_AHEAD))
            e_view = picked[:, 2].rearrange("p t (h k) -> p (t h) k", k=K)
            own.link(nc.vector.tensor_copy(e_sum, e_view[:, :, 0]))
            nc.vector.tensor_tensor(e_view, e_view, e_sum.unsqueeze(2).to_broadcast([P, TT * HEADS, K]),
                                    ALU.subtract).then_inc(gate_shift, 1)
            ia, ib = picked[:, 0, ND, :], picked[:, 1, ND, :]
            own.mark(nc.vector.scalar_tensor_tensor(out=expert_f[:, 0, :], in0=ia, scalar=float(NKEY), in1=ib,
                                                    op0=ALU.mult, op1=ALU.add))
            own.mark(nc.vector.tensor_scalar(expert_f[:, 1, :], ib, float(NKEY), float(T_V * NKEY), ALU.mult,
                                             ALU.add))
            own.settle()
            own.link(nc.vector.tensor_tensor(expert_f[:, 1, :], expert_f[:, 1, :], ia, ALU.add))
            nc.vector.tensor_copy(expert_id[:], expert_f[:]).then_inc(ids_done, 1)
            for tt in range(TT):
                dve.wait_ge(gate_lin, 2 * tt + 2)
                gate_t = ple_gate[:, 2 * tt:2 * tt + 2, :].rearrange("p a n -> p (a n)")
                nc.vector.tensor_tensor(gate_t, gate_t, gate_b_row[:], ALU.add).then_inc(gate_biased, 1)
                if tt == 1:
                    split_lo(t.plus(SPLIT_AHEAD + 1))
            dve.wait_ge(gate_exp, 1)
            own.link(nc.vector.tensor_reduce(e_sum, e_view, AX.X, ALU.add))
            own.link(nc.vector.reciprocal(e_inv, e_sum))
            nc.vector.tensor_tensor(e_view, e_view, e_inv.unsqueeze(2).to_broadcast([P, TT * HEADS, K]),
                                    ALU.mult).then_inc(gates_done, 1)
            split_lo(t.plus(SPLIT_AHEAD + 2))
            for tt in range(TT):
                dve.wait_ge(gate_sig, tt + 1)
                nc.vector.scalar_tensor_tensor(out=ple_gate[:, 2 * tt:2 * tt + 2, :],
                                               in0=ple_sb[:, 2 * tt:2 * tt + 2, :], scalar=1 / ALPHA,
                                               in1=ple_gate[:, 2 * tt:2 * tt + 2, :], op0=ALU.mult,
                                               op1=ALU.mult).then_inc(gated, 1)
                if tt == 1:
                    split_lo(t.plus(SPLIT_AHEAD + 3))
            split_lo(t.plus(SPLIT_AHEAD + 4))
            dve.wait_ge(gated, TT)
            for tt in range(ND):
                nc.vector.tensor_tensor(hn[:, tt, :], hn[:, tt, :],
                                        ple_gate[:, 2 * tt:2 * tt + 2, :].rearrange("p a n -> p (a n)"),
                                        ALU.add).then_inc(ple_added, 1)
                split_lo(t.plus(SPLIT_AHEAD + 5 + tt))
            dve.wait_ge(ple_added, ND)
            dve.wait_ge(rows_turned, 3)
            nc.vector.tensor_scalar(rows[:, 2, :], bank[:, 2, 0:TD], S_G, None, ALU.mult).then_inc(rows_hi, 1)
            dve.wait_ge(rows_hi, 1)
            nc.vector.scalar_tensor_tensor(out=rows[:, 3, :], in0=bank[:, 2, 0:TD], scalar=S_G, in1=rows[:, 2, :],
                                           op0=ALU.mult, op1=ALU.subtract).then_inc(rows_done, 1)
            dve.wait_ge(rows_done, 1)
            dve.wait_ge(rows_idx, 2)

            def dot(j, g_round):
                dve.wait_ge(rows_in[j % ROW_RING], 16 * (g_round + 1))
                own.settle()
                own.mark(nc.vector.memset(word[:], 0.0))
                slot = expert_rows[:, j % ROW_RING, :]
                nc.vector.tensor_tensor_reduce(slot, slot, hn[:, ND, :], 1.0, 0.0, ALU.mult, ALU.add,
                                               dots_now[:, j:j + 1]).then_inc(rows_used, 1)

            def keep_dots(first, count):
                dve.wait_ge(rows_used, first + count)
                own.link(nc.vector.tensor_copy(dots[:, bass.ds(first, count)], dots_now[:, 0:count]))

            def onehots(q, b, first):
                shape = [P, BATCH // OT, NKEY, OT]
                if not first:
                    dve.wait_ge(gates_prod, 4 * q - 4)
                own.link(nc.vector.tensor_copy(staged[:, b], rows[:, :, bass.ds(BATCH * q, BATCH)]))
                cols = [staged[:, b, w, :].rearrange("p (a t) -> p a t", t=OT).unsqueeze(2).to_broadcast(shape)
                        for w in range(4)]
                keys = iota_oh_sb[:].unsqueeze(1).to_broadcast(shape)
                own.mark(nc.vector.tensor_tensor(onehot[:, b], keys, cols[0], ALU.is_equal))
                own.mark(nc.vector.tensor_tensor(onehot[:, 2], keys, cols[1], ALU.is_equal))
                own.settle()
                own.mark(nc.vector.tensor_tensor(onehot_hi[:, b], onehot[:, 2], cols[2], ALU.mult))
                nc.vector.tensor_tensor(onehot_lo[:, b], onehot[:, 2], cols[3], ALU.mult).then_inc(onehot_done, 1)

            def build_gates(it, first):
                for s in range(2):
                    for j in range(4):
                        c = U_TOPK + U_SOFTMAX + 4 * s + j
                        split_lo(Tile(T_U + c + SPLIT_AHEAD, 8, it))
                        dot(4 * s + j, 2 * it + s)
                        if j % 2 == 0:
                            q = 4 * it + 2 * s + j // 2
                            if not (first and s == 0 and j == 0):
                                dve.wait_ge(onehot_done, q)
                            onehots(q, j // 2, first and s == 0)

            build_gates(0, True)
            keep_dots(0, 8)
            before = own.count

            def build_gates_loop(it):
                own.turns, own.count = GATES_OWN * (it - 1), before
                build_gates(it, False)
                keep_dots(8 * it, 8)
                assert own.count - before == GATES_OWN, own.count - before

            with dve.Fori(1, U_GATES // 8) as it:
                build_gates_loop(it)
            own.turns, own.count = 0, before + GATES_OWN * (U_GATES // 8 - 1)
            e0 = U_TOPK + U_SOFTMAX + U_GATES
            before = own.count
            with dve.Fori(0, (U_LAST - U_TAIL) // 8) as it:
                own.turns, own.count = LAST_OWN * it, before
                for j in range(8):
                    split_lo(Tile(T_U + e0 + j + SPLIT_AHEAD, 8, it))
                    for d in (2 * j, 2 * j + 1):
                        dot(d, DOTS_GATES // ROW_RING + 4 * it + d // ROW_RING)
                keep_dots(DOTS_GATES + 16 * it, 16)
                assert own.count - before == LAST_OWN, own.count - before
            own.turns, own.count = 0, before + LAST_OWN * ((U_LAST - U_TAIL) // 8)
            nc.vector.memset(word[:], 0.0).then_inc(dots_done, 1)
            for j in range(U_TAIL - 4):
                split_lo(Tile(T_V - U_TAIL + j + SPLIT_AHEAD))

            def make_weight(v, slot, parity, rounds):
                dve.wait_ge(pair_in[parity], 32 * (rounds + 1))
                at_least(dve, weight_lo, v - RING + 1)
                nc.vector.tensor_tensor(
                    weight[:, slot, :].rearrange("p (c t) -> p c t", t=TOK),
                    gelu_in[:, parity, slot, :].rearrange("p (c t) -> p c t", t=TOK),
                    gates_in[:, parity, :, slot, :], ALU.mult).then_inc(weight_done, 1)

            def weight_low(v, slot):
                dve.wait_ge(weight_hi, v + 1)
                nc.vector.tensor_tensor(weight_cut[:, slot, 1, :], weight[:, slot, :], weight_cut[:, slot, 0, :],
                                        ALU.subtract).then_inc(weight_lo, 1)

            for j in range(4):
                m = T_V - 4 + j + SPLIT_AHEAD
                split_lo(Tile(m), S_W if m < T_V else S_V)
            dve.wait_ge(dots_gelu, 1)
            own.link(nc.vector.scalar_tensor_tensor(out=sparse_w[:], in0=dots[:], scalar=1 / ALPHA,
                                                    in1=picked[:, 2, ND, :], op0=ALU.mult, op1=ALU.mult))
            for v in range(SPLIT_AHEAD + 1):
                make_weight(v, v, 0, 0)
            for v in range(SPLIT_AHEAD):
                weight_low(v, v)

            def experts(pair):
                fixed = isinstance(pair, int)
                dve.wait_ge(rows_used, HK + 8 * pair)
                own.link(nc.vector.tensor_copy(sparse_w_now[:], sparse_w[:, bass.ds(8 * pair, 8)]))
                for v in range(8):
                    dve.wait_ge(rows_in[v % ROW_RING], 16 * (HK // ROW_RING + 2 * pair + v // ROW_RING + 1))
                    dve.wait_ge(rows_used, HK + 8 * pair + v)
                    nc.vector.scalar_tensor_tensor(out=sparse_sum, in0=expert_rows[:, v % ROW_RING, :],
                                                   scalar=sparse_w_now[:, v:v + 1], in1=sparse_sum,
                                                   op0=ALU.mult, op1=ALU.add).then_inc(rows_used, 1)
                    t = Tile(T_V + 8 * pair + v) if fixed else Tile(T_V + v, 8, pair)
                    if not fixed or t.n + SPLIT_AHEAD + 1 < T_ALL:
                        w = v + SPLIT_AHEAD + 1
                        make_weight(8 * pair + w, w % RING, (w // 4) % 2, pair + w // 8)
                    if not fixed or t.n + SPLIT_AHEAD < T_ALL:
                        weight_low(8 * pair + v + SPLIT_AHEAD, (v + SPLIT_AHEAD) % RING)
                        split_lo(t.plus(SPLIT_AHEAD), S_V)

            experts(0)
            before = own.count
            with dve.Fori(1, N_V // 8 - 1) as pair:
                own.turns, own.count = pair - 1, before
                experts(pair)
            own.turns, own.count = 0, before + N_V // 8 - 2
            experts(N_V // 8 - 1)
            dve.wait_ge(rows_used, 2 * HK)
            nc.vector.tensor_tensor(hn[:, ND, :], hn[:, ND, :], sparse_sum, ALU.add).then_inc(final_sum, 2)
            dve.wait_ge(final_sum, 2)
            row_stats(ND)
            for t in range(ND):
                if t < ND - 1:
                    dve.wait_ge(experts_done, t + 1)
                else:
                    dve.wait_ge(tile_used, T_ALL)
                for h in range(2):
                    rows_b = hn[:, t, h * HALF:(h + 1) * HALF]
                    nc.vector.scalar_tensor_tensor(out=rows_b, in0=bank[:, 2 * t + h, :],
                                                   scalar=1 / (S_G * S_V * ALPHA), in1=rows_b, op0=ALU.mult,
                                                   op1=ALU.add).then_inc(final_sum, 1)
                dve.wait_ge(final_sum, 2 * t + 4)
                row_stats(t)
            row_moments(2, EPS / ALPHA ** 2)
            dve.wait_ge(norms_in, 48)
            for t in FINAL_ORDER:
                layer_norm(2, t, final_done)


def _tables():
    q, k = np.arange(CHUNK)[:, None], np.arange(P)[None, :] - CHUNK
    dist = np.abs(q - k).astype(np.float32)
    heads = [m // 2 + 4 * (m % 2) for m in range(8)]
    slopes = np.array([2.0 ** (-(h + 1)) for h in heads], np.float32)
    alibi = np.tile(-slopes[None, :, None] * dist[:, None, :], (2, 1, 1)).astype(np.float32)
    counts = np.stack([1.0 / np.minimum(np.arange(1, PAD + 1), w) for w in WINDOWS]).astype(np.float32)
    counts = np.broadcast_to(counts.reshape(1, -1), (P, GROUPS * PAD))
    onehot = np.broadcast_to(np.arange(NKEY, dtype=np.float16)[None, :, None], (P, NKEY, OT))
    keys = np.broadcast_to(np.arange(K, dtype=np.float32)[None, :], (P, K))
    return alibi, counts, np.eye(P, dtype=np.float32), onehot, keys


def kernel(x, p, ln_in_g, ln_in_b, w_in, pool_w, pool_scale, attn_sinks, w_o, ln1_g, ln1_b, peer_wq,
           peer_subkeys, peer_u, peer_v, ple_w, ple_gate_w, ple_gate_b, ln2_g, ln2_b):
    import concourse.bacc as bacc
    from concourse.bass_utils import run_bass_kernel_spmd

    alibi, counts, ident, onehot, keys = _tables()
    a = np.asarray
    c = lambda v: np.ascontiguousarray(v, dtype=np.float32)
    w_in, w_o = a(w_in)[0], a(w_o)[0]
    pool_n = GROUPS * P
    pair_cols = [np.r_[j * HD:(j + 1) * HD, (j + 4) * HD:(j + 5) * HD] for j in range(PAIRS)]
    named = {"k": 2 * pool_n + np.arange(P), "v": 2 * pool_n + P + np.arange(P)}
    named.update({f"q{j}": pool_n + pc for j, pc in enumerate(pair_cols)})
    named.update({f"u{g}": g * P + np.arange(P) for g in range(GROUPS)})
    cols = [named[name] for name in COLUMNS]
    w_in = w_in[:, np.concatenate(cols)]
    rows = [pool_n + pc for pc in pair_cols] + [np.arange(pool_n)]
    w_o = w_o[np.concatenate(rows)]
    by_columns = lambda w, n: w.reshape(KD, P, n, P).transpose(2, 1, 0, 3).reshape(n, P, D)
    by_rows = lambda w: w.reshape(KD, P, D)
    u = a(peer_u)[0].reshape(P, N_U, KD, P).transpose(1, 3, 2, 0).reshape(N_U, P, D)
    v = a(peer_v)[0].reshape(P, N_V, D).transpose(1, 0, 2)
    tiles = np.concatenate([by_columns(w_in, N_IN), by_rows(w_o), by_columns(a(peer_wq)[0], N_Q),
                            by_rows(a(ple_gate_w)[0]), u, v])
    order = [m // 2 + 4 * (m % 2) for m in range(8)]
    small = np.concatenate([
        np.broadcast_to(a(attn_sinks)[0][order][None, :], (P, 8)),
        a(pool_scale)[0].reshape(GROUPS, P).T, counts], axis=1)
    arrays = {
        "tiles": c(tiles),
        "u_rows": c(a(peer_u)[0]),
        "x": c(a(x).reshape(T, D)),
        "ple_in": c(a(p).reshape(T, 2, P).transpose(2, 1, 0)),
        "ple_w": c(a(ple_w)[0].reshape(2, P, D).transpose(1, 0, 2)),
        "norms": c(np.stack([a(ln_in_g), a(ln_in_b), a(ln1_g)[0], a(ln1_b)[0], a(ln2_g)[0],
                             a(ln2_b)[0]]).reshape(3, 2, D)),
        "gate_b": c(a(ple_gate_b)[0]),
        "small": c(small),
        "pool_w": c(a(pool_w)[0].transpose(1, 0, 2)),
        "subkeys": c(a(peer_subkeys)[0].reshape(2 * HEADS, NKEY, P).transpose(2, 0, 1)),
        "alibi": c(alibi),
        "ident": c(ident),
        "iota_oh": np.ascontiguousarray(onehot),
        "iota_k": c(keys),
    }
    nc = bacc.Bacc("TRN2", target_bir_lowering=False, num_devices=1)
    args = [nc.dram_tensor(f"{n}_dram", v_.shape, mybir.dt.from_np(v_.dtype), kind="ExternalInput").ap()
            for n, v_ in arrays.items()]
    out = nc.dram_tensor("out_dram", [T, D], F32, kind="ExternalOutput").ap()
    layer(nc, *args, out)
    r = run_bass_kernel_spmd(nc, [{f"{n}_dram": v_ for n, v_ in arrays.items()}], core_ids=[0])
    return r.results[0]["out_dram"].reshape(1, T, D)
```

```python
from contextlib import ExitStack

import numpy as np

import concourse.bass as bass
from concourse import mybir

F32 = mybir.dt.float32
F16 = mybir.dt.float16
U32 = mybir.dt.uint32
ALU = mybir.AluOpType
ACT = mybir.ActivationFunctionType
AX = mybir.AxisListType

P = 128
D = 1024
T = 512
TT = T // P
ND = TT - 1
TD = ND * P
KD = D // P
HALF = 512
CHUNK = 64
HD = 64
NCH = T // CHUNK
PAIRS = 4
GROUPS = 4
WINDOWS = (2, 4, 8, 16)
PAD = 16
HEADS = 8
K = 16
NKEY = 128
N_IN, N_O, N_Q, N_G, N_U = 10, 8, 16, 8, 128
COLUMNS = ("k", "v", "q0", "q1", "u0", "q2", "u1", "q3", "u2", "u3")
IN_SBUF = {name: i + 1 for i, name in enumerate(COLUMNS)}
T_IN = 0
T_O = T_IN + N_IN
T_Q = T_O + N_O
T_G = T_Q + N_Q
T_U = T_G + N_G
AREA = 21500
RING = 4
SPLIT_AHEAD = 2
LOAD_AHEAD = 6
S_ACT = 16.0
S_W = 256.0
S_V = 16.0
S_G = 64.0
ALPHA = 2.0 ** 0.25
EPS = 1e-5
NEG = -1e30
LOWEST = -3.0e38

U_TOPK = 24
U_SOFTMAX = 8
U_GATES = TD // 8
POOL_FIRST, POOL_TILES = T_Q + SPLIT_AHEAD, N_Q + N_G + U_TOPK + U_SOFTMAX
U_EARLY = U_TOPK + U_SOFTMAX + U_GATES
N_BOTH = N_U - U_EARLY
T_BOTH = T_U + U_EARLY
T_LATE = T_BOTH + 2 * N_BOTH
N_LATE = U_EARLY
T_ALL = T_LATE + N_LATE
KEPT = 8
STORED = (N_LATE - KEPT) // 4
EIGHTS = N_BOTH // 8
TOK = 32
GCH = TD // TOK
HK = HEADS * K
ROW_RING = 4
EIGHT_DOTS = (20, 20, 20, 20)
EIGHT_SUMS = (24, 24)
assert U_GATES + sum(EIGHT_DOTS) == HK and sum(EIGHT_SUMS) + N_LATE == HK
assert len(EIGHT_DOTS) + len(EIGHT_SUMS) == EIGHTS and N_LATE % 8 == 0
BATCH = 16
OT = 8
VG = 4


FINAL_ORDER = (ND, *range(ND))
POOL_ADDS = ((0, 2), (0, 1, 2), (0, 1, 2))


def norm_order(stage):
    return FINAL_ORDER if stage == 2 else range(TT)


def turn_bank(stage, i):
    return i % 4 if stage else i


def norm_batch(stage, i):
    return 0 if stage == 0 else 1 + TT * (stage - 1) + i


class Tile:

    def __init__(self, c, k=0, it=0):
        self.c, self.k, self.it = c, k, it
        self.n = c + k * it if k else c
        self.slot = c % RING
        self.round = c // RING + (k // RING) * it if k else c // RING

    def plus(self, d):
        return Tile(self.c + d, self.k, self.it)

    @property
    def scale(self):
        is_v = self.c >= T_LATE - 2 or T_BOTH + 3 <= self.c and (self.c - T_BOTH) % 2 == 1
        return S_V if is_v else S_W


class Tally:

    def __init__(self, eng, sem):
        self.eng, self.sem, self.count, self.turns = eng, sem, 0, 0

    def mark(self, instruction):
        instruction.then_inc(self.sem, 1)
        self.count += 1

    def settle(self):
        self.eng.wait_ge(self.sem, self.turns + self.count)

    def link(self, instruction):
        self.mark(instruction)
        self.settle()


def at_least(eng, sem, value):
    if isinstance(value, int) and value <= 0:
        return
    eng.wait_ge(sem, value)


def layer(nc, tiles, u_rows, v_rows, x, ple_in, ple_w, norms, gate_b, small, pool_w, subkeys, alibi, ident, iota_oh, iota_k,
          out):
    gelu_dram = nc.dram_tensor("gelu_scratch", [STORED, P, VG, TD], F32, kind="Internal").ap()
    gates_dram = nc.dram_tensor("gates_scratch", [GCH, P, P, TOK], F32, kind="Internal").ap()

    with ExitStack() as ctx:
        def sb(name, shape, dt=F32):
            return ctx.enter_context(nc.sbuf_tensor(name, shape, dt))

        def sem(name):
            return ctx.enter_context(nc.semaphore(name))

        bank = ctx.enter_context(nc.psum_tensor("bank", [P, 8, HALF], F32))

        raw = sb("raw", [P, RING, D])
        cut = sb("cut", [P, RING, 2, D], F16)
        hn = sb("hn", [P, TT, D])
        hT = sb("hT", [P, 2, KD, T], F16)
        norm_rows = sb("norm_rows", [P, 2, D])
        gate_b_row = sb("gate_b_row", [P, D])
        stats = sb("stats", [P, TT, 12])
        moments = sb("moments", [P, TT, 2])
        word = sb("word", [P, 1])
        variance = sb("variance", [P, TT])
        std = sb("std", [P, TT])
        rstd = sb("rstd", [P, TT])
        newton = sb("newton", [P, TT])
        shift = sb("shift", [P, TT])
        pool_scale_s = sb("pool_scale_s", [P, GROUPS])
        small_sb = sb("small_sb", [P, 8 + GROUPS + GROUPS * PAD])
        sink = small_sb[:, 0:8]
        pool_scale = small_sb[:, 8:8 + GROUPS]
        inv_count = small_sb[:, 8 + GROUPS:].rearrange("p (g t) -> p g t", g=GROUPS)
        ident_sb = sb("ident_sb", [P, P])
        iota_oh_sb = sb("iota_oh_sb", [P, NKEY, OT], F16)
        iota_k_sb = sb("iota_k_sb", [P, K])
        area = sb("area", [P, AREA])
        taken = [0]

        def part(shape, dt=F32):
            size = int(np.prod(shape)) * (2 if dt == F16 else 4) // 4
            a = area[:, taken[0]:taken[0] + size]
            taken[0] += size
            assert taken[0] <= AREA, taken
            if dt != F32:
                a = a.bitcast(dt)
            names = "abcd"[:len(shape)]
            if len(shape) > 1:
                a = a.rearrange(f"p ({' '.join(names)}) -> p {' '.join(names)}",
                                **{c: s for c, s in zip(names, shape)})
            return a

        kT = part([CHUNK + T])
        vT = part([CHUNK + T])
        qT = part([PAIRS, T])
        pool_u = part([GROUPS, PAD + T])
        pool_a = part([PAD + T])
        pool_b = part([PAD + T])
        pool_d = part([GROUPS, T])
        pool_w_sb = part([GROUPS, P])
        alibi_sb = part([8, P])
        v_band = part([NCH, P])
        probs = part([2, TT, P])
        probs_T = part([2, T])
        row_max = part([2, TT])
        neg_max = part([2, TT])
        row_sum = part([2, TT])
        sink_exp = part([2, TT])
        denom = part([2, TT])
        inv_den = part([2, TT])
        mixT = part([2, KD, T], F16)
        taken[0] = 0
        scores = part([2 * HEADS, T])
        queries = part([2, T])
        subkeys_sb = part([2 * HEADS, NKEY])
        side = part([2, T])
        replaced = part([2 * TT, NKEY])
        sums = part([TT, K * K])
        sums_rep = part([TT, K * K])
        top_v = part([2, TT, K])
        top_i = part([2, TT, K], U32)
        sum_v = part([TT, K])
        sum_i = part([TT, K], U32)
        half_i = part([2, TT, K], U32)
        half_f = part([2, TT, K])
        top_f = part([2, TT, K])
        hit = part([2 * TT * K, K])
        picks_at = taken[0]
        picked = part([3, TT, HEADS * K])
        e_sum = part([TT * HEADS])
        e_inv = part([TT * HEADS])
        rows = part([4, TD], F16)
        staged = part([2, 4, BATCH], F16)
        gelu_out = sb("gelu_out", [P, VG, TD])
        ple_gate = sb("ple_gate", [P, 8, HALF])
        ple_in_sb = gelu_out[:, :, :].rearrange("p s t -> p (s t)")[:, 0:2 * T].rearrange("p (k t) -> p k t", k=2)
        ple_w_sb = ple_gate[:, 0:4, :].rearrange("p (k a) n -> p k (a n)", k=2)
        ple_sb = sb("ple_sb", [P, 8, HALF])
        onehot = ple_gate[:, :, :].rearrange("p a b -> p (a b)").bitcast(F16).rearrange(
            "p (s a n t) -> p s a n t", s=4, a=BATCH // OT, t=OT)
        sparse_sum = ple_gate[:, 2 * ND:, :].rearrange("p a n -> p (a n)")
        expert_rows = ple_sb[:, :, :].rearrange("p (s a) n -> p s (a n)", s=ROW_RING)
        pool_word = sb("pool_word", [P, 1])
        expert_f = sb("expert_f", [P, HK])
        expert_id = sb("expert_id", [P, HK], U32)
        ids_now = sb("ids_now", [P, 2, 8], U32)
        dots_now = sb("dots_now", [P, 24])
        dots = sb("dots", [P, HK])
        sparse_w = sb("sparse_w", [P, HK])
        sparse_w_now = sb("sparse_w_now", [P, 24])
        taken[0] = 0
        gate_chunk = part([2, P, TOK])
        onehot_hi = part([2, BATCH // OT, NKEY, OT], F16)
        onehot_lo = part([2, BATCH // OT, NKEY, OT], F16)
        gelu_kept = part([KEPT, TD])
        assert taken[0] <= picks_at
        taken[0] = 0
        gelu_in = part([2, VG, TD])
        gates_in = part([2, GCH, VG, TOK])
        weight = part([RING, TD])
        weight_cut = part([RING, 2, TD], F16)

        ident_in, consts_in, tables_in, ple_loaded, subkeys_in, norms_in = (sem(n) for n in (
            "ident_in", "consts_in", "tables_in", "ple_loaded", "subkeys_in", "norms_in"))
        x_in = [sem(f"x_in{t}") for t in range(TT)]
        tile_in = [sem(f"tile_in{s}") for s in range(RING)]
        hi_cut, lo_cut, tile_used = sem("hi_cut"), sem("lo_cut"), sem("tile_used")
        raw_scaled = sem("raw_scaled")
        columns_out = sem("columns_out")
        stats_done, rstd_done, norm_done = sem("stats_done"), sem("rstd_done"), sem("norm_done")
        shift_done, centred, rows_scaled = sem("shift_done"), sem("centred"), sem("rows_scaled")
        turned, turned_hi, turned_lo = sem("turned"), sem("turned_hi"), sem("turned_lo")
        pads_zero, v_turned, v_band_done = sem("pads_zero"), sem("v_turned"), sem("v_band_done")
        s_done, s_out, max_done, exp_done, probs_done = (sem(n) for n in (
            "s_done", "s_out", "max_done", "exp_done", "probs_done"))
        probs_turned, probs_T_done, pv_done, o_hi, o_lo = (sem(n) for n in (
            "probs_turned", "probs_T_done", "pv_done", "o_hi", "o_lo"))
        pool_d_done, pool_prod, pool_own, scale_done, y_hi, y_lo = (sem(n) for n in (
            "pool_d_done", "pool_prod", "pool_own", "scale_done", "y_hi", "y_lo"))
        mix_done, resid_done = sem("mix_done"), sem("resid_done")
        scores_done, scores_out = sem("scores_done"), sem("scores_out")
        ple_prod, ple_out, gate_prod, gate_lin, gate_biased, gate_sig, gated, ple_added = (sem(n) for n in (
            "ple_prod", "ple_out", "gate_prod", "gate_lin", "gate_biased", "gate_sig", "gated", "ple_added"))
        rows_in = [sem(f"rows_in{s}") for s in range(ROW_RING)]
        ids_done, rows_used, dots_done, dots_gelu = (sem(n) for n in (
            "ids_done", "rows_used", "dots_done", "dots_gelu"))
        picks_done, gate_shift, gate_exp, gates_done = (sem(n) for n in (
            "picks_done", "gate_shift", "gate_exp", "gates_done"))
        rows_turned, rows_idx, rows_hi, rows_done = (sem(n) for n in (
            "rows_turned", "rows_idx", "rows_hi", "rows_done"))
        onehot_done, gates_prod, gates_out = sem("onehot_done"), sem("gates_prod"), sem("gates_out")
        gelu_stored = [sem(f"gelu_stored{s}") for s in range(VG)]
        gates_stored = [sem(f"gates_stored{s}") for s in range(2)]
        gates_loaded = [sem(f"gates_loaded{s}") for s in range(2)]
        gelu_loaded = [sem(f"gelu_loaded{s}") for s in range(2)]
        weight_done, weight_hi, weight_lo = sem("weight_done"), sem("weight_hi"), sem("weight_lo")
        experts_done, final_sum, final_done, stored = (sem(n) for n in (
            "experts_done", "final_sum", "final_done", "stored"))
        dve_own = sem("dve_own")

        block = ctx.enter_context(nc.Block())

        @block.sync
        def _(sp):
            def load(t):
                at_least(sp, lo_cut, t.plus(1 - RING).n)
                src = tiles[t.n] if isinstance(t.n, int) else tiles[bass.ds(t.n, 1)].rearrange("a p n -> (a p) n")
                sp.dma_start(raw[:, t.slot, :], src).then_inc(tile_in[t.slot], 16)

            def store_gelu(group, slot, expert):
                sp.wait_ge(columns_out, N_IN + N_Q + 1 + expert)
                dst = gelu_dram[group, :, slot, :] if isinstance(group, int) else \
                    gelu_dram[bass.ds(group, 1), :, slot, :].rearrange("a p t -> (a p) t")
                sp.dma_start(dst, gelu_out[:, slot, :]).then_inc(gelu_stored[slot], 16)

            def load_gates(group, first, parity):
                at_least(sp, weight_done, VG * (group - 1))
                sp.dma_start(gates_in[:, parity],
                             gates_dram[:, :, bass.ds(first, VG), :].rearrange("c p e t -> p c e t")
                             ).then_inc(gates_loaded[parity], 16)

            def load_gelu(group, parity):
                src = gelu_dram[group] if isinstance(group, int) else \
                    gelu_dram[bass.ds(group, 1)].rearrange("a p e t -> (a p) e t")
                sp.dma_start(gelu_in[:, parity], src).then_inc(gelu_loaded[parity], 16)

            def load_norms(stage):
                at_least(sp, norm_done, TT * stage)
                sp.dma_start(norm_rows[:], norms[stage].partition_broadcast(P)).then_inc(norms_in, 16)

            for t in range(TT):
                sp.dma_start(hn[:, t, :], x[t * P:(t + 1) * P, :]).then_inc(x_in[t], 16)
            load_norms(0)
            sp.dma_start(ident_sb[:], ident).then_inc(ident_in, 16)
            load(Tile(0))
            load(Tile(1))
            load(Tile(2))
            sp.dma_start(alibi_sb, alibi).then_inc(consts_in, 16)
            sp.dma_start(small_sb[:], small).then_inc(consts_in, 16)
            sp.dma_start(pool_w_sb, pool_w).then_inc(consts_in, 16)
            load(Tile(3))
            sp.dma_start(ple_in_sb, ple_in).then_inc(ple_loaded, 16)
            sp.dma_start(ple_w_sb, ple_w).then_inc(ple_loaded, 16)
            sp.dma_start(iota_oh_sb[:], iota_oh).then_inc(tables_in, 16)
            sp.dma_start(iota_k_sb[:], iota_k).then_inc(tables_in, 16)
            sp.dma_start(gate_b_row[:], gate_b.partition_broadcast(P)).then_inc(tables_in, 16)
            load_norms(1)
            for n in range(4, T_Q + RING):
                load(Tile(n))
            sp.wait_ge(resid_done, 8)
            sp.dma_start(subkeys_sb, subkeys).then_inc(subkeys_in, 16)
            for n in range(T_Q + RING, T_Q + LOAD_AHEAD):
                load(Tile(n))
            load_norms(2)
            for n in range(T_Q, T_U):
                load(Tile(n + LOAD_AHEAD))
            with sp.Fori(0, U_TOPK // 4) as it:
                for j in range(4):
                    load(Tile(T_U + j + LOAD_AHEAD, 4, it))
                    store_gelu(it, j, 4 * it + j)
            for c in range(U_TOPK, U_TOPK + U_SOFTMAX):
                load(Tile(T_U + c + LOAD_AHEAD))
                store_gelu(c // 4, c % 4, c)
            e0 = U_TOPK + U_SOFTMAX

            def build_gates(it):
                for s in range(2):
                    for j in range(4):
                        c = e0 + 4 * s + j
                        load(Tile(T_U + c + LOAD_AHEAD, 8, it))
                        if not isinstance(it, int):
                            store_gelu(e0 // 4 + s + 2 * it, j, c + 8 * it)
                    sp.wait_ge(gates_out, 16 * it + 8 * s + 8)
                    sp.dma_start(gates_dram[bass.ds(2 * it + s, 1)].rearrange("a p n t -> (a p) n t"),
                                 gate_chunk[:, s]).then_inc(gates_stored[s], 16)

            with sp.Fori(0, U_GATES // 8 - 1) as it:
                build_gates(it)
            build_gates(U_GATES // 8 - 1)
            load(Tile(T_BOTH + LOAD_AHEAD))
            for s in range(2):
                sp.wait_ge(gates_stored[s], 16 * (GCH // 2))
            load_gates(0, U_EARLY, 0)
            load_gates(1, U_EARLY + VG, 1)
            load(Tile(T_BOTH + 1 + LOAD_AHEAD))

            def both(e):
                for p in range(8):
                    t = Tile(T_BOTH + 2 + 16 * e + 2 * p) if isinstance(e, int) else Tile(T_BOTH + 2 + 2 * p, 16, e)
                    if t.c < T_LATE - 2:
                        load(t.plus(LOAD_AHEAD))
                        load(t.plus(1 + LOAD_AHEAD))
                    if p % 4 == 2:
                        s = p // 4
                        if isinstance(e, int) and e == EIGHTS - 1:
                            load_gates(2 * e + 2 + s, VG * s, s)
                        else:
                            load_gates(2 * e + 2 + s, U_EARLY + VG * (2 * e + 2 + s), s)

            for j in range(VG):
                sp.wait_ge(gelu_stored[j], 16 * STORED)
            with sp.Fori(0, EIGHTS - 2) as e:
                both(e)
            load_gelu(0, 0)
            load_gelu(1, 1)
            both(EIGHTS - 2)
            both(EIGHTS - 1)
            for n in range(T_LATE - 2, T_LATE):
                load(Tile(n + LOAD_AHEAD))

            def late(e):
                fixed = isinstance(e, int)
                for j in range(8):
                    t = Tile(T_LATE + 8 * e + j) if fixed else Tile(T_LATE + j, 8, e)
                    if not fixed or t.n + LOAD_AHEAD < T_ALL:
                        load(t.plus(LOAD_AHEAD))
                    if j % 4 == 1 and not fixed:
                        s = j // 4
                        load_gates(2 * EIGHTS + 2 * e + s + 2, VG * (2 * e + s + 2), s)
                        load_gelu(2 * e + s + 2, s)
                    elif j % 4 == 1 and 2 * e + j // 4 + 2 < N_LATE // VG:
                        s = j // 4
                        load_gates(2 * EIGHTS + 2 * e + s + 2, VG * (2 * e + s + 2), s)

            with sp.Fori(0, N_LATE // 8 - 2) as e:
                late(e)
            late(N_LATE // 8 - 2)
            late(N_LATE // 8 - 1)
            for i, t in enumerate(FINAL_ORDER):
                sp.wait_ge(final_done, i + 1)
                sp.dma_start(out[t * P:(t + 1) * P, :], hn[:, t, :]).then_inc(stored, 16)
            sp.wait_ge(stored, 16 * TT)

        @block.gpsimd
        def _(pool):
            own = Tally(pool, pool_own)

            def add_b(stage):
                for i in POOL_ADDS[stage]:
                    pool.wait_ge(rows_scaled, TT * stage + i + 1)
                    done, before = (final_done, 0) if stage == 2 else (norm_done, TT * stage)
                    at_least(pool, done, before + i)
                    rows_t = hn[:, norm_order(stage)[i], :]
                    nc.gpsimd.tensor_tensor(rows_t, rows_t, norm_rows[:, 1, :], ALU.add).then_inc(done, 1)

            add_b(0)
            pool.wait_ge(pads_zero, 3)
            pool.wait_ge(consts_in, 16 * 3)
            for g in range(GROUPS):
                pool.wait_ge(columns_out, IN_SBUF[f"u{g}"])
                u = pool_u[:, g, :]
                cur, start, step, bufs = u, 0, 1, [pool_a, pool_b]
                while step < WINDOWS[g]:
                    start += step
                    nxt = bufs[0]
                    bufs.reverse()
                    own.link(nc.gpsimd.tensor_tensor(nxt[:, start:], cur[:, start:],
                                                     cur[:, start - step:PAD + T - step], ALU.add))
                    cur, step = nxt, 2 * step
                own.mark(nc.gpsimd.tensor_tensor(pool_d[:, g, 0:PAD], cur[:, PAD:2 * PAD], inv_count[:, g, :],
                                                 ALU.mult))
                own.mark(nc.gpsimd.tensor_scalar(pool_d[:, g, PAD:], cur[:, 2 * PAD:], 1.0 / WINDOWS[g], None,
                                                 ALU.mult))
                own.settle()
                nc.gpsimd.tensor_tensor(pool_d[:, g, :], pool_d[:, g, :], u[:, PAD:],
                                        ALU.subtract).then_inc(pool_d_done, 1)

            add_b(1)
            pool.wait_ge(lo_cut, POOL_FIRST)
            with pool.Fori(0, POOL_TILES // 4) as it:
                for j in range(4):
                    t = Tile(POOL_FIRST + j, 4, it)
                    pool.wait_ge(hi_cut, t.n + 1)
                    pool.wait_ge(tile_used, t.n - RING + 1)
                    nc.gpsimd.tensor_tensor(cut[:, t.slot, 1, :], raw[:, t.slot, :], cut[:, t.slot, 0, :],
                                            ALU.subtract).then_inc(lo_cut, 1)
            pool.wait_ge(ids_done, 1)
            pool.wait_ge(ple_added, ND)
            pool.wait_ge(gated, TT)

            def gather(kind, it):
                def carry():
                    own.settle()
                    own.mark(nc.gpsimd.tensor_tensor(pool_word[:], pool_word[:], pool_word[:], ALU.add))

                for s in range(2):
                    carry()
                    own.mark(nc.gpsimd.tensor_copy(ids_now[:, s, :],
                                                   expert_id[:, bass.ds(16 * it + 8 * s, 8)]))
                    for j in range(8):
                        if kind == 1 or not isinstance(it, int) or 8 * s + j >= ROW_RING:
                            pool.wait_ge(rows_used, HK * kind + 16 * it + 8 * s + j - ROW_RING + 1)
                        carry()
                        nc.gpsimd.indirect_dma_start(
                            expert_rows[:, j % ROW_RING, :], None, v_rows if kind else u_rows,
                            bass.IndirectOffsetOnAxis(ap=ids_now[:, s, j:j + 1], axis=0)
                        ).then_inc(rows_in[j % ROW_RING], 16)

            GATHER_OWN = 20
            own.link(nc.gpsimd.memset(pool_word[:], 0.0))
            gather(0, 0)
            before = own.count
            with pool.Fori(1, HK // 16) as it:
                own.turns, own.count = GATHER_OWN * (it - 1), before
                gather(0, it)
            before += GATHER_OWN * (HK // 16 - 1)
            with pool.Fori(0, HK // 16) as it:
                own.turns, own.count = GATHER_OWN * it, before
                gather(1, it)
                assert own.count - before == GATHER_OWN
            add_b(2)

        @block.tensor
        def _(pe):
            def ple_products(first):
                for b in (first, first + 1):
                    at_least(pe, ple_out, b - 1)
                    for k in range(2):
                        mm = nc.tensor.matmul(bank[:, 4 + b % 2, :], ple_in_sb[:, k, (b // 2) * P:(b // 2 + 1) * P],
                                              ple_w_sb[:, k, (b % 2) * HALF:(b % 2 + 1) * HALF],
                                              start=(k == 0), stop=(k == 1))
                    mm.then_inc(ple_prod, 1)

            def turn(stage, mine=range(2 * TT)):
                for i in mine:
                    t, kh = i // 2, i % 2
                    pe.wait_ge(norm_done, TT * stage + t + 1)
                    if stage:
                        pe.wait_ge(turned_hi, KD * stage + i - 3)
                        pe.wait_ge(turned_lo, KD * stage + i - 3)
                    for k in range(4):
                        last = nc.tensor.transpose(bank[:, turn_bank(stage, i), k * P:(k + 1) * P],
                                                   hn[:, t, (4 * kh + k) * P:(4 * kh + k + 1) * P], ident_sb[:])
                    last.then_inc(turned, 1)

            def columns(t, index, parity, width=T, first_bank=4):
                pe.wait_ge(lo_cut, t.n + 1)
                at_least(pe, columns_out, index - 1)
                for k in range(KD):
                    w = [cut[:, t.slot, part_, k * P:(k + 1) * P] for part_ in range(2)]
                    dst = bank[:, first_bank + parity, 0:width]
                    nc.tensor.matmul(dst, w[0], hT[:, 0, k, 0:width], start=(k == 0), stop=False)
                    nc.tensor.matmul(dst, w[0], hT[:, 1, k, 0:width], start=False, stop=False)
                    last = nc.tensor.matmul(dst, w[1], hT[:, 0, k, 0:width], start=False, stop=(k == KD - 1))
                last.then_inc(tile_used, 1)

            def tokens(t, lhs, first, last_tile, count=None, token_tiles=TT):
                pe.wait_ge(lo_cut, t.n + 1)
                for tt in range(token_tiles):
                    for step, (a, b) in enumerate(((0, 0), (0, 1), (1, 0))):
                        for h in range(2):
                            mm = nc.tensor.matmul(bank[:, 2 * tt + h, :], lhs(a)[:, tt * P:(tt + 1) * P],
                                                  cut[:, t.slot, b, h * HALF:(h + 1) * HALF],
                                                  start=(first and step == 0), stop=(last_tile and step == 2))
                    if count is not None and tt < token_tiles - 1:
                        mm.then_inc(count, 1)
                mm.then_inc(tile_used, 1)

            def tokens_in_turn(run, lhs, count, token_tiles, ready=None):
                for tt in range(token_tiles):
                    for i, t in enumerate(run):
                        if tt == 0:
                            pe.wait_ge(lo_cut, t.n + 1)
                            if ready is not None:
                                pe.wait_ge(weight_lo, ready + i)
                        for step, (a, b) in enumerate(((0, 0), (0, 1), (1, 0))):
                            for h in range(2):
                                mm = nc.tensor.matmul(bank[:, 2 * tt + h, :], lhs(i, a)[:, tt * P:(tt + 1) * P],
                                                      cut[:, t.slot, b, h * HALF:(h + 1) * HALF],
                                                      start=False, stop=(i == len(run) - 1 and step == 2))
                        if tt == token_tiles - 1:
                            mm.then_inc(tile_used, 1)
                        elif i == len(run) - 1:
                            mm.then_inc(count, 1)

            def values():
                pe.wait_ge(columns_out, 2)
                for c in range(NCH):
                    last = nc.tensor.transpose(bank[:, 6 + c // 4, (c % 4) * P:(c % 4 + 1) * P],
                                               vT[:, c * CHUNK:c * CHUNK + P], ident_sb[:])
                last.then_inc(v_turned, 1)

            def attn_scores(m):
                j, kv = m // 2, m % 2
                pe.wait_ge(columns_out, IN_SBUF[f"q{j}"])
                at_least(pe, s_out, m - 1)
                r = slice(kv * HD, (kv + 1) * HD)
                for c in range(NCH):
                    last = nc.tensor.matmul(
                        bank[(c % 2) * CHUNK:(c % 2 + 1) * CHUNK, m % 2, (c // 2) * P:(c // 2 + 1) * P],
                        qT[r, j, c * CHUNK:(c + 1) * CHUNK], kT[r, c * CHUNK:c * CHUNK + P],
                        start=True, stop=True, skip_group_check=True)
                last.then_inc(s_done, 1)

            def turn_probs(m, pooled=0):
                pe.wait_ge(probs_done, m + 1)
                at_least(pe, probs_T_done, m - 1)
                at_least(pe, y_lo, pooled)
                for t in range(TT):
                    last = nc.tensor.transpose(bank[:, 2 + m % 2, t * P:(t + 1) * P], probs[:, m % 2, t, :],
                                               ident_sb[:])
                last.then_inc(probs_turned, 1)

            def attend(m):
                j, kv = m // 2, m % 2
                pe.wait_ge(probs_T_done, m + 1)
                pe.wait_ge(v_band_done, 2)
                at_least(pe, o_lo, j - 1)
                r = slice(kv * HD, (kv + 1) * HD)
                for c in range(NCH):
                    last = nc.tensor.matmul(bank[r, 6 + j % 2, c * CHUNK:(c + 1) * CHUNK], v_band[:, c, r],
                                            probs_T[:, m % 2, c * CHUNK:(c + 1) * CHUNK],
                                            start=True, stop=True, skip_group_check=True)
                last.then_inc(pv_done, 1)

            def pool_product(g, turned_m):
                pe.wait_ge(pool_d_done, g + 1)
                pe.wait_ge(probs_T_done, turned_m)
                at_least(pe, y_lo, g - 1)
                nc.tensor.matmul(bank[:, 2 + g % 2, :], pool_w_sb[:, g, :], pool_d[:, g, :],
                                 start=True, stop=True).then_inc(pool_prod, 1)

            pe.wait_ge(ident_in, 16)
            turn(0)
            pe.wait_ge(turned_lo, KD)
            pe.wait_ge(pads_zero, 3)
            pe.wait_ge(consts_in, 16 * 3)
            for n in range(3):
                columns(Tile(n), n, n % 2)
            values()
            attn_scores(0)
            columns(Tile(3), 3, 1)
            attn_scores(1)
            columns(Tile(4), 4, 0)
            turn_probs(0)
            attn_scores(2)
            columns(Tile(5), 5, 1)
            attend(0)
            turn_probs(1)
            attn_scores(3)
            columns(Tile(6), 6, 0)
            attend(1)
            turn_probs(2)
            attn_scores(4)
            columns(Tile(7), 7, 1)
            attend(2)
            pool_product(0, 3)
            turn_probs(3)
            attn_scores(5)
            columns(Tile(8), 8, 0)
            attend(3)
            turn_probs(4, 1)
            attn_scores(6)
            columns(Tile(9), 9, 1)
            attend(4)
            pool_product(1, 5)
            turn_probs(5, 2)
            attn_scores(7)
            attend(5)
            pool_product(2, 6)
            turn_probs(6, 3)
            attend(6)
            turn_probs(7)
            attend(7)
            pool_product(3, 8)
            pe.wait_ge(columns_out, N_IN)
            pe.wait_ge(o_lo, PAIRS)
            pe.wait_ge(y_lo, GROUPS)
            pe.wait_ge(s_out, 8)
            for k in range(KD - RING):
                tokens(Tile(T_O + k), lambda a, k=k: mixT[:, a, k, :], k == 0, False)
            tokens_in_turn([Tile(T_Q - RING + i) for i in range(RING)],
                           lambda i, a: mixT[:, a, KD - RING + i, :], mix_done, TT)
            pe.wait_ge(ple_loaded, 32)
            pe.wait_ge(resid_done, 6)
            ple_products(0)
            turn(1, range(4))
            ple_products(2)
            turn(1, range(4, 6))
            ple_products(4)
            turn(1, range(6, 8))
            ple_products(6)
            pe.wait_ge(turned_lo, 2 * KD)
            pe.wait_ge(ple_out, 8)
            pe.wait_ge(subkeys_in, 16)

            def key_scores(hp, j, index):
                pe.wait_ge(columns_out, index + 1)
                at_least(pe, scores_out, hp - 1)
                for t in range(TT):
                    last = nc.tensor.matmul(bank[:, 6 + j % 2, t * P:(t + 1) * P],
                                            queries[:, j % 2, t * P:(t + 1) * P],
                                            subkeys_sb[:, hp, :] if isinstance(hp, int) else
                                            subkeys_sb[:, bass.ds(hp, 1), :].rearrange("p a n -> p (a n)"),
                                            start=True, stop=True, skip_group_check=True)
                last.then_inc(scores_done, 1)

            def retrieve(it):
                for j in range(4):
                    columns(Tile(T_Q + j, 4, it), N_IN + 4 * it + j, j % 2)
                    if j:
                        key_scores(4 * it + j - 1, j - 1, N_IN + 4 * it + j - 1)
                key_scores(4 * it + 3, 3, N_IN + 4 * it + 3)

            retrieve(0)
            with pe.Fori(1, N_Q // 4) as it:
                retrieve(it)
            pe.wait_ge(columns_out, N_IN + N_Q)
            pe.wait_ge(scores_out, N_Q)
            for k in range(KD):
                tokens(Tile(T_G + k), lambda a, k=k: hT[:, a, k, :], k == 0, k == KD - 1,
                       gate_prod if k == KD - 1 else None)
            pe.wait_ge(gate_lin, 8)
            u_index = N_IN + N_Q
            with pe.Fori(0, U_TOPK // 4) as it:
                for j in range(4):
                    columns(Tile(T_U + j, 4, it), u_index + 4 * it + j, j % 2, TD, 6)
            for j in range(U_SOFTMAX):
                columns(Tile(T_U + U_TOPK + j), u_index + U_TOPK + j, j % 2, TD, 6)
            pe.wait_ge(gates_done, 1)
            for w in range(3):
                for t in range(ND):
                    last = nc.tensor.transpose(bank[:, w, t * P:(t + 1) * P], picked[:, w, t, :], ident_sb[:])
                last.then_inc(rows_turned, 1)
            pe.wait_ge(rows_idx, 2)
            pe.wait_ge(rows_done, 1)

            def gate_products(q, b):
                pe.wait_ge(onehot_done, q + 1)
                for four in range(4):
                    at_least(pe, gates_out, 4 * q + four - 3)
                    for u in range(4):
                        a, t = (4 * four + u) // OT, (4 * four + u) % OT
                        dst = bank[:, four, u * P:(u + 1) * P]
                        nc.tensor.matmul(dst, onehot[:, b, a, :, t], onehot_hi[:, b, a, :, t],
                                         start=True, stop=False, skip_group_check=True)
                        mm = nc.tensor.matmul(dst, onehot[:, b, a, :, t], onehot_lo[:, b, a, :, t],
                                              start=False, stop=True, skip_group_check=True)
                    mm.then_inc(gates_prod, 1)

            def build_gates(it):
                for s in range(2):
                    for j in range(4):
                        c = U_TOPK + U_SOFTMAX + 4 * s + j
                        columns(Tile(T_U + c, 8, it), u_index + c + 8 * it, j % 2, TD, 6)
                        if j % 2:
                            gate_products(4 * it + 2 * s + j // 2, j // 2)

            build_gates(0)
            with pe.Fori(1, U_GATES // 8) as it:
                build_gates(it)
            u_index += U_EARLY
            for i in range(2):
                columns(Tile(T_BOTH + i), u_index + i, i % 2, TD, 6)
            pe.wait_ge(gates_out, TD // 4)

            def both(e):
                for p in range(8):
                    t = Tile(T_BOTH + 2 + 16 * e + 2 * p) if isinstance(e, int) else Tile(T_BOTH + 2 + 2 * p, 16, e)
                    i = 8 * e + p
                    if t.c < T_LATE - 2:
                        columns(t, u_index + i + 2, p % 2, TD, 6)
                        t = t.plus(1)
                    else:
                        t = Tile(T_LATE + i - N_BOTH)
                    pe.wait_ge(weight_lo, i + 1)
                    tokens(t, lambda a, p=p: weight_cut[:, p % RING, a, :], isinstance(i, int) and i == 0, False,
                           None, ND)

            both(0)
            with pe.Fori(1, EIGHTS - 1) as e:
                both(e)
            both(EIGHTS - 1)

            def late(e):
                fixed = isinstance(e, int)
                for v in range(8 - RING if fixed else 8):
                    t = Tile(T_LATE + 8 * e + v) if fixed else Tile(T_LATE + v, 8, e)
                    pe.wait_ge(weight_lo, N_BOTH + 8 * e + v + 1)
                    tokens(t, lambda a, v=v: weight_cut[:, v % RING, a, :], False, False, None, ND)

            with pe.Fori(0, N_LATE // 8 - 1) as e:
                late(e)
            late(N_LATE // 8 - 1)
            tokens_in_turn([Tile(T_ALL - RING + i) for i in range(RING)], lambda i, a: weight_cut[:, i, a, :],
                           experts_done, ND, N_BOTH + N_LATE - RING + 1)

        @block.scalar
        def _(act):
            def split_hi(t):
                act.wait_ge(tile_in[t.slot], 16 * (t.round + 1))
                at_least(act, tile_used, t.n - RING + 1)
                nc.scalar.activation(cut[:, t.slot, 0, :], raw[:, t.slot, :], ACT.Copy,
                                     scale=t.scale).then_inc(hi_cut, 1)

            def scale_and_split_hi(t):
                act.wait_ge(tile_in[t.slot], 16 * (t.round + 1))
                nc.scalar.activation(raw[:, t.slot, :], raw[:, t.slot, :], ACT.Copy,
                                     scale=S_W).then_inc(raw_scaled, 1)
                act.wait_ge(raw_scaled, t.n - POOL_FIRST + 1)
                act.wait_ge(tile_used, t.n - RING + 1)
                nc.scalar.activation(cut[:, t.slot, 0, :], raw[:, t.slot, :], ACT.Copy).then_inc(hi_cut, 1)

            def take_ple(first):
                for b in (first, first + 1):
                    act.wait_ge(ple_prod, b + 1)
                    nc.scalar.activation(ple_sb[:, b, :], bank[:, 4 + b % 2, :], ACT.Copy).then_inc(ple_out, 1)

            def turn_hi(stage, mine=range(2 * TT)):
                for i in mine:
                    t, kh = i // 2, i % 2
                    act.wait_ge(turned, KD * stage + i + 1)
                    nc.scalar.activation(hT[:, 0, 4 * kh:4 * kh + 4, t * P:(t + 1) * P],
                                         bank[:, turn_bank(stage, i), :].rearrange("p (k t) -> p k t", k=4), ACT.Copy,
                                         scale=S_ACT).then_inc(turned_hi, 1)

            def take(n, dst):
                act.wait_ge(tile_used, n + 1)
                nc.scalar.activation(dst, bank[:, 4 + n % 2, :], ACT.Copy,
                                     scale=1 / (S_W * S_ACT)).then_inc(columns_out, 1)

            def exponentials(m):
                act.wait_ge(max_done, m + 1)
                for t in range(TT):
                    nc.scalar.activation(probs[:, m % 2, t, :], probs[:, m % 2, t, :], ACT.Exp,
                                         bias=neg_max[:, m % 2, t:t + 1],
                                         accum_out=row_sum[:, m % 2, t:t + 1])
                nc.scalar.activation(sink_exp[:, m % 2, :], neg_max[:, m % 2, :], ACT.Exp,
                                     bias=sink[:, m:m + 1]).then_inc(exp_done, 1)

            def take_probs_T(m):
                act.wait_ge(probs_turned, m + 1)
                at_least(act, pv_done, m - 1)
                nc.scalar.activation(probs_T[:, m % 2, :], bank[:, 2 + m % 2, :], ACT.Copy).then_inc(probs_T_done, 1)

            def take_o(j):
                act.wait_ge(pv_done, 2 * j + 2)
                nc.scalar.activation(mixT[:, 0, j, :], bank[:, 6 + j % 2, :], ACT.Copy,
                                     scale=S_ACT).then_inc(o_hi, 1)

            def roots(stage, i=None):
                order = norm_order(stage)
                mine = range(TT) if i is None else (i,)
                cols = slice(0, TT) if i is None else slice(order[i], order[i] + 1)
                n = norm_batch(stage, i)
                act.wait_ge(stats_done, n + 1)
                nc.scalar.activation(std[:, cols], variance[:, cols], ACT.Sqrt).then_inc(rstd_done, 1)
                act.wait_ge(shift_done, n + 1)
                for m in mine:
                    t = order[m]
                    nc.scalar.activation(hn[:, t, :], hn[:, t, :], ACT.Identity, bias=shift[:, t:t + 1],
                                         scale=rstd[:, t:t + 1]).then_inc(centred, 1)

            def take_y(g):
                act.wait_ge(pool_prod, g + 1)
                act.wait_ge(scale_done, 1)
                nc.scalar.activation(mixT[:, 0, PAIRS + g, :], bank[:, 2 + g % 2, :], ACT.Copy,
                                     scale=pool_scale_s[:, g:g + 1]).then_inc(y_hi, 1)

            roots(0)
            split_hi(Tile(0))
            split_hi(Tile(1))
            turn_hi(0)
            act.wait_ge(pads_zero, 3)
            act.wait_ge(consts_in, 16 * 3)
            split_hi(Tile(2))
            take(0, kT[:, CHUNK:])
            split_hi(Tile(3))
            take(1, vT[:, CHUNK:])
            split_hi(Tile(4))
            take(2, qT[:, 0, :])
            act.wait_ge(v_turned, 1)
            for c in range(2):
                nc.scalar.activation(v_band[:, 4 * c:4 * c + 4, :],
                                     bank[:, 6 + c, :].rearrange("p (a b) -> p a b", a=4),
                                     ACT.Copy).then_inc(v_band_done, 1)
            split_hi(Tile(5))
            exponentials(0)
            take(3, qT[:, 1, :])
            split_hi(Tile(6))
            exponentials(1)
            take(4, pool_u[:, 0, PAD:])
            take_probs_T(0)
            split_hi(Tile(7))
            exponentials(2)
            take(5, qT[:, 2, :])
            take_probs_T(1)
            split_hi(Tile(8))
            exponentials(3)
            take(6, pool_u[:, 1, PAD:])
            take_probs_T(2)
            take_o(0)
            split_hi(Tile(9))
            exponentials(4)
            take(7, qT[:, 3, :])
            take_y(0)
            take_probs_T(3)
            split_hi(Tile(10))
            exponentials(5)
            take(8, pool_u[:, 2, PAD:])
            take_probs_T(4)
            take_o(1)
            split_hi(Tile(11))
            exponentials(6)
            take(9, pool_u[:, 3, PAD:])
            take_y(1)
            take_probs_T(5)
            exponentials(7)
            split_hi(Tile(12))
            take_y(2)
            take_probs_T(6)
            take_o(2)
            split_hi(Tile(13))
            take_probs_T(7)
            take_o(3)
            take_y(3)
            for n in range(T_O + 4, T_Q):
                split_hi(Tile(n))
            for i in range(TT - 1):
                roots(1, i)
            for n in range(T_Q, T_Q + SPLIT_AHEAD):
                split_hi(Tile(n))
            take_ple(0)
            roots(1, TT - 1)
            turn_hi(1, range(4))
            take_ple(2)
            turn_hi(1, range(4, 6))
            take_ple(4)
            turn_hi(1, range(6, 8))
            take_ple(6)

            def take_scores(hp, j):
                act.wait_ge(scores_done, hp + 1)
                dst = scores[:, hp, :] if isinstance(hp, int) else \
                    scores[:, bass.ds(hp, 1), :].rearrange("p a n -> p (a n)")
                nc.scalar.activation(dst, bank[:, 6 + j % 2, :], ACT.Copy).then_inc(scores_out, 1)

            def retrieve(it):
                for j in range(4):
                    t = Tile(T_Q + j, 4, it)
                    scale_and_split_hi(t.plus(SPLIT_AHEAD))
                    act.wait_ge(tile_used, t.n + 1)
                    at_least(act, scores_done, 4 * it + j - 1)
                    nc.scalar.activation(queries[:, j % 2, :], bank[:, 4 + j % 2, :], ACT.Copy,
                                         scale=1 / (S_W * S_ACT)).then_inc(columns_out, 1)
                    if j:
                        take_scores(4 * it + j - 1, j - 1)
                take_scores(4 * it + 3, 3)

            retrieve(0)
            with act.Fori(1, N_Q // 4) as it:
                retrieve(it)
            for n in range(T_G, T_U):
                scale_and_split_hi(Tile(n + SPLIT_AHEAD))
            for b in range(8):
                if b < 6:
                    act.wait_ge(gate_prod, b // 2 + 1)
                else:
                    act.wait_ge(tile_used, T_U)
                nc.scalar.activation(ple_gate[:, b, :], bank[:, b, :], ACT.Copy,
                                     scale=1 / (S_W * S_ACT)).then_inc(gate_lin, 1)

            def gelu(t, slot, group=None, used=None, kept=None):
                act.wait_ge(tile_used, t.n + 1)
                dst = gelu_out[:, slot, :]
                if kept is not None:
                    dst = gelu_kept[:, kept, :]
                elif group is not None:
                    at_least(act, gelu_stored[slot], 16 * group)
                else:
                    act.wait_ge(weight_done, used)
                nc.scalar.activation(dst, bank[:, 6 + slot % 2, 0:TD], ACT.Gelu,
                                     scale=1 / (S_W * S_ACT)).then_inc(columns_out, 1)

            for j in range(4):
                scale_and_split_hi(Tile(T_U + j + SPLIT_AHEAD))
                gelu(Tile(T_U + j), j, 0)
            with act.Fori(1, U_TOPK // 4) as it:
                for j in range(4):
                    t = Tile(T_U + j, 4, it)
                    scale_and_split_hi(t.plus(SPLIT_AHEAD))
                    gelu(t, j, it)
            for j in range(U_SOFTMAX):
                t = Tile(T_U + U_TOPK + j)
                scale_and_split_hi(t.plus(SPLIT_AHEAD))
                if j == 0:
                    act.wait_ge(gate_shift, 1)
                    nc.scalar.activation(picked[:, 2], picked[:, 2], ACT.Exp).then_inc(gate_exp, 1)
                if j == 2:
                    for tt in range(TT):
                        act.wait_ge(gate_biased, tt + 1)
                        nc.scalar.activation(ple_gate[:, 2 * tt:2 * tt + 2, :], ple_gate[:, 2 * tt:2 * tt + 2, :],
                                             ACT.Sigmoid).then_inc(gate_sig, 1)
                gelu(t, j % 4, (U_TOPK + j) // 4)
            for w in range(2):
                act.wait_ge(rows_turned, w + 1)
                nc.scalar.activation(rows[:, w, :], bank[:, w, 0:TD], ACT.Copy).then_inc(rows_idx, 1)

            def take_gates(q, b, s, chunk_round):
                for four in range(4):
                    act.wait_ge(gates_prod, 4 * q + four + 1)
                    if b == 0 and four == 0:
                        at_least(act, gates_stored[s], 16 * chunk_round)
                    first = BATCH * b + 4 * four
                    nc.scalar.activation(gate_chunk[:, s, :, first:first + 4].rearrange("p n t -> p t n"),
                                         bank[:, four, :].rearrange("p (t n) -> p t n", t=4),
                                         ACT.Copy).then_inc(gates_out, 1)

            def build_gates(it, last=False):
                for s in range(2):
                    for j in range(4):
                        c = U_TOPK + U_SOFTMAX + 4 * s + j
                        t = Tile(T_U + c, 8, it)
                        split_hi(t.plus(SPLIT_AHEAD))
                        gelu(t, j, c // 4 + 2 * it, kept=4 * s + j if last else None)
                        if j % 2:
                            take_gates(4 * it + 2 * s + j // 2, j // 2, s, it)

            build_gates(0)
            with act.Fori(1, U_GATES // 8 - 1) as it:
                build_gates(it)
            build_gates(U_GATES // 8 - 1, True)
            def weight_high(i, slot, last_use):
                act.wait_ge(weight_done, i + 1)
                if last_use is not None:
                    act.wait_ge(tile_used, last_use + 1)
                nc.scalar.activation(weight_cut[:, slot, 0, :], weight[:, slot, :], ACT.Copy).then_inc(weight_hi, 1)

            for i in range(2):
                split_hi(Tile(T_BOTH + i + SPLIT_AHEAD))
                gelu(Tile(T_BOTH + i), i, STORED)
            weight_high(0, 0, None)

            def v_tile(i):
                if isinstance(i, int) and i >= N_BOTH - 2:
                    return T_LATE + i - N_BOTH
                return T_BOTH + 3 + 2 * i

            def both(e):
                for p in range(8):
                    t = Tile(T_BOTH + 2 + 16 * e + 2 * p) if isinstance(e, int) else Tile(T_BOTH + 2 + 2 * p, 16, e)
                    i = 8 * e + p
                    no_use = isinstance(i, int) and i + 1 < RING
                    if t.c >= T_LATE - 2:
                        split_hi(Tile(T_LATE + i - N_BOTH + SPLIT_AHEAD))
                        for w in ((i + 1, i + 2) if i == N_BOTH - 2 else (i + 2,)):
                            weight_high(w, w % RING, v_tile(w - RING))
                        continue
                    split_hi(t.plus(SPLIT_AHEAD))
                    weight_high(i + 1, (p + 1) % RING, None if no_use else v_tile(i + 1 - RING))
                    if isinstance(i, int) and i + 2 < VG:
                        gelu(t, (p + 2) % VG, STORED)
                    else:
                        gelu(t, (p + 2) % VG, used=i + 2 - VG + 1)
                    split_hi(t.plus(1 + SPLIT_AHEAD))

            both(0)
            with act.Fori(1, len(EIGHT_DOTS)) as e:
                both(e)
            act.wait_ge(dots_done, 1)
            nc.scalar.activation(dots[:], dots[:], ACT.Gelu).then_inc(dots_gelu, 1)
            for e in range(len(EIGHT_DOTS), EIGHTS):
                both(e)

            def late(e):
                fixed = isinstance(e, int)
                for v in range(8):
                    t = Tile(T_LATE + 8 * e + v) if fixed else Tile(T_LATE + v, 8, e)
                    if not fixed or t.n + SPLIT_AHEAD < T_ALL:
                        split_hi(t.plus(SPLIT_AHEAD))
                        weight_high(N_BOTH + 8 * e + v + 2, (v + 2) % RING, T_LATE + 8 * e + v + 2 - RING)

            with act.Fori(0, N_LATE // 8 - 1) as e:
                late(e)
            late(N_LATE // 8 - 1)
            for i in range(TT):
                roots(2, i)

        @block.vector
        def _(dve):
            own = Tally(dve, dve_own)

            def split_lo(t):
                dve.wait_ge(hi_cut, t.n + 1)
                at_least(dve, tile_used, t.n - RING + 1)
                nc.vector.scalar_tensor_tensor(out=cut[:, t.slot, 1, :], in0=raw[:, t.slot, :], scalar=t.scale,
                                               in1=cut[:, t.slot, 0, :], op0=ALU.mult,
                                               op1=ALU.subtract).then_inc(lo_cut, 1)

            def turn_lo(stage):
                for i in range(2 * TT):
                    t, kh = i // 2, i % 2
                    dve.wait_ge(turned_hi, KD * stage + i + 1)
                    nc.vector.scalar_tensor_tensor(
                        out=hT[:, 1, 4 * kh:4 * kh + 4, t * P:(t + 1) * P],
                        in0=bank[:, turn_bank(stage, i), :].rearrange("p (k t) -> p k t", k=4), scalar=S_ACT,
                        in1=hT[:, 0, 4 * kh:4 * kh + 4, t * P:(t + 1) * P], op0=ALU.mult,
                        op1=ALU.subtract).then_inc(turned_lo, 1)

            def layer_norm(stage, i):
                t = norm_order(stage)[i]
                dve.wait_ge(centred, TT * stage + i + 1)
                dve.wait_ge(norms_in, 16 * (stage + 1))
                nc.vector.tensor_tensor(hn[:, t, :], hn[:, t, :], norm_rows[:, 0, :],
                                        ALU.mult).then_inc(rows_scaled, 1)

            def add_b(stage, i):
                t = norm_order(stage)[i]
                dve.wait_ge(rows_scaled, TT * stage + i + 1)
                done, before = (final_done, 0) if stage == 2 else (norm_done, TT * stage)
                at_least(dve, done, before + i)
                nc.vector.tensor_tensor(hn[:, t, :], hn[:, t, :], norm_rows[:, 1, :], ALU.add).then_inc(done, 1)

            def row_stats(t):
                for h in range(2):
                    own.mark(nc.vector.bn_stats(stats[:, t, 6 * h:6 * h + 6], hn[:, t, h * HALF:(h + 1) * HALF]))

            def row_moments(stage, eps, i=None):
                mine = range(TT) if i is None else (norm_order(stage)[i],)
                cols = slice(mine[0], mine[-1] + 1)
                own.settle()
                for t in mine:
                    own.mark(nc.vector.bn_aggr(moments[:, t, :], stats[:, t, :]))
                own.settle()
                nc.vector.tensor_scalar(variance[:, cols], moments[:, cols, 1], eps, None,
                                        ALU.add).then_inc(stats_done, 1)
                dve.wait_ge(rstd_done, norm_batch(stage, i) + 1)
                r, n = rstd[:, cols], newton[:, cols]
                own.link(nc.vector.reciprocal(r, std[:, cols]))
                own.link(nc.vector.tensor_tensor(n, r, r, ALU.mult))
                own.link(nc.vector.tensor_tensor(n, n, variance[:, cols], ALU.mult))
                own.link(nc.vector.tensor_scalar(n, n, -0.5, 1.5, ALU.mult, ALU.add))
                own.link(nc.vector.tensor_tensor(r, r, n, ALU.mult))
                nc.vector.scalar_tensor_tensor(out=shift[:, cols], in0=moments[:, cols, 0], scalar=-1.0, in1=r,
                                               op0=ALU.mult, op1=ALU.mult).then_inc(shift_done, 1)

            def mask_and_max(m):
                dve.wait_ge(s_done, m + 1)
                at_least(dve, probs_turned, m - 1)
                buf = probs[:, m % 2]
                nc.vector.scalar_tensor_tensor(
                    out=buf, in0=bank[:, m % 2, :].rearrange("p (t k) -> p t k", t=TT), scalar=HD ** -0.5,
                    in1=alibi_sb[:, m:m + 1, :].to_broadcast([P, TT, P]), op0=ALU.mult,
                    op1=ALU.add).then_inc(s_out, 1)
                dve.wait_ge(s_out, m + 1)
                own.link(nc.vector.memset(buf[0:CHUNK, 0, 0:CHUNK], NEG))
                own.link(nc.vector.tensor_reduce(row_max[:, m % 2, :], buf, AX.X, ALU.max))
                nc.vector.tensor_scalar(neg_max[:, m % 2, :], row_max[:, m % 2, :], sink[:, m:m + 1], -1.0,
                                        ALU.max, ALU.mult).then_inc(max_done, 1)

            def normalise(m):
                dve.wait_ge(exp_done, m + 1)
                own.link(nc.vector.tensor_tensor(denom[:, m % 2, :], row_sum[:, m % 2, :], sink_exp[:, m % 2, :],
                                                 ALU.add))
                own.link(nc.vector.reciprocal(inv_den[:, m % 2, :], denom[:, m % 2, :]))
                nc.vector.tensor_tensor(probs[:, m % 2], probs[:, m % 2],
                                        inv_den[:, m % 2, :].unsqueeze(2).to_broadcast([P, TT, P]),
                                        ALU.mult).then_inc(probs_done, 1)

            def take_o(j):
                dve.wait_ge(o_hi, j + 1)
                nc.vector.scalar_tensor_tensor(out=mixT[:, 1, j, :], in0=bank[:, 6 + j % 2, :], scalar=S_ACT,
                                               in1=mixT[:, 0, j, :], op0=ALU.mult,
                                               op1=ALU.subtract).then_inc(o_lo, 1)

            def take_y(g):
                dve.wait_ge(y_hi, g + 1)
                nc.vector.scalar_tensor_tensor(out=mixT[:, 1, PAIRS + g, :], in0=bank[:, 2 + g % 2, :],
                                               scalar=pool_scale_s[:, g:g + 1], in1=mixT[:, 0, PAIRS + g, :],
                                               op0=ALU.mult, op1=ALU.subtract).then_inc(y_lo, 1)

            nc.vector.memset(kT[:, 0:CHUNK], 0.0).then_inc(pads_zero, 1)
            nc.vector.memset(vT[:, 0:CHUNK], 0.0).then_inc(pads_zero, 1)
            nc.vector.memset(pool_u[:, :, 0:PAD], 0.0).then_inc(pads_zero, 1)
            dve.wait_ge(pads_zero, 3)
            for t in range(TT):
                dve.wait_ge(x_in[t], 16)
                row_stats(t)
            row_moments(0, EPS)
            for i in range(TT):
                layer_norm(0, i)
            for i in (1, 3):
                add_b(0, i)
            split_lo(Tile(0))
            split_lo(Tile(1))
            turn_lo(0)
            split_lo(Tile(2))
            dve.wait_ge(consts_in, 16 * 3)
            nc.vector.tensor_scalar(pool_scale_s[:], pool_scale, S_ACT, None, ALU.mult).then_inc(scale_done, 1)
            dve.wait_ge(scale_done, 1)
            split_lo(Tile(3))
            split_lo(Tile(4))
            mask_and_max(0)
            split_lo(Tile(5))
            mask_and_max(1)
            normalise(0)
            split_lo(Tile(6))
            mask_and_max(2)
            normalise(1)
            split_lo(Tile(7))
            mask_and_max(3)
            normalise(2)
            split_lo(Tile(8))
            mask_and_max(4)
            normalise(3)
            take_o(0)
            split_lo(Tile(9))
            take_y(0)
            mask_and_max(5)
            normalise(4)
            split_lo(Tile(10))
            mask_and_max(6)
            normalise(5)
            take_o(1)
            split_lo(Tile(11))
            take_y(1)
            mask_and_max(7)
            normalise(6)
            split_lo(Tile(12))
            take_y(2)
            normalise(7)
            take_o(2)
            split_lo(Tile(13))
            take_o(3)
            take_y(3)
            for n in range(T_O + 4, T_Q):
                split_lo(Tile(n))
            for t in range(TT):
                if t < TT - 1:
                    dve.wait_ge(mix_done, t + 1)
                else:
                    dve.wait_ge(tile_used, T_Q)
                for h in range(2):
                    rows_b = hn[:, t, h * HALF:(h + 1) * HALF]
                    nc.vector.scalar_tensor_tensor(out=rows_b, in0=bank[:, 2 * t + h, :],
                                                   scalar=1 / (S_W * S_ACT * ALPHA), in1=rows_b, op0=ALU.mult,
                                                   op1=ALU.add).then_inc(resid_done, 1)
                dve.wait_ge(resid_done, 2 * t + 2)
                row_stats(t)
                row_moments(1, EPS / ALPHA ** 2, t)
                if t:
                    layer_norm(1, t - 1)
            layer_norm(1, TT - 1)
            add_b(1, TT - 1)
            turn_lo(1)
            for n in range(T_Q, T_Q + SPLIT_AHEAD):
                split_lo(Tile(n))

            def top16(values, index, source, spare):
                rows_n = source.shape[1]

                def settle():
                    own.settle()
                    own.mark(nc.vector.memset(word[:], 0.0))

                settle()
                for t in range(rows_n):
                    own.mark(nc.vector.max(values[:, t, 0:8], source[:, t, :]))
                settle()
                for t in range(rows_n):
                    own.mark(nc.vector.max_index(index[:, t, 0:8], values[:, t, 0:8], source[:, t, :]))
                for t in range(rows_n):
                    own.mark(nc.vector.match_replace(spare[:, t, :], values[:, t, 0:8], source[:, t, :], LOWEST))
                settle()
                for t in range(rows_n):
                    own.mark(nc.vector.max(values[:, t, 8:16], spare[:, t, :]))
                settle()
                for t in range(rows_n):
                    own.mark(nc.vector.max_index(index[:, t, 8:16], values[:, t, 8:16], spare[:, t, :]))

            def add_sides():
                own.settle()
                own.mark(nc.vector.tensor_tensor(
                    sums.rearrange("p t (a b) -> p t a b", a=K),
                    top_v[:, 0].unsqueeze(3).to_broadcast([P, TT, K, K]),
                    top_v[:, 1].unsqueeze(2).to_broadcast([P, TT, K, K]), ALU.add))
                own.mark(nc.vector.tensor_copy(top_f, top_i))
                own.settle()

            def pick(head):
                own.settle()
                own.mark(nc.vector.tensor_single_scalar(half_i[:, 0], sum_i, 4, ALU.logical_shift_right))
                own.mark(nc.vector.tensor_single_scalar(half_i[:, 1], sum_i, K - 1, ALU.bitwise_and))
                own.settle()
                own.link(nc.vector.tensor_copy(half_f, half_i))
                shape = [P, 2 * TT * K, K]
                own.link(nc.vector.tensor_tensor(
                    hit, iota_k_sb[:].unsqueeze(1).to_broadcast(shape),
                    half_f.rearrange("p s t k -> p (s t k)").unsqueeze(2).to_broadcast(shape), ALU.is_equal))
                hit_rows = hit.rearrange("p (r k) m -> p r k m", k=K)
                own.link(nc.vector.tensor_tensor(
                    hit_rows, hit_rows, top_f.rearrange("p s t k -> p (s t) k").unsqueeze(2).to_broadcast(
                        [P, 2 * TT, K, K]), ALU.mult))
                for p in range(2):
                    own.mark(nc.vector.tensor_reduce(
                        picked[:, p, :, bass.ds(K * head, K)], hit_rows[:, TT * p:TT * (p + 1)], AX.X, ALU.add))
                own.mark(nc.vector.tensor_copy(picked[:, 2, :, bass.ds(K * head, K)], sum_v))
                own.settle()

            def top_k(head):
                start = own.count
                own.settle()
                own.link(nc.vector.tensor_copy(side, scores[:, bass.ds(2 * head, 2), :]))
                top16(top_v.rearrange("p s t k -> p (s t) k"), top_i.rearrange("p s t k -> p (s t) k"),
                      side.rearrange("p s (t n) -> p (s t) n", t=TT), replaced)
                add_sides()
                top16(sum_v, sum_i, sums, sums_rep)
                pick(head)
                assert own.count - start == STEPS, own.count - start

            STEPS, GATES_OWN = 79, 25
            dve.wait_ge(tables_in, 16 * 3)
            before = own.count
            with dve.Fori(0, HEADS) as head:
                own.turns, own.count = STEPS * head, before
                dve.wait_ge(scores_out, 2 * head + 2)
                top_k(head)
            own.turns, own.count = 0, before + STEPS * HEADS
            e_view = picked[:, 2].rearrange("p t (h k) -> p (t h) k", k=K)
            own.link(nc.vector.tensor_copy(e_sum, e_view[:, :, 0]))
            nc.vector.tensor_tensor(e_view, e_view, e_sum.unsqueeze(2).to_broadcast([P, TT * HEADS, K]),
                                    ALU.subtract).then_inc(gate_shift, 1)
            own.link(nc.vector.scalar_tensor_tensor(out=expert_f[:], in0=picked[:, 0, ND, :], scalar=float(NKEY),
                                                    in1=picked[:, 1, ND, :], op0=ALU.mult, op1=ALU.add))
            nc.vector.tensor_copy(expert_id[:], expert_f[:]).then_inc(ids_done, 1)
            def add_gate_b(tt):
                dve.wait_ge(gate_lin, 2 * tt + 2)
                gate_t = ple_gate[:, 2 * tt:2 * tt + 2, :].rearrange("p a n -> p (a n)")
                nc.vector.tensor_tensor(gate_t, gate_t, gate_b_row[:], ALU.add).then_inc(gate_biased, 1)

            add_gate_b(0)
            add_gate_b(1)
            dve.wait_ge(gate_exp, 1)
            own.link(nc.vector.tensor_reduce(e_sum, e_view, AX.X, ALU.add))
            own.link(nc.vector.reciprocal(e_inv, e_sum))
            nc.vector.tensor_tensor(e_view, e_view, e_inv.unsqueeze(2).to_broadcast([P, TT * HEADS, K]),
                                    ALU.mult).then_inc(gates_done, 1)
            add_gate_b(2)
            add_gate_b(3)
            for tt in range(TT):
                dve.wait_ge(gate_sig, tt + 1)
                nc.vector.scalar_tensor_tensor(out=ple_gate[:, 2 * tt:2 * tt + 2, :],
                                               in0=ple_sb[:, 2 * tt:2 * tt + 2, :], scalar=1 / ALPHA,
                                               in1=ple_gate[:, 2 * tt:2 * tt + 2, :], op0=ALU.mult,
                                               op1=ALU.mult).then_inc(gated, 1)
            dve.wait_ge(gated, TT)
            for tt in range(ND):
                nc.vector.tensor_tensor(hn[:, tt, :], hn[:, tt, :],
                                        ple_gate[:, 2 * tt:2 * tt + 2, :].rearrange("p a n -> p (a n)"),
                                        ALU.add).then_inc(ple_added, 1)
            dve.wait_ge(ple_added, ND)
            dve.wait_ge(rows_turned, 3)
            nc.vector.tensor_scalar(rows[:, 2, :], bank[:, 2, 0:TD], S_G, None, ALU.mult).then_inc(rows_hi, 1)
            dve.wait_ge(rows_hi, 1)
            nc.vector.scalar_tensor_tensor(out=rows[:, 3, :], in0=bank[:, 2, 0:TD], scalar=S_G, in1=rows[:, 2, :],
                                           op0=ALU.mult, op1=ALU.subtract).then_inc(rows_done, 1)
            dve.wait_ge(rows_done, 1)
            dve.wait_ge(rows_idx, 2)

            def dot(j, g_round):
                dve.wait_ge(rows_in[j % ROW_RING], 16 * (g_round + 1))
                own.settle()
                own.mark(nc.vector.memset(word[:], 0.0))
                slot = expert_rows[:, j % ROW_RING, :]
                nc.vector.tensor_tensor_reduce(slot, slot, hn[:, ND, :], 1.0, 0.0, ALU.mult, ALU.add,
                                               dots_now[:, j:j + 1]).then_inc(rows_used, 1)

            def keep_dots(first, count):
                dve.wait_ge(rows_used, first + count)
                own.link(nc.vector.tensor_copy(dots[:, bass.ds(first, count)], dots_now[:, 0:count]))

            def onehots(q, b, first):
                shape = [P, BATCH // OT, NKEY, OT]
                if not first:
                    dve.wait_ge(gates_prod, 4 * q - 4)
                own.link(nc.vector.tensor_copy(staged[:, b], rows[:, :, bass.ds(BATCH * q, BATCH)]))
                cols = [staged[:, b, w, :].rearrange("p (a t) -> p a t", t=OT).unsqueeze(2).to_broadcast(shape)
                        for w in range(4)]
                keys = iota_oh_sb[:].unsqueeze(1).to_broadcast(shape)
                own.mark(nc.vector.tensor_tensor(onehot[:, b], keys, cols[0], ALU.is_equal))
                own.mark(nc.vector.tensor_tensor(onehot[:, 2], keys, cols[1], ALU.is_equal))
                own.settle()
                own.mark(nc.vector.tensor_tensor(onehot_hi[:, b], onehot[:, 2], cols[2], ALU.mult))
                nc.vector.tensor_tensor(onehot_lo[:, b], onehot[:, 2], cols[3], ALU.mult).then_inc(onehot_done, 1)

            def build_gates(it, first):
                for s in range(2):
                    for j in range(4):
                        c = U_TOPK + U_SOFTMAX + 4 * s + j
                        split_lo(Tile(T_U + c + SPLIT_AHEAD, 8, it))
                        if j % 2 == 0:
                            q = 4 * it + 2 * s + j // 2
                            if not (first and s == 0 and j == 0):
                                dve.wait_ge(onehot_done, q)
                            onehots(q, j // 2, first and s == 0)
                        dot(4 * s + j, 2 * it + s)

            dve.wait_ge(lo_cut, POOL_FIRST + POOL_TILES)
            build_gates(0, True)
            keep_dots(0, 8)
            before = own.count

            def build_gates_loop(it):
                own.turns, own.count = GATES_OWN * (it - 1), before
                build_gates(it, False)
                keep_dots(8 * it, 8)
                assert own.count - before == GATES_OWN, own.count - before

            with dve.Fori(1, U_GATES // 8) as it:
                build_gates_loop(it)
            own.turns, own.count = 0, before + GATES_OWN * (U_GATES // 8 - 1)

            def make_weight(i, slot, parity, rounds, values, ready, target):
                dve.wait_ge(gates_loaded[parity], 16 * (rounds + 1))
                dve.wait_ge(ready, target)
                at_least(dve, weight_lo, i - RING + 1)
                nc.vector.tensor_tensor(
                    weight[:, slot, :].rearrange("p (c t) -> p c t", t=TOK),
                    values.rearrange("p (c t) -> p c t", t=TOK),
                    gates_in[:, parity, :, slot, :], ALU.mult).then_inc(weight_done, 1)

            def make_both(e, q):
                i = 8 * e + q
                make_weight(i, q % RING, (q // 4) % 2, e + q // 8, gelu_out[:, q % VG, :], columns_out,
                            N_IN + N_Q + U_EARLY + i + 1)

            def make_late(e, q):
                parity, rounds = (q // 4) % 2, e + q // 8
                if isinstance(e, int) and 8 * e + q >= N_LATE - KEPT:
                    make_weight(N_BOTH + 8 * e + q, q % RING, parity, EIGHTS + rounds,
                                gelu_kept[:, q % 8, :], columns_out, N_IN + N_Q + U_EARLY)
                    return
                make_weight(N_BOTH + 8 * e + q, q % RING, parity, EIGHTS + rounds,
                            gelu_in[:, parity, q % VG, :], gelu_loaded[parity], 16 * (rounds + 1))

            def weight_low(i, slot):
                dve.wait_ge(weight_hi, i + 1)
                nc.vector.tensor_tensor(weight_cut[:, slot, 1, :], weight[:, slot, :], weight_cut[:, slot, 0, :],
                                        ALU.subtract).then_inc(weight_lo, 1)

            def weights_now(first, count):
                dve.wait_ge(rows_used, HK + first)
                own.link(nc.vector.tensor_copy(sparse_w_now[:, 0:count], sparse_w[:, bass.ds(first, count)]))

            def add_row(j, a, a_round):
                dve.wait_ge(rows_in[j % ROW_RING], 16 * (HK // ROW_RING + a_round + 1))
                dve.wait_ge(rows_used, HK + a)
                nc.vector.scalar_tensor_tensor(out=sparse_sum, in0=expert_rows[:, j % ROW_RING, :],
                                               scalar=sparse_w_now[:, j:j + 1], in1=sparse_sum,
                                               op0=ALU.mult, op1=ALU.add).then_inc(rows_used, 1)

            split_lo(Tile(T_BOTH + SPLIT_AHEAD))
            split_lo(Tile(T_BOTH + 1 + SPLIT_AHEAD))
            make_both(0, 0)
            make_both(0, 1)
            weight_low(0, 0)

            def both(e, step, steps):
                step_at = [steps * q // 8 for q in range(9)]
                for p in range(8):
                    t = Tile(T_BOTH + 2 + 16 * e + 2 * p) if isinstance(e, int) else Tile(T_BOTH + 2 + 2 * p, 16, e)
                    i = 8 * e + p
                    mine = list(range(step_at[p], step_at[p + 1]))
                    if t.c < T_LATE - 2:
                        split_lo(t.plus(SPLIT_AHEAD))
                        weight_low(i + 1, (p + 1) % RING)
                        for j in mine[:2]:
                            step(j)
                        split_lo(t.plus(1 + SPLIT_AHEAD))
                        make_both(e, p + 2)
                        for j in mine[2:]:
                            step(j)
                    else:
                        split_lo(Tile(T_LATE + i - N_BOTH + SPLIT_AHEAD))
                        if i == N_BOTH - 2:
                            weight_low(i + 1, (i + 1) % RING)
                            make_late(0, 0)
                            step(mine[0])
                            weight_low(i + 2, (i + 2) % RING)
                            make_late(0, 1)
                        else:
                            step(mine[0])
                            weight_low(i + 2, (i + 2) % RING)
                            make_late(0, 2)
                        for j in mine[1:]:
                            step(j)

            def both_dots(e, first, count):
                both(e, lambda j: dot(j, first // ROW_RING + j // ROW_RING), count)
                keep_dots(first, count)

            def both_sums(e, first, count):
                weights_now(first, count)
                both(e, lambda j: add_row(j, first + j, first // ROW_RING + j // ROW_RING), count)

            count, rounds = EIGHT_DOTS[0], EIGHT_DOTS[0] // ROW_RING
            both_dots(0, U_GATES, count)
            before = own.count
            with dve.Fori(1, len(EIGHT_DOTS)) as e:
                own.turns, own.count = (count + 1) * (e - 1), before
                both(e, lambda j: dot(j, U_GATES // ROW_RING + rounds * e + j // ROW_RING), count)
                keep_dots(U_GATES + count * e, count)
                assert own.count - before == count + 1
            own.turns, own.count = 0, before + (count + 1) * (len(EIGHT_DOTS) - 1)
            nc.vector.memset(word[:], 0.0).then_inc(dots_done, 1)
            dve.wait_ge(dots_gelu, 1)
            own.link(nc.vector.scalar_tensor_tensor(out=sparse_w[:], in0=dots[:], scalar=1 / ALPHA,
                                                    in1=picked[:, 2, ND, :], op0=ALU.mult, op1=ALU.mult))
            first = 0
            for n, count in enumerate(EIGHT_SUMS):
                both_sums(len(EIGHT_DOTS) + n, first, count)
                first += count

            def late(e):
                fixed = isinstance(e, int)
                end = fixed and e == N_LATE // 8 - 1
                weights_now(first + 8 * e, 8)
                for v in range(8):
                    if not end:
                        add_row(v, first + 8 * e + v, first // ROW_RING + 2 * e + v // ROW_RING)
                    t = Tile(T_LATE + 8 * e + v) if fixed else Tile(T_LATE + v, 8, e)
                    if not fixed or t.n + SPLIT_AHEAD + 1 < T_ALL:
                        make_late(e, v + 3)
                    if not fixed or t.n + SPLIT_AHEAD < T_ALL:
                        weight_low(N_BOTH + 8 * e + v + 2, (v + 2) % RING)
                        split_lo(t.plus(SPLIT_AHEAD))
                    if end:
                        add_row(v, first + 8 * e + v, first // ROW_RING + 2 * e + v // ROW_RING)

            before = own.count
            with dve.Fori(0, N_LATE // 8 - 2) as e:
                own.turns, own.count = e, before
                late(e)
            own.turns, own.count = 0, before + N_LATE // 8 - 2
            late(N_LATE // 8 - 2)
            late(N_LATE // 8 - 1)
            for i, t in enumerate(FINAL_ORDER):
                if t == ND:
                    dve.wait_ge(rows_used, 2 * HK)
                    nc.vector.tensor_tensor(hn[:, t, :], hn[:, t, :], sparse_sum, ALU.add).then_inc(final_sum, 2)
                else:
                    if t < ND - 1:
                        dve.wait_ge(experts_done, t + 1)
                    else:
                        dve.wait_ge(tile_used, T_ALL)
                    for h in range(2):
                        rows_b = hn[:, t, h * HALF:(h + 1) * HALF]
                        nc.vector.scalar_tensor_tensor(out=rows_b, in0=bank[:, 2 * t + h, :],
                                                       scalar=1 / (S_G * S_V * ALPHA), in1=rows_b, op0=ALU.mult,
                                                       op1=ALU.add).then_inc(final_sum, 1)
                dve.wait_ge(final_sum, 2 * i + 2)
                row_stats(t)
                row_moments(2, EPS / ALPHA ** 2, i)
                if i:
                    layer_norm(2, i - 1)
            layer_norm(2, TT - 1)
            add_b(2, TT - 1)


def _tables():
    q, k = np.arange(CHUNK)[:, None], np.arange(P)[None, :] - CHUNK
    dist = np.abs(q - k).astype(np.float32)
    heads = [m // 2 + 4 * (m % 2) for m in range(8)]
    slopes = np.array([2.0 ** (-(h + 1)) for h in heads], np.float32)
    alibi = np.tile(-slopes[None, :, None] * dist[:, None, :], (2, 1, 1)).astype(np.float32)
    counts = np.stack([1.0 / np.minimum(np.arange(1, PAD + 1), w) for w in WINDOWS]).astype(np.float32)
    counts = np.broadcast_to(counts.reshape(1, -1), (P, GROUPS * PAD))
    onehot = np.broadcast_to(np.arange(NKEY, dtype=np.float16)[None, :, None], (P, NKEY, OT))
    keys = np.broadcast_to(np.arange(K, dtype=np.float32)[None, :], (P, K))
    return alibi, counts, np.eye(P, dtype=np.float32), onehot, keys


def kernel(x, p, ln_in_g, ln_in_b, w_in, pool_w, pool_scale, attn_sinks, w_o, ln1_g, ln1_b, peer_wq,
           peer_subkeys, peer_u, peer_v, ple_w, ple_gate_w, ple_gate_b, ln2_g, ln2_b):
    import concourse.bacc as bacc
    from concourse.bass_utils import run_bass_kernel_spmd

    alibi, counts, ident, onehot, keys = _tables()
    a = np.asarray
    c = lambda v: np.ascontiguousarray(v, dtype=np.float32)
    w_in, w_o = a(w_in)[0], a(w_o)[0]
    pool_n = GROUPS * P
    pair_cols = [np.r_[j * HD:(j + 1) * HD, (j + 4) * HD:(j + 5) * HD] for j in range(PAIRS)]
    named = {"k": 2 * pool_n + np.arange(P), "v": 2 * pool_n + P + np.arange(P)}
    named.update({f"q{j}": pool_n + pc for j, pc in enumerate(pair_cols)})
    named.update({f"u{g}": g * P + np.arange(P) for g in range(GROUPS)})
    cols = [named[name] for name in COLUMNS]
    w_in = w_in[:, np.concatenate(cols)]
    rows = [pool_n + pc for pc in pair_cols] + [np.arange(pool_n)]
    w_o = w_o[np.concatenate(rows)]
    by_columns = lambda w, n: w.reshape(KD, P, n, P).transpose(2, 1, 0, 3).reshape(n, P, D)
    by_rows = lambda w: w.reshape(KD, P, D)
    u = a(peer_u)[0].reshape(P, N_U, KD, P).transpose(1, 3, 2, 0).reshape(N_U, P, D)
    v = a(peer_v)[0].reshape(P, N_U, D).transpose(1, 0, 2)
    turns = np.stack([u[U_EARLY + 2:], v[U_EARLY:-2]], axis=1).reshape(-1, P, D)
    tiles = np.concatenate([by_columns(w_in, N_IN), by_rows(w_o), by_columns(a(peer_wq)[0], N_Q),
                            by_rows(a(ple_gate_w)[0]), u[:U_EARLY + 2], turns, v[-2:], v[:U_EARLY]])
    order = [m // 2 + 4 * (m % 2) for m in range(8)]
    small = np.concatenate([
        np.broadcast_to(a(attn_sinks)[0][order][None, :], (P, 8)),
        a(pool_scale)[0].reshape(GROUPS, P).T, counts], axis=1)
    arrays = {
        "tiles": c(tiles),
        "u_rows": c(a(peer_u)[0]),
        "v_rows": c(a(peer_v)[0]),
        "x": c(a(x).reshape(T, D)),
        "ple_in": c(a(p).reshape(T, 2, P).transpose(2, 1, 0)),
        "ple_w": c(a(ple_w)[0].reshape(2, P, D).transpose(1, 0, 2)),
        "norms": c(np.stack([a(ln_in_g), a(ln_in_b), a(ln1_g)[0], a(ln1_b)[0], a(ln2_g)[0],
                             a(ln2_b)[0]]).reshape(3, 2, D)),
        "gate_b": c(a(ple_gate_b)[0]),
        "small": c(small),
        "pool_w": c(a(pool_w)[0].transpose(1, 0, 2)),
        "subkeys": c(a(peer_subkeys)[0].reshape(2 * HEADS, NKEY, P).transpose(2, 0, 1)),
        "alibi": c(alibi),
        "ident": c(ident),
        "iota_oh": np.ascontiguousarray(onehot),
        "iota_k": c(keys),
    }
    nc = bacc.Bacc("TRN2", target_bir_lowering=False, num_devices=1)
    args = [nc.dram_tensor(f"{n}_dram", v_.shape, mybir.dt.from_np(v_.dtype), kind="ExternalInput").ap()
            for n, v_ in arrays.items()]
    out = nc.dram_tensor("out_dram", [T, D], F32, kind="ExternalOutput").ap()
    layer(nc, *args, out)
    r = run_bass_kernel_spmd(nc, [{f"{n}_dram": v_ for n, v_ in arrays.items()}], core_ids=[0])
    return r.results[0]["out_dram"].reshape(1, T, D)
```
